# Optimizing a Trainium2 kernel written in Bass

```python
import math
import jax, jax.numpy as jnp
from jax import lax
import numpy as np

D_MODEL = 1024
BATCH = 1
SEQ = 512
DEPTH = 2

HEAD_DIM = 64
H_A = D_MODEL // HEAD_DIM
KV_A = 4
G_A = H_A // KV_A
WINDOW_A = 128
BLOCK_A = 128
H_B = D_MODEL // HEAD_DIM
DILATED_GROUPS = ((128, 1), (512, 4), (2048, 16))
N_GROUPS_B = len(DILATED_GROUPS)
BLOCK_B = 64
D_FF = -(-8 * D_MODEL // (3 * 256)) * 256
RMS_EPS = 1e-6
NEG = -1e30


def rmsnorm(x, g):
    x32 = x.astype(jnp.float32)
    y = x32 * lax.rsqrt(jnp.mean(x32 * x32, axis=-1, keepdims=True) + RMS_EPS)
    return (y * g.astype(jnp.float32)).astype(x.dtype)

def alibi_slopes(n):
    return 2.0 ** (-8.0 * jnp.arange(1, n + 1, dtype=jnp.float32) / n)

def banded_attention(q, k, v, slopes, dist_unit, window, block):
    n, L, hk, g, dh = q.shape
    c = window // block
    nb = -(-L // block)
    lp = nb * block
    kw = (2 * c + 1) * block
    qb = jnp.pad(q, ((0, 0), (0, lp - L), (0, 0), (0, 0), (0, 0))).reshape(n, nb, block, hk, g, dh)
    pad_k = ((0, 0), (window, window + lp - L), (0, 0), (0, 0))
    kb = jnp.pad(k, pad_k).reshape(n, nb + 2 * c, block, hk, dh)
    vb = jnp.pad(v, pad_k).reshape(n, nb + 2 * c, block, hk, dh)
    kwin = jnp.concatenate([kb[:, j:j + nb] for j in range(2 * c + 1)], axis=2)
    vwin = jnp.concatenate([vb[:, j:j + nb] for j in range(2 * c + 1)], axis=2)
    scores = jnp.einsum('nbqhgd,nbkhd->nbhgqk', qb, kwin,
                        preferred_element_type=jnp.float32) * (dh ** -0.5)
    rel = jnp.arange(kw)[None, :] - window - jnp.arange(block)[:, None]
    key_pos = jnp.arange(nb)[:, None] * block - window + jnp.arange(kw)[None, :]
    valid = (jnp.abs(rel)[None] <= window) & ((key_pos >= 0) & (key_pos < L))[:, None, :]
    dist = jnp.abs(rel).astype(jnp.float32) * dist_unit
    scores = scores - slopes.astype(jnp.float32)[:, :, None, None] * dist
    scores = jnp.where(valid[None, :, None, None], scores, NEG)
    m = jnp.max(scores, axis=-1)
    p = jnp.exp(scores - m[..., None])
    den = jnp.sum(p, axis=-1)
    lse = m + jnp.log(den)
    out = jnp.einsum('nbhgqk,nbkhd->nbqhgd', p.astype(v.dtype), vwin,
                     preferred_element_type=jnp.float32)
    out = out / jnp.moveaxis(den, -1, 2)[..., None]
    out = out.reshape(n, lp, hk, g, dh)[:, :L]
    lse = jnp.moveaxis(lse, -1, 2).reshape(n, lp, hk, g)[:, :L]
    return out.astype(q.dtype), lse

def window_gqa_sink(h, w_qkv, w_out, sink):
    b, s, _ = h.shape
    qkv = h @ w_qkv
    q = qkv[..., :H_A * HEAD_DIM].reshape(b, s, KV_A, G_A, HEAD_DIM)
    k = qkv[..., H_A * HEAD_DIM:(H_A + KV_A) * HEAD_DIM].reshape(b, s, KV_A, HEAD_DIM)
    v = qkv[..., (H_A + KV_A) * HEAD_DIM:].reshape(b, s, KV_A, HEAD_DIM)
    slopes = alibi_slopes(H_A).reshape(KV_A, G_A)
    o, lse = banded_attention(q, k, v, slopes, 1, WINDOW_A, BLOCK_A)
    o = o * jax.nn.sigmoid(lse - sink.astype(jnp.float32).reshape(KV_A, G_A))[..., None]
    return o.astype(h.dtype).reshape(b, s, H_A * HEAD_DIM) @ w_out

def to_residue(t, dil):
    b, s, hh, dh = t.shape
    return t.reshape(b, s // dil, dil, hh, dh).transpose(0, 2, 1, 3, 4).reshape(b * dil, s // dil, hh, dh)

def from_residue(t, b, dil):
    rest = t.shape[2:]
    L = t.shape[1]
    t = t.reshape((b, dil, L) + rest)
    t = jnp.swapaxes(t, 1, 2)
    return t.reshape((b, L * dil) + rest)

def dilated_mixture_attention(h, w_qkv, w_out):
    b, s, _ = h.shape
    qkv = (h @ w_qkv).reshape(b, s, N_GROUPS_B, 3, H_B, HEAD_DIM)
    slopes = alibi_slopes(H_B)[:, None]
    outs, lses = [], []
    for gi, (win, dil) in enumerate(DILATED_GROUPS):
        q = to_residue(qkv[:, :, gi, 0], dil)[:, :, :, None]
        k = to_residue(qkv[:, :, gi, 1], dil)
        v = to_residue(qkv[:, :, gi, 2], dil)
        o, lse = banded_attention(q, k, v, slopes, dil, win // (2 * dil), BLOCK_B)
        outs.append(from_residue(o[:, :, :, 0], b, dil))
        lses.append(from_residue(lse[:, :, :, 0], b, dil))
    wts = jax.nn.softmax(jnp.stack(lses), axis=0)
    o = jnp.einsum('gbsh,gbshd->bshd', wts, jnp.stack(outs).astype(jnp.float32))
    return o.astype(h.dtype).reshape(b, s, H_B * HEAD_DIM) @ w_out

def swiglu(h, w_gate, w_up, w_down):
    return (jax.nn.silu(h @ w_gate) * (h @ w_up)) @ w_down

def first_inputs(seed: int = 0) -> dict:
    key = jax.random.key(seed)
    ks = jax.random.split(key, 14)
    n_a = (DEPTH + 1) // 2
    n_b = DEPTH // 2
    qkv_a = (H_A + 2 * KV_A) * HEAD_DIM
    qkv_b = N_GROUPS_B * 3 * H_B * HEAD_DIM
    f32 = jnp.float32

    def w(k, shape, fan_in):
        return jax.random.normal(k, shape, f32) * fan_in ** -0.5

    return {
        "x": jax.random.normal(ks[0], (BATCH, SEQ, D_MODEL), f32),
        "norm_mix": 1.0 + 0.02 * jax.random.normal(ks[1], (DEPTH, D_MODEL), f32),
        "norm_ffn": 1.0 + 0.02 * jax.random.normal(ks[2], (DEPTH, D_MODEL), f32),
        "w_qkv_a": w(ks[3], (n_a, D_MODEL, qkv_a), D_MODEL),
        "w_out_a": w(ks[4], (n_a, H_A * HEAD_DIM, D_MODEL), H_A * HEAD_DIM),
        "sink_a": 0.5 * jax.random.normal(ks[5], (n_a, H_A), f32),
        "w_qkv_b": w(ks[6], (n_b, D_MODEL, qkv_b), D_MODEL),
        "w_out_b": w(ks[7], (n_b, H_B * HEAD_DIM, D_MODEL), H_B * HEAD_DIM),
        "w_gate": w(ks[8], (DEPTH, D_MODEL, D_FF), D_MODEL),
        "w_up": w(ks[9], (DEPTH, D_MODEL, D_FF), D_MODEL),
        "w_down": w(ks[10], (DEPTH, D_FF, D_MODEL), D_FF),
        "norm_final": 1.0 + 0.02 * jax.random.normal(ks[11], (D_MODEL,), f32),
    }

def first_block(x, norm_mix, norm_ffn, w_qkv_a, w_out_a, sink_a, w_qkv_b, w_out_b,
              w_gate, w_up, w_down, norm_final):
    for i in range(DEPTH):
        h = rmsnorm(x, norm_mix[i])
        j = i // 2
        if i % 2 == 0:
            x = x + window_gqa_sink(h, w_qkv_a[j], w_out_a[j], sink_a[j])
        else:
            x = x + dilated_mixture_attention(h, w_qkv_b[j], w_out_b[j])
        h = rmsnorm(x, norm_ffn[i])
        x = x + swiglu(h, w_gate[i], w_up[i], w_down[i])
    return rmsnorm(x, norm_final)


CTX_LEN = 256
GRID_W = 64

F_GROUPS = 4
F_GROUP_DIM = D_MODEL // 16
F_WIDTH = F_GROUPS * F_GROUP_DIM
G_HEADS = 4
G_HEAD_DIM = D_MODEL // 16
G_WIDTH = G_HEADS * G_HEAD_DIM
CHUNK = 128
A_HEADS = 8
A_NOPE = D_MODEL // 16
A_ROPE = D_MODEL // 32
A_V = D_MODEL // 16
A_QK = A_NOPE + A_ROPE
A_WIDTH = A_HEADS * A_V
Q_LORA = D_MODEL // 4
KV_LORA = D_MODEL // 8

MIX_WIDTH = F_WIDTH + G_WIDTH + A_WIDTH
IN_WIDTH = 2 * F_WIDTH + 3 * G_WIDTH + Q_LORA + KV_LORA + A_ROPE + A_WIDTH
ROPE_BASE = 10000.0
EPS = 1e-6
Q_BLOCK = 128


def _rmsnorm(t, g):
    tf = t.astype(jnp.float32)
    tf = tf * lax.rsqrt(jnp.mean(tf * tf, axis=-1, keepdims=True) + EPS)
    return (tf * g.astype(jnp.float32)).astype(t.dtype)

def _layernorm(t, g):
    tf = t.astype(jnp.float32)
    tf = tf - jnp.mean(tf, axis=-1, keepdims=True)
    tf = tf * lax.rsqrt(jnp.mean(tf * tf, axis=-1, keepdims=True) + EPS)
    return (tf * g.astype(jnp.float32)).astype(t.dtype)

def _split_in(p):
    sizes = (F_WIDTH, F_WIDTH, G_WIDTH, G_WIDTH, G_WIDTH, Q_LORA, KV_LORA, A_ROPE, A_WIDTH)
    parts = []
    start = 0
    for s in sizes:
        parts.append(p[..., start:start + s])
        start += s
    return parts

def _axial_rope(n):
    rows = n // GRID_W
    row = jnp.repeat(jnp.arange(rows, dtype=jnp.float32), GRID_W)
    col = jnp.tile(jnp.arange(GRID_W, dtype=jnp.float32), rows)
    half = A_ROPE // 2
    inv = ROPE_BASE ** (-jnp.arange(0, half, 2, dtype=jnp.float32) / half)
    ang_r = row[:, None] * inv[None, :]
    ang_c = col[:, None] * inv[None, :]
    ang = jnp.concatenate([ang_r, ang_r, ang_c, ang_c], axis=-1)
    return jnp.cos(ang), jnp.sin(ang)

def _apply_rope(t, rope):
    cos, sin = rope
    q = A_ROPE // 4
    x1, x2, x3, x4 = t[..., :q], t[..., q:2 * q], t[..., 2 * q:3 * q], t[..., 3 * q:]
    rot = jnp.concatenate([-x2, x1, -x4, x3], axis=-1)
    cos = cos[:, None, :].astype(t.dtype)
    sin = sin[:, None, :].astype(t.dtype)
    return t * cos + rot * sin

def _fourier(u):
    b, n, _ = u.shape
    ug = u.astype(jnp.float32).reshape(b, n, F_GROUPS, F_GROUP_DIM).transpose(0, 2, 1, 3)
    f = jnp.fft.fft2(ug, norm="ortho").real
    return f.transpose(0, 2, 1, 3).reshape(b, n, F_WIDTH).astype(u.dtype)

def _spatial_gate(u, v, ln_g, ws, bs):
    b, n, _ = v.shape
    vh = v.reshape(b, n // CHUNK, CHUNK, G_HEADS, G_HEAD_DIM)
    vh = _layernorm(vh, ln_g)
    mixed = jnp.einsum('hpq,bcqhd->bcphd', ws, vh) + bs.T[None, None, :, :, None]
    return u * mixed.reshape(b, n, G_WIDTH)

def _mla_qkv(c_q, c_kv, k_rope, q_a_g, w_uq, kv_a_g, w_ukv, q_norm_g, k_norm_g, rope):
    b, n, _ = c_q.shape
    q = (_rmsnorm(c_q, q_a_g) @ w_uq).reshape(b, n, A_HEADS, A_QK)
    kv = (_rmsnorm(c_kv, kv_a_g) @ w_ukv).reshape(b, n, A_HEADS, A_NOPE + A_V)
    k_nope, v = kv[..., :A_NOPE], kv[..., A_NOPE:]
    k_r = jnp.broadcast_to(k_rope[:, :, None, :], (b, n, A_HEADS, A_ROPE))
    k = jnp.concatenate([k_nope, k_r], axis=-1)
    q = _rmsnorm(q, q_norm_g)
    k = _rmsnorm(k, k_norm_g)
    if rope is not None:
        q = jnp.concatenate([q[..., :A_NOPE], _apply_rope(q[..., A_NOPE:], rope)], axis=-1)
        k = jnp.concatenate([k[..., :A_NOPE], _apply_rope(k[..., A_NOPE:], rope)], axis=-1)
    return q, k, v

def _branches(h, w_in, w_fmix, g_ln_g, g_ws, g_bs, q_a_g, w_uq, kv_a_g, w_ukv, q_norm_g, k_norm_g, rope):
    f_in, f_gate, g_u, g_v, g_gate, c_q, c_kv, k_rope, a_gate = _split_in(h @ w_in)
    f_out = (_fourier(f_in) @ w_fmix) * jax.nn.silu(f_gate)
    g_out = _spatial_gate(g_u, g_v, g_ln_g, g_ws, g_bs) * jax.nn.silu(g_gate)
    q, k, v = _mla_qkv(c_q, c_kv, k_rope, q_a_g, w_uq, kv_a_g, w_ukv, q_norm_g, k_norm_g, rope)
    return f_out, g_out, q, k, v, a_gate

def _attend(q, k, v):
    s = jnp.einsum('bqhd,bkhd->bhqk', q, k).astype(jnp.float32) * (A_QK ** -0.5)
    p = jax.nn.softmax(s, axis=-1).astype(v.dtype)
    return jnp.einsum('bhqk,bkhd->bqhd', p, v)

def _blocked_attention(q, k, v):
    b, n, h, d = q.shape
    nb = n // Q_BLOCK
    qb = q.reshape(b, nb, Q_BLOCK, h, d).transpose(1, 0, 2, 3, 4)
    o = lax.map(lambda blk: _attend(blk, k, v), qb)
    return o.transpose(1, 0, 2, 3, 4).reshape(b, n, h * A_V)

def second_inputs(seed: int = 0) -> dict:
    key = jax.random.key(seed)
    ks = jax.random.split(key, 24)
    f32 = jnp.float32
    nrm = lambda k, shape, s: jax.random.normal(k, shape, f32) * s
    gain = lambda k, shape: 1.0 + 0.02 * jax.random.normal(k, shape, f32)
    return {
        "x": nrm(ks[0], (BATCH, SEQ, D_MODEL), 1.0),
        "c": nrm(ks[1], (BATCH, D_MODEL), 1.0),
        "ctx": nrm(ks[2], (BATCH, CTX_LEN, D_MODEL), 1.0),
        "c_ctx": nrm(ks[3], (D_MODEL,), 1.0),
        "w_mod": nrm(ks[4], (DEPTH, D_MODEL, 3 * D_MODEL), 0.5 * D_MODEL ** -0.5),
        "b_mod": nrm(ks[5], (DEPTH, 3 * D_MODEL), 0.01),
        "norm_g": gain(ks[6], (DEPTH, D_MODEL)),
        "w_in": nrm(ks[7], (DEPTH, D_MODEL, IN_WIDTH), D_MODEL ** -0.5),
        "w_fmix": nrm(ks[8], (DEPTH, F_WIDTH, F_WIDTH), F_WIDTH ** -0.5),
        "g_ln_g": gain(ks[9], (DEPTH, G_HEAD_DIM)),
        "g_ws": nrm(ks[10], (DEPTH, G_HEADS, CHUNK, CHUNK), CHUNK ** -0.5),
        "g_bs": 1.0 + nrm(ks[11], (DEPTH, G_HEADS, CHUNK), 0.01),
        "q_a_g": gain(ks[12], (DEPTH, Q_LORA)),
        "w_uq": nrm(ks[13], (DEPTH, Q_LORA, A_HEADS * A_QK), Q_LORA ** -0.5),
        "kv_a_g": gain(ks[14], (DEPTH, KV_LORA)),
        "w_ukv": nrm(ks[15], (DEPTH, KV_LORA, A_HEADS * (A_NOPE + A_V)), KV_LORA ** -0.5),
        "q_norm_g": gain(ks[16], (DEPTH, A_QK)),
        "k_norm_g": gain(ks[17], (DEPTH, A_QK)),
        "w_out": nrm(ks[18], (DEPTH, MIX_WIDTH, D_MODEL), MIX_WIDTH ** -0.5),
    }

def second_block(x, c, ctx, c_ctx, w_mod, b_mod, norm_g, w_in, w_fmix, g_ln_g, g_ws, g_bs,
              q_a_g, w_uq, kv_a_g, w_ukv, q_norm_g, k_norm_g, w_out):
    n = x.shape[1]
    rope = _axial_rope(n)
    y = ctx
    silu_c = jax.nn.silu(c)
    silu_cc = jax.nn.silu(c_ctx)
    for l in range(DEPTH):
        shift, scale, gate = jnp.split(silu_c @ w_mod[l] + b_mod[l], 3, axis=-1)
        shift_c, scale_c, gate_c = jnp.split(silu_cc @ w_mod[l] + b_mod[l], 3, axis=-1)
        hx = _rmsnorm(x, norm_g[l]) * (1.0 + scale[:, None, :]) + shift[:, None, :]
        hy = _rmsnorm(y, norm_g[l]) * (1.0 + scale_c) + shift_c
        params = (w_in[l], w_fmix[l], g_ln_g[l], g_ws[l], g_bs[l], q_a_g[l], w_uq[l],
                  kv_a_g[l], w_ukv[l], q_norm_g[l], k_norm_g[l])
        fy, gy, qy, ky, vy, ay = _branches(hy, *params, None)
        fx, gx, qx, kx, vx, ax = _branches(hx, *params, rope)
        k_all = jnp.concatenate([ky, kx], axis=1)
        v_all = jnp.concatenate([vy, vx], axis=1)
        ox = _blocked_attention(qx, k_all, v_all) * jax.nn.silu(ax)
        x = x + gate[:, None, :] * (jnp.concatenate([fx, gx, ox], axis=-1) @ w_out[l])
        if l < DEPTH - 1:
            b = y.shape[0]
            oy = _attend(qy, ky, vy).reshape(b, y.shape[1], A_WIDTH) * jax.nn.silu(ay)
            y = y + gate_c * (jnp.concatenate([fy, gy, oy], axis=-1) @ w_out[l])
    return x


def setup_inputs(seed=0):
    out = dict(first_inputs(seed))
    for name, value in second_inputs(seed + 1).items():
        if name != "x":
            out[name + "_2"] = value
    return out


def reference(
    x, norm_mix, norm_ffn, w_qkv_a, w_out_a, sink_a, w_qkv_b, w_out_b, w_gate, w_up, w_down,
    norm_final, c_2, ctx_2, c_ctx_2, w_mod_2, b_mod_2, norm_g_2, w_in_2, w_fmix_2, g_ln_g_2,
    g_ws_2, g_bs_2, q_a_g_2, w_uq_2, kv_a_g_2, w_ukv_2, q_norm_g_2, k_norm_g_2, w_out_2,
):
    x = first_block(
        x, norm_mix, norm_ffn, w_qkv_a, w_out_a, sink_a, w_qkv_b, w_out_b, w_gate, w_up, w_down,
        norm_final,
    )
    return second_block(
        x, c_2, ctx_2, c_ctx_2, w_mod_2, b_mod_2, norm_g_2, w_in_2, w_fmix_2, g_ln_g_2, g_ws_2,
        g_bs_2, q_a_g_2, w_uq_2, kv_a_g_2, w_ukv_2, q_norm_g_2, k_norm_g_2, w_out_2,
    )


_drawn_inputs = setup_inputs


def setup_inputs(seed=0):
    import zlib

    import numpy as np

    out = dict(_drawn_inputs(seed))
    spreads = {}
    factors = {'norm_mix': 4.547,
     'sink_a': 4.811,
     'norm_final': 2.728,
     'ctx_2': 8.0,
     'c_ctx_2': 3.093,
     'b_mod_2': 5.935,
     'norm_g_2': 7.586,
     'g_ln_g_2': 8.0,
     'g_bs_2': 8.0,
     'q_a_g_2': 8.0,
     'w_uq_2': 3.103,
     'kv_a_g_2': 8.0,
     'q_norm_g_2': 8.0,
     'k_norm_g_2': 8.0}
    for name, (base, spread) in spreads.items():
        noise = np.random.default_rng([zlib.crc32(name.encode()), seed]).standard_normal(out[name].shape)
        drawn = base * np.exp(spread * noise) if base else spread * noise
        out[name] = __import__('jax').numpy.asarray(drawn.astype(out[name].dtype))
    for name, factor in factors.items():
        out[name] = (out[name] * factor).astype(out[name].dtype)
    return out
```

```python
import numpy as np
from concourse import bass, mybir
from concourse.alu_op_type import AluOpType as ALU

F32 = mybir.dt.float32
F32R = mybir.dt.float32r
ACT = mybir.ActivationFunctionType
AX = mybir.AxisListType

P = 128
D_MODEL = 1024
KT = D_MODEL // P
SEQ = 512
TT = SEQ // P
CTX = 256
ALLT = SEQ + CTX
NT = ALLT // P
EPS = 1e-6
HD = 64
D_FF = 2816
FT = D_FF // P
WIN = 128
DIL = 4
MT = 3 * KT
A_HEADS, A_NOPE, A_ROPE, A_V = 8, 64, 32, 64
A_QK = A_NOPE + A_ROPE
BIG = 1e32
RING = 4
LEAD = 3
PRIME = 8


def stream_plan():
    s = []
    mod = [(0, t) for t in range(MT)]
    mod1 = [(1, t) for t in range(MT)]
    for m in range(2):
        s += [("ak", m), ("av", m)] + [("aq", 4 * m + i) for i in range(4)]
        s += [("mod", *mod1.pop(0)) for _ in range(2)]
    s += [("oa", t) for t in range(KT)]
    for j in range(FT):
        s += [("gate", 0, j), ("up", 0, j)]
    s += [("down", 0, j) for j in range(FT)]
    for p in range(8):
        for g in range(3):
            s += [("bq", g, p), ("bk", g, p), ("bv", g, p)]
        s += [("mod", *mod.pop(0)) for _ in range(3)]
    s += [("ob", t) for t in range(KT)]
    for j in range(FT):
        s += [("gate", 1, j), ("up", 1, j)]
        if mod1:
            s += [("mod", *mod1.pop(0))]
    s += [("down", 1, j) for j in range(FT)]
    for l in range(2):
        s += [("kr", l)] + [("tok", l, b) for b in range(4)]
        s += [("feat", l, t) for t in range(13)]
        s += [("out", l, t) for t in range(KT)]
    assert not mod and not mod1
    return s


PLAN = stream_plan()


class Blk:

    def __init__(self, const, i=0, per=0):
        assert per % RING == 0
        self.c, self.i, self.per = const, i, per
        self.slot = const % RING
        self.n = const + i * per if per else const
        self.round = const // RING + i * (per // RING) if per else const // RING

    def plus(self, k):
        return Blk(self.c + k, self.i, self.per)


class Sem:

    def __init__(self, nc, name, eng):
        self.h = nc.alloc_semaphore(name)
        eng.nop().then_inc(self.h, PRIME)
        self.n = PRIME

    def up(self, ins):
        ins.then_inc(self.h, 1)
        self.n += 1
        return self.n


def wt(eng, sem, value=None):
    eng.wait_ge(sem.h, sem.n if value is None else value)


class Core:

    def __init__(self, nc, io):
        self.nc, self.io = nc, io
        self.T, self.V, self.A, self.G, self.S = nc.tensor, nc.vector, nc.scalar, nc.gpsimd, nc.sync
        self.dummy = {}
        for name, eng in (("t", self.T), ("v", self.V), ("a", self.A), ("g", self.G)):
            self.dummy[id(eng)] = nc.alloc_semaphore("own_" + name)
        sb = self.sb
        self.ps = nc.alloc_psum_tensor("ps", [P, 8, 512], F32)
        off = (nc.sbuf_base + 31) // 32 * 32
        self.w_lo = nc.alloc_sbuf_tensor("w_lo", [P, RING, 1024], F32R)
        self.w_raw = nc.alloc_sbuf_tensor_at("w_raw", [P, RING, 1024], F32, offset=off)
        self.w_hi = sb("w_hi", [P, RING, 1024], F32R)
        self.x = sb("x", [P, KT, SEQ])
        self.ident = sb("ident", [P, P])
        self.ones = sb("ones", [P, P])
        self.vec = sb("vec", [P, io["vec"].shape[1]])
        self.slope = sb("slope", [P, 32])
        self.c4 = sb("c4", [P, KT, 4], F32R)
        self.modraw = [sb(f"modraw{l}", [P, MT * 4]) for l in range(2)]
        self.modv = sb("modv", [P, 2, MT, 2])
        self.r_tok = sb("r_tok", [P, 3, NT])
        self.diag = sb("diag", [P, NT, P])
        self.RB = sb("RB", [P, ALLT])
        self.sq = sb("sq", [P, 2, ALLT])
        self.d_raw = [nc.alloc_semaphore(f"d_raw{i}") for i in range(RING)]
        self.s_hi = Sem(nc, "s_hi", self.A)
        self.s_lo = Sem(nc, "s_lo", self.G)
        self.s_used = Sem(nc, "s_used", self.T)
        mk = lambda n, e: Sem(nc, n, e)
        self.s_x = mk("s_x", self.V)
        self.s_sq = mk("s_sq", self.A)
        self.s_ssq = mk("s_ssq", self.T)
        self.s_std = mk("s_std", self.A)
        self.s_diag = mk("s_diag", self.V)
        self.s_rbp = mk("s_rbp", self.T)
        self.s_RB = mk("s_RB", self.A)
        self.s_hh = mk("s_hh", self.A)
        self.s_hl = mk("s_hl", self.V)
        self.s_acc = mk("s_acc", self.T)
        self.s_v = mk("s_v", self.V)
        self.s_a = mk("s_a", self.A)
        self.s_t = mk("s_t", self.T)
        self.d_const = nc.alloc_semaphore("d_const")
        self.nsplit = 0

    def sb(self, name, shape, dt=F32):
        return self.nc.alloc_sbuf_tensor(name, shape, dt)

    def absorb(self, eng):
        eng.sem_inc(self.dummy[id(eng)])

    def stream_loops(self):
        nb = len(PLAN)
        w = self.io["wstream"]

        def load(b):
            self.S.wait_ge(self.s_used.h, b.n + 1 + PRIME - RING)
            self.S.dma_start(self.w_raw[:, b.slot, :], w[b.n] if isinstance(b.n, int) else
                             w[bass.ds(b.n, 1)].rearrange("a p n -> (a p) n")).then_inc(self.d_raw[b.slot], 16)

        def split_lo(b):
            self.G.wait_ge(self.s_hi.h, b.n + 1 + PRIME)
            self.G.tensor_tensor(self.w_lo[:, b.slot, :], self.w_raw[:, b.slot, :],
                                 self.w_hi[:, b.slot, :].bitcast(F32), ALU.subtract).then_inc(self.s_lo.h, 1)

        for eng, f in ((self.S, load), (self.G, split_lo)):
            with eng.Fori(0, nb // RING, 1) as i:
                for u in range(RING):
                    f(Blk(u, i, RING))
            for n in range(nb // RING * RING, nb):
                f(Blk(n))

    def split_hi(self, b):
        b = b.plus(LEAD)
        if b.per == 0 and b.c >= len(PLAN):
            return
        self.A.wait_ge(self.d_raw[b.slot], (b.round + 1) * 16)
        self.A.activation(self.w_hi[:, b.slot, :], self.w_raw[:, b.slot, :], ACT.Copy).then_inc(self.s_hi.h, 1)

    def use(self, b):
        self.T.wait_ge(self.s_lo.h, b.n + 1 + PRIME)

    def used(self, ins):
        ins.then_inc(self.s_used.h, 1)

    def mm3(self, out, wh, wl, ah, al, start, stop, w_is_lhs=True):
        T = self.T
        if w_is_lhs:
            T.matmul(out, wh, ah, start=start, stop=False)
            T.matmul(out, wh, al, start=False, stop=False)
            return T.matmul(out, wl, ah, start=False, stop=stop)
        T.matmul(out, ah, wh, start=start, stop=False)
        T.matmul(out, ah, wl, start=False, stop=False)
        return T.matmul(out, al, wh, start=False, stop=stop)

    def feat_chunk(self, b, out, h, ks, last=KT - 1):
        wh = self.w_hi[:, b.slot, :].rearrange("p (k m) -> p k m", k=KT)
        wl = self.w_lo[:, b.slot, :].rearrange("p (k m) -> p k m", k=KT)
        for k in ks:
            ins = self.mm3(out, wh[:, k, :], wl[:, k, :], h[0][:, k, :], h[1][:, k, :], k == 0, k == last)
        return ins

    def mod_chunk(self, b, out, ks):
        wh = self.w_hi[:, b.slot, :].rearrange("p (k m) -> p k m", k=KT)
        wl = self.w_lo[:, b.slot, :].rearrange("p (k m) -> p k m", k=KT)
        for k in ks:
            self.T.matmul(out[:, 0:4], wh[:, k, :], self.c4[:, k, :], start=k == 0, stop=False)
            ins = self.T.matmul(out[:, 0:2], wl[:, k, :], self.c4[:, k, 0:2], start=False, stop=k == KT - 1)
        return ins

    def square(self, src, n, width, sem, value):
        self.A.wait_ge(sem, value)
        wt(self.A, self.s_ssq, self.s_ssq_base + n - 1)
        self.s_sq.up(self.A.activation(self.sq[:, n % 2, 0:width], src, ACT.Square))

    def sum_squares(self, n, ntiles, cols, bank, tiles):
        wt(self.T, self.s_sq, self.s_sq_base + n + 1)
        for t in range(tiles):
            ins = self.T.matmul(self.ps[:, bank, cols + t:cols + t + 1], self.sq[:, n % 2, t * P:(t + 1) * P],
                                self.ones[:, 0:1], start=(n == 0 and t == 0),
                                stop=(n == ntiles - 1 and t == tiles - 1), skip_group_check=True)
        self.s_ssq.up(ins)

    def norm_begin(self):
        self.s_ssq_base, self.s_sq_base = self.s_ssq.n, self.s_sq.n

    def rstd(self, bank, tiles, width, row=0):
        A, V = self.A, self.V
        wt(A, self.s_ssq)
        self.s_std.up(A.activation(self.r_tok[:, row, 0:tiles], self.ps[:, bank, 0:tiles], ACT.Sqrt,
                                   bias=EPS, scale=1.0 / width))
        wt(V, self.s_std)
        V.reciprocal(self.r_tok[:, row, 0:tiles], self.r_tok[:, row, 0:tiles]).then_inc(self.s_diag.h, 1)
        self.s_diag.n += 1
        V.drain()

    def broadcast_rstd(self, banks, tiles, row=0):
        T, V, A = self.T, self.V, self.A
        for t in range(tiles):
            self.s_diag.up(V.tensor_scalar(self.diag[:, t, :], self.ident[:, :], self.r_tok[:, row, t:t + 1],
                                           None, ALU.mult))
        wt(T, self.s_diag)
        for t in range(tiles):
            ins = T.matmul(self.flat(banks, t * P, P), self.ones[:, :], self.diag[:, t, :], start=True, stop=True)
        self.s_rbp.up(ins)
        wt(A, self.s_rbp)
        self.s_RB.up(A.activation(self.RB[:, 0:tiles * P], self.flat(banks, 0, tiles * P), ACT.Copy))
        wt(V, self.s_RB)

    def flat(self, bank, start, n):
        return self.ps[:, :, :].rearrange("p b n -> p (b n)")[:, bank * 512 + start:bank * 512 + start + n]



def norm_tile(c, h, k, gain, order, sem_value, sem=None):
    A = c.A
    xin = order(c.x[:, k, :])
    A.wait_ge(sem if sem is not None else c.s_x.h, sem_value)
    c.s_hh.up(A.activation(h[0][:, k, :], xin, ACT.Copy, scale=gain[:, k:k + 1]))
    wt(A, c.s_ssq, c.s_ssq_base + k - 1)
    c.s_sq.up(A.activation(c.sq[:, k % 2, 0:SEQ], xin, ACT.Square))


def norm_tile_lo(c, h, k, gain, order):
    V = c.V
    wt(V, c.s_hh, c.s_hh_base + k + 1)
    c.s_hl.up(V.scalar_tensor_tensor(h[1][:, k, :], order(c.x[:, k, :]), gain[:, k:k + 1],
                                     h[0][:, k, :].bitcast(F32), ALU.mult, ALU.subtract))


def norm_finish(c):
    c.rstd(0, TT, D_MODEL)
    c.broadcast_rstd(1, TT)
    wt(c.T, c.s_hl)


def contract_out(c, n0, nb, act, order, nxt, ready):
    T, A, V = c.T, c.A, c.V
    ah, al = act

    def rows(b, m):
        return c.w_hi[:, b.slot, m * P:(m + 1) * P], c.w_lo[:, b.slot, m * P:(m + 1) * P]

    def outer(b, k, start):
        c.use(b)
        cols = bass.ds(k * SEQ, SEQ)
        for m in range(KT):
            wh, wl = rows(b, m)
            ins = c.mm3(c.ps[:, m, :], wh, wl, ah[:, cols], al[:, cols], start, False)
        c.used(ins)

    for e, v in ready:
        e(T, v)
    head = min(4, nb - 2)
    loops = (nb - 2 - head) // RING
    for k in range(head):
        outer(Blk(n0 + k), k, k == 0)
    if loops:
        with T.Fori(0, loops, 1) as i:
            for u in range(RING):
                outer(Blk(n0 + head + u, i, RING), i * RING + (head + u), False)
    for k in range(head + loops * RING, nb - 2):
        outer(Blk(n0 + k), k, False)
    for k in range(head):
        c.split_hi(Blk(n0 + k))
    if loops:
        with A.Fori(0, loops, 1) as i:
            for u in range(RING):
                c.split_hi(Blk(n0 + head + u, i, RING))
    for k in range(head + loops * RING, nb - 2):
        c.split_hi(Blk(n0 + k))
    b0, b1 = Blk(n0 + nb - 2), Blk(n0 + nb - 1)
    c.norm_begin()
    c.s_hh_base = c.s_hh.n
    x_base, acc_base = c.s_x.n, c.s_acc.n
    c.use(b0)
    c.use(b1)
    for m in range(KT):
        for b, k in ((b0, nb - 2), (b1, nb - 1)):
            wh, wl = rows(b, m)
            cols = slice(k * SEQ, (k + 1) * SEQ)
            ins = c.mm3(c.ps[:, m, :], wh, wl, ah[:, cols], al[:, cols], False, k == nb - 1)
            if m == KT - 1:
                c.used(ins)
        if m < KT - 1:
            c.s_acc.up(ins)
        if m >= 2:
            if m == 2:
                wt(T, c.s_x, x_base + 1)
            c.sum_squares(m - 2, KT, 0, 0, TT)
    c.acc_last = c.s_used.h, n0 + nb + PRIME
    c.sum_squares(KT - 2, KT, 0, 0, TT)
    c.sum_squares(KT - 1, KT, 0, 0, TT)
    c.split_hi(b0)
    h, gain, norder = nxt
    for m in range(KT):
        if m < KT - 1:
            wt(V, c.s_acc, acc_base + m + 1)
        else:
            V.wait_ge(*c.acc_last)
        c.s_x.up(V.tensor_tensor(order(c.x[:, m, :]), tokens(c.ps[:, m, :], order), order(c.x[:, m, :]), ALU.add))
        if h is not None:
            norm_tile(c, h, m, gain, norder, x_base + m + 1)
            if m >= 1:
                norm_tile_lo(c, h, m - 1, gain, norder)
        else:
            c.square(c.x[:, m, :], m, SEQ, c.s_x.h, x_base + m + 1)
    if h is not None:
        norm_tile_lo(c, h, KT - 1, gain, norder)
    c.split_hi(b1)
    c.s_used.n = n0 + nb + PRIME


def natural(ap):
    return ap


def residues(ap):
    return ap.rearrange("p (j r) -> p r j", r=DIL)


def tokens(ap, order):
    return ap if order is natural else ap.rearrange("p (r j) -> p r j", r=DIL)


class Attention:

    def __init__(self, c, name, nbuf, s_bank, t_bank, width, sink=None, bias=True):
        nc = c.nc
        self.c, self.nbuf, self.s_bank, self.t_bank, self.width, self.sink = c, nbuf, s_bank, t_bank, width, sink
        self.bias = bias
        mk = lambda n, e: Sem(nc, name + n, e)
        self.qk_, self.t_, self.pv_, self.ot_ = (mk(n, c.T) for n in ("qk", "t", "pv", "ot"))
        self.ttr_, self.sink_, self.on_, self.olo_ = (mk(n, c.V) for n in ("ttr", "sink", "on", "olo"))
        self.exp_, self.pt_, self.e8_, self.ohi_ = (mk(n, c.A) for n in ("exp", "pt", "e8", "ohi"))
        self.prob = [c.ctx(name + f"prob{i}", [P, width]) for i in range(2)]
        self.probT = [c.ctx(name + f"probT{i}", [P, width]) for i in range(2)]
        self.nm = [c.ctx(name + f"nm{i}", [P, 8]) for i in range(2)]
        self.den = [c.ctx(name + f"den{i}", [P, 8]) for i in range(2)]
        self.tmp8 = c.ctx(name + "tmp8", [P, 8])
        self.osb = c.ctx(name + "osb", [P, 512])

    def u(self, tile, s, sem):
        return tile * 8 + (s + 1 + PRIME)

    def qk(self, tile, s, pieces, extra=()):
        T = self.c.T
        for sem, v in extra:
            wt(T, sem, v)
        wt(T, self.ttr_, self.u(tile, s - self.nbuf, 0))
        for cols, q, k in pieces:
            ins = T.matmul(self.c.flat(self.s_bank + (s % self.nbuf), cols[0], cols[1]), q, k, start=True, stop=True)
        ins.then_inc(self.qk_.h, 1)

    def ttr(self, tile, s, par, n, bias):
        c = self.c
        V = c.V
        wt(V, self.qk_, self.u(tile, s, 0))
        wt(V, self.t_, self.u(tile, s - 2, 0))
        c.absorb(V)
        src = c.flat(self.s_bank + (s % self.nbuf), 0, n)
        V.tensor_tensor_reduce(self.prob[s % 2][:, 0:n], src, bias, -(HD ** -0.5), 3e38, ALU.add, ALU.min,
                               self.nm[par][:, s:s + 1]).then_inc(self.ttr_.h, 1)

    def exp(self, tile, s, par, n):
        A = self.c.A
        wt(A, self.ttr_, self.u(tile, s, 0))
        p = self.prob[s % 2][:, 0:n]
        A.activation(p, p, ACT.Exp, bias=self.nm[par][:, s:s + 1], scale=-1.0,
                     accum_out=self.den[par][:, s:s + 1]).then_inc(self.exp_.h, 1)

    def transpose(self, tile, s, n):
        c = self.c
        wt(c.T, self.exp_, self.u(tile, s, 0))
        wt(c.T, self.pt_, self.u(tile, s - self.nbuf, 0))
        for k in range(n // P):
            ins = c.T.transpose(c.flat(self.t_bank + (s % self.nbuf), k * P, P),
                                self.prob[s % 2][:, k * P:(k + 1) * P], c.ident[:, :])
        ins.then_inc(self.t_.h, 1)

    def copy_pt(self, tile, s, n):
        c = self.c
        wt(c.A, self.t_, self.u(tile, s, 0))
        wt(c.A, self.pv_, self.u(tile, s - 2, 0))
        c.A.activation(self.probT[s % 2][:, 0:n], c.flat(self.t_bank + (s % self.nbuf), 0, n),
                       ACT.Copy).then_inc(self.pt_.h, 1)

    def pv(self, tile, s, vs, col):
        c = self.c
        wt(c.T, self.pt_, self.u(tile, s, 0))
        if s == 0:
            wt(c.T, self.on_, tile + PRIME)
        for k, v in enumerate(vs):
            ins = c.T.matmul(c.flat(self.o_bank, col, HD), self.probT[s % 2][:, k * P:(k + 1) * P], v,
                             start=k == 0, stop=k == len(vs) - 1)
        ins.then_inc(self.pv_.h, 1)

    def norm_out(self, tile, par, perm):
        c = self.c
        V = c.V
        wt(V, self.exp_, self.u(tile, 7, 0))
        c.absorb(V)
        if self.sink is not None:
            V.tensor_tensor(self.tmp8[:, :], self.nm[par][:, :], self.sink(tile), ALU.add).then_inc(self.sink_.h, 1)
            wt(V, self.e8_, tile + 1 + PRIME)
            V.tensor_tensor(self.den[par][:, :], self.den[par][:, :], self.tmp8[:, :], ALU.add)
            V.drain()
        V.reciprocal(self.den[par][:, :], self.den[par][:, :])
        V.drain()
        wt(V, self.pv_, self.u(tile, 7, 0))
        wt(V, self.ot_, tile + PRIME)
        V.tensor_tensor(self.osb[:, :].rearrange("p (u d) -> p u d", u=8),
                        c.flat(self.o_bank, 0, 512).rearrange("p (u d) -> p u d", u=8),
                        perm(self.den[par][:, :]), ALU.mult).then_inc(self.on_.h, 1)

    def sink_exp(self, tile):
        c = self.c
        wt(c.A, self.sink_, tile + 1 + PRIME)
        c.A.activation(self.tmp8[:, :], self.tmp8[:, :], ACT.Exp).then_inc(self.e8_.h, 1)

    def turn(self, tile):
        c = self.c
        wt(c.T, self.on_, tile + 1 + PRIME)
        wt(c.T, self.olo_, tile + PRIME)
        for b in range(4):
            ins = c.T.transpose(c.flat(self.ot_bank, b * P, P), self.osb[:, b * P:(b + 1) * P], c.ident[:, :])
        ins.then_inc(self.ot_.h, 1)

    def out_hi(self, tile, dst):
        c = self.c
        wt(c.A, self.ot_, tile + 1 + PRIME)
        c.absorb(c.A)
        c.A.activation(dst[:, bass.ds(tile * 512, 512)], c.flat(self.ot_bank, 0, 512),
                       ACT.Copy).then_inc(self.ohi_.h, 1)

    def out_lo(self, tile, dst, hi):
        c = self.c
        wt(c.V, self.ohi_, tile + 1 + PRIME)
        cols = bass.ds(tile * 512, 512)
        c.V.tensor_tensor(dst[:, cols], c.flat(self.ot_bank, 0, 512), hi[:, cols].bitcast(F32),
                          ALU.subtract).then_inc(self.olo_.h, 1)

    def finish(self, tiles):
        for s in (self.qk_, self.t_, self.pv_, self.ttr_, self.exp_, self.pt_):
            s.n = PRIME + 8 * tiles
        for s in (self.ot_, self.on_, self.olo_, self.ohi_):
            s.n = PRIME + tiles


def window_attention(c, n0, h, ah, al):
    nc, T, V, A = c.nc, c.T, c.V, c.A
    dist = c.ctx("dist0", [P, 3 * P])
    bias = [[c.ctx(f"bias0_{i}{e}", [P, 3 * P]) for e in range(2)] for i in range(2)]
    kT = c.ctx("kT", [P, SEQ])
    vS = c.ctx("vS", [P, TT, P])
    qT = [c.ctx(f"qT{i}", [P, SEQ]) for i in range(2)]
    sinks = c.ctx("sinks", [P, 64])
    at = Attention(c, "wa_", 2, 2, 4, 3 * P, sink=lambda tile: sinks[:, bass.ds(tile * 8, 8)])
    at.o_bank, at.ot_bank = 0, 1
    pb = (6, 7)
    ev = Sem(nc, "wa_ev", V)
    em = Sem(nc, "wa_em", A)
    pj = Sem(nc, "wa_pj", T)
    bs = Sem(nc, "wa_bs", A)
    d_c = nc.alloc_semaphore("d_wa")
    c.A.dma_start(dist[:, :], c.io["dist0"]).then_inc(d_c, 16)
    c.A.dma_start(sinks[:, :], c.io["sinks"]).then_inc(d_c, 16)
    A.wait_ge(d_c, 32)
    V.wait_ge(d_c, 32)

    def keys(b):
        lo, hi = max(b - 1, 0), min(b + 1, TT - 1)
        return lo, hi - lo + 1

    def unit(s):
        b, e = s // 2, s % 2
        lo, nk = keys(b)
        return b, e, lo, nk, nk * P

    def chunk(b, m, cpos, ks):
        if ks[0] == 0:
            c.use(b)
            if cpos < 2:
                wt(T, em, m * 2 + (PRIME - 1 + cpos))
            elif cpos < 8:
                wt(T, ev, m * 6 + (PRIME + cpos - 1))
        bank = pb[cpos % 2]
        if cpos == 1:
            wh = c.w_hi[:, b.slot, :].rearrange("p (k m) -> p k m", k=KT)
            wl = c.w_lo[:, b.slot, :].rearrange("p (k m) -> p k m", k=KT)
            for t in range(TT):
                for k in range(KT):
                    ins = c.mm3(c.ps[:, bank, t * P:(t + 1) * P], wh[:, k, :], wl[:, k, :],
                                h[0][:, k, t * P:(t + 1) * P], h[1][:, k, t * P:(t + 1) * P],
                                k == 0, k == KT - 1, w_is_lhs=False)
        elif cpos >= 6:
            ins = c.mod_chunk(b, c.ps[:, bank, :], ks)
        else:
            ins = c.feat_chunk(b, c.ps[:, bank, :], h, ks)
        if ks[-1] == KT - 1:
            c.used(ins)

    def blocks(m):
        return [Blk(n0 + u, m, 8) for u in range(8)]

    with T.Fori(0, 2, 1) as m:
        bl = blocks(m)
        for cpos in range(3):
            chunk(bl[cpos], m, cpos, range(KT))
        for i in range(4):
            tile = m * 4 + i
            for s in range(8):
                if i < 3:
                    chunk(bl[3 + i], m, 3 + i, [s])
                else:
                    chunk(bl[6 + s // 4], m, 6 + s // 4, [2 * (s % 4), 2 * (s % 4) + 1])
                b, e, lo, nk, n = unit(s)
                rows = slice(HD * e, HD * e + HD)
                at.qk(tile, s, [((0, n), qT[i % 2][rows, b * P:(b + 1) * P], kT[rows, lo * P:lo * P + n])],
                      extra=[(ev, m * 6 + (PRIME + 3 + i))] if s == 0 else ())
                if s >= 1:
                    at.transpose(tile, s - 1, unit(s - 1)[4])
                if s >= 2:
                    b2, e2, lo2, nk2, _ = unit(s - 2)
                    at.pv(tile, s - 2, [vS[:, lo2 + k, HD * e2:HD * e2 + HD] for k in range(nk2)], (s - 2) * HD)
                if s == 3 and i > 0:
                    at.turn(m * 4 + (i - 1))
            at.transpose(tile, 7, unit(7)[4])
            for s in (6, 7):
                b2, e2, lo2, nk2, _ = unit(s)
                at.pv(tile, s, [vS[:, lo2 + k, HD * e2:HD * e2 + HD] for k in range(nk2)], s * HD)
        at.turn(m * 4 + 3)

    with V.Fori(0, 2, 1) as m:
        def evac(cpos):
            V.wait_ge(c.s_used.h, m * 8 + (n0 + cpos + 1 + PRIME))
            bank = pb[cpos % 2]
            if cpos == 0:
                ins = V.tensor_tensor(kT[:, :], c.ps[:, bank, :], c.RB[:, 0:SEQ], ALU.mult)
            elif cpos == 1:
                ins = V.tensor_tensor(vS[:, :, :], c.ps[:, bank, :].rearrange("p (t n) -> p t n", t=TT),
                                      c.r_tok[:, 0, 0:TT].unsqueeze(2).broadcast_to([P, TT, P]), ALU.mult)
            else:
                ins = V.tensor_tensor(qT[cpos % 2][:, :], c.ps[:, bank, :], c.RB[:, 0:SEQ], ALU.mult)
            ins.then_inc(ev.h, 1)
        for cpos in range(3):
            evac(cpos)
        for i in range(4):
            tile = m * 4 + i
            for s in range(8):
                b, e, lo, nk, n = unit(s)
                if s == 0:
                    wt(V, bs, m * 4 + (i + 1 + PRIME))
                off = P * (lo - b + 1)
                at.ttr(tile, s, i % 2, n, bias[i % 2][e][:, off:off + n])
                if s == 6 and i > 0:
                    at.out_lo(m * 4 + (i - 1), al, ah)
            if i < 3:
                evac(3 + i)
            at.norm_out(tile, i % 2, lambda r: r.unsqueeze(2).broadcast_to([P, 8, HD]))
        at.out_lo(m * 4 + 3, al, ah)

    with A.Fori(0, 2, 1) as m:
        bl = blocks(m)

        def make_bias(i):
            wt(A, at.ttr_, at.u(m * 4 + i, -9, 0))
            c.absorb(A)
            for e in range(2):
                ins = A.activation(bias[i % 2][e][:, :], dist[:, :], ACT.Copy,
                                   scale=c.slope[:, bass.ds((m * 4 + i) * 2 + e, 1)])
            ins.then_inc(bs.h, 1)
        for cpos in range(3):
            c.split_hi(bl[cpos])
        make_bias(0)
        for i in range(4):
            tile = m * 4 + i
            if i < 3:
                c.split_hi(bl[3 + i])
                make_bias(i + 1)
            for s in range(8):
                at.exp(tile, s, i % 2, unit(s)[4])
                if s >= 1:
                    at.copy_pt(tile, s - 1, unit(s - 1)[4])
                if s == 5 and i > 0:
                    at.out_hi(m * 4 + (i - 1), ah)
                if i == 3 and s in (3, 7):
                    c.split_hi(bl[6 + s // 4])
            at.copy_pt(tile, 7, unit(7)[4])
            at.sink_exp(tile)
        for q in range(2):
            A.wait_ge(c.s_used.h, m * 8 + (n0 + 6 + q + 1 + PRIME))
            c.absorb(A)
            A.activation(c.modraw[1][:, bass.ds((m * 2 + q) * 4, 4)], c.ps[:, pb[q], 0:4], ACT.Copy).then_inc(em.h, 1)
        at.out_hi(m * 4 + 3, ah)
    at.finish(8)
    ev.n, em.n, bs.n = PRIME + 12, PRIME + 4, PRIME + 8
    return [(lambda e, v: wt(e, v), s) for s in (at.olo_, ev, em)]


def dilated_attention(c, n0, h, ah, al):
    nc, T, V, A = c.nc, c.T, c.V, c.A
    W1 = SEQ
    NK = W1 + 2 * P
    dist = c.ctx("dist1", [P, DIL * NK])
    bias = [c.ctx(f"bias1_{i}", [P, NK]) for i in range(2)]
    qT = [[c.ctx(f"dqT{i}{g}", [P, SEQ]) for g in range(3)] for i in range(2)]
    kT = [[c.ctx(f"dkT{i}{g}", [P, SEQ]) for g in range(3)] for i in range(2)]
    vS = [[c.ctx(f"dvS{i}{g}", [P, DIL, P]) for g in range(3)] for i in range(2)]
    at = Attention(c, "da_", 1, 2, 4, NK)
    at.o_bank, at.ot_bank = 0, 1
    pb = (6, 7)
    ev = Sem(nc, "da_ev", V)
    em = Sem(nc, "da_em", A)
    bs = Sem(nc, "da_bs", A)
    d_c = nc.alloc_semaphore("d_da")
    A.wait_ge(c.s_x.h, c.s_x.n)
    c.A.dma_start(dist[:, :], c.io["dist1"]).then_inc(d_c, 16)
    A.wait_ge(d_c, 16)

    def tokens_of(s):
        e, r = s // 4, s % 4
        return e, r, slice(HD * e, HD * e + HD)

    def pe(j, par, bl, proj, attn):
        tile = j - 1
        q, k, v = qT[1 - par], kT[1 - par], vS[1 - par]
        for s in range(12):
            if proj:
                b, bank = bl[s], pb[s % 2]
                c.use(b)
                if s < 2:
                    wt(T, em, j * 3 + (PRIME + s - 1))
                elif s < 11:
                    wt(T, ev, j * 9 + (PRIME + s - 1))
                else:
                    wt(T, em, j * 3 + (PRIME + 1))
                if s >= 9:
                    ins = c.mod_chunk(b, c.ps[:, bank, :], range(KT))
                elif s % 3 == 2:
                    wh = c.w_hi[:, b.slot, :].rearrange("p (k m) -> p k m", k=KT)
                    wl = c.w_lo[:, b.slot, :].rearrange("p (k m) -> p k m", k=KT)
                    for t in range(DIL):
                        for kk in range(KT):
                            ins = c.mm3(c.ps[:, bank, t * P:(t + 1) * P], wh[:, kk, :], wl[:, kk, :],
                                        h[0][:, kk, t * P:(t + 1) * P], h[1][:, kk, t * P:(t + 1) * P],
                                        kk == 0, kk == KT - 1, w_is_lhs=False)
                else:
                    ins = c.feat_chunk(b, c.ps[:, bank, :], h, range(KT))
                c.used(ins)
            if not attn:
                continue
            if s < 8:
                e, r, rows = tokens_of(s)
                own = slice(r * P, (r + 1) * P)
                at.qk(tile, s, [((0, W1), q[0][rows, own], k[0][rows, :]),
                                ((W1, P), q[1][rows, own], k[1][rows, own]),
                                ((W1 + P, P), q[2][rows, own], k[2][rows, own])],
                      extra=[(ev, tile * 9 + (9 + PRIME))] if s == 0 else ())
            if 1 <= s <= 8:
                at.transpose(tile, s - 1, NK)
            if 2 <= s <= 9:
                e, r, _ = tokens_of(s - 2)
                cols = slice(HD * e, HD * e + HD)
                at.pv(tile, s - 2, [v[0][:, t, cols] for t in range(DIL)] + [v[1][:, r, cols], v[2][:, r, cols]],
                      (2 * r + e) * HD)
            if s == 11:
                at.turn(tile)

    def ve(j, par, proj, attn):
        tile = j - 1
        for s in range(12):
            if proj and s < 9:
                V.wait_ge(c.s_used.h, j * 12 + (n0 + s + 1 + PRIME))
                g, what = s // 3, s % 3
                src = c.ps[:, pb[s % 2], :]
                if what == 2:
                    V.tensor_tensor(vS[par][g][:, :, :], src.rearrange("p (t n) -> p t n", t=DIL),
                                    c.r_tok[:, 0, 0:DIL].unsqueeze(2).broadcast_to([P, DIL, P]),
                                    ALU.mult).then_inc(ev.h, 1)
                else:
                    V.tensor_tensor((qT, kT)[what][par][g][:, :], src, c.RB[:, 0:SEQ], ALU.mult).then_inc(ev.h, 1)
            if attn and s < 8:
                e, r, _ = tokens_of(s)
                wt(V, bs, at.u(tile, s, 0))
                at.ttr(tile, s, 1 - par, NK, bias[s % 2][:, :])
            if attn and s == 10:
                at.norm_out(tile, 1 - par, lambda d: d.rearrange("p (e r) -> p r e", e=2).unsqueeze(3)
                            .broadcast_to([P, 4, 2, HD]))
        if attn:
            at.out_lo(tile, al, ah)

    def ac(j, par, bl, proj, attn):
        tile = j - 1

        def make_bias(s):
            e, r, _ = tokens_of(s)
            wt(A, at.ttr_, at.u(tile, s - 2, 0))
            c.absorb(A)
            A.activation(bias[s % 2][:, :], dist[:, r * NK:(r + 1) * NK], ACT.Copy,
                         scale=c.slope[:, bass.ds(tile * 2 + (16 + e), 1)]).then_inc(bs.h, 1)
        for s in range(12):
            if proj:
                c.split_hi(bl[s])
            if attn and s == 0:
                make_bias(0)
                make_bias(1)
            if attn and s < 8:
                at.exp(tile, s, 1 - par, NK)
            if attn and s < 6:
                make_bias(s + 2)
            if attn and 1 <= s <= 8:
                at.copy_pt(tile, s - 1, NK)
            if proj and s >= 9:
                A.wait_ge(c.s_used.h, j * 12 + (n0 + s + 1 + PRIME))
                c.absorb(A)
                A.activation(c.modraw[0][:, bass.ds((j * 3 + (s - 9)) * 4, 4)], c.ps[:, pb[s % 2], 0:4],
                             ACT.Copy).then_inc(em.h, 1)
        if attn:
            at.out_hi(tile, ah)

    for eng, part in ((T, pe),
                      (V, lambda j, par, bl, proj, attn: ve(j, par, proj, attn)),
                      (A, ac)):
        part(0, 0, [Blk(n0 + u) for u in range(12)], True, False)
        with eng.Fori(0, 3, 1) as i:
            for q in range(2):
                part(i * 2 + (q + 1), (q + 1) % 2, [Blk(n0 + 12 * (q + 1) + u, i, 24) for u in range(12)],
                     True, True)
        part(7, 1, [Blk(n0 + 84 + u) for u in range(12)], True, True)
        part(8, 0, None, False, True)
    at.finish(8)
    ev.n, em.n, bs.n = PRIME + 72, PRIME + 24, PRIME + 64
    return [(lambda e, v: wt(e, v), s) for s in (at.olo_, ev, em)]


def swiglu(c, n0, name, h, mh, ml, mod):
    nc, T, V, A = c.nc, c.T, c.V, c.A
    per = 3 if mod else 2
    pairs = 20 if mod else FT
    unroll = 4 if mod else 2
    gr = [c.ctx(name + f"gr{i}", [P, SEQ]) for i in range(2)]
    ur = [c.ctx(name + f"ur{i}", [P, SEQ]) for i in range(2)]
    s_gr, s_ur, s_m = (Sem(nc, name + x, V) for x in ("s_gr", "s_ur", "s_m"))
    s_sl, s_mh, s_md = (Sem(nc, name + x, A) for x in ("s_sl", "s_mh", "s_md"))
    s_ml = Sem(nc, name + "s_ml", V)

    def pe(j, q, b, withmod):
        g_bank, u_bank = 2 + 2 * (q % 2), 3 + 2 * (q % 2)
        c.use(b[0])
        wt(T, s_gr, j + (PRIME - 1))
        c.used(c.feat_chunk(b[0], c.ps[:, g_bank, :], h, range(KT)))
        c.use(b[1])
        wt(T, s_ur, j + (PRIME - 1))
        c.used(c.feat_chunk(b[1], c.ps[:, u_bank, :], h, range(KT)))
        if withmod:
            c.use(b[2])
            wt(T, s_md, j + (PRIME - 1))
            c.used(c.mod_chunk(b[2], c.ps[:, 6 + q % 2, :], range(KT)))

    def ve(j, q, used, withmod):
        i = q % 2
        V.wait_ge(c.s_used.h, used + 1)
        wt(V, s_m, j + (PRIME - 1))
        V.tensor_tensor(gr[i][:, :], c.ps[:, 2 + 2 * i, :], c.RB[:, 0:SEQ], ALU.mult).then_inc(s_gr.h, 1)
        V.wait_ge(c.s_used.h, used + 2)
        V.tensor_tensor(ur[i][:, :], c.ps[:, 3 + 2 * i, :], c.RB[:, 0:SEQ], ALU.mult).then_inc(s_ur.h, 1)
        wt(V, s_sl, j + (PRIME + 1))
        wt(V, s_ur, j + (PRIME + 1))
        V.tensor_tensor(ur[i][:, :], gr[i][:, :], ur[i][:, :], ALU.mult).then_inc(s_m.h, 1)
        wt(V, s_mh, j + (PRIME + 1))
        cols = bass.ds(j * SEQ, SEQ)
        V.tensor_tensor(ml[:, cols], ur[i][:, :], mh[:, cols].bitcast(F32), ALU.subtract).then_inc(s_ml.h, 1)

    def ac(j, q, b, used, withmod):
        i = q % 2
        for x in b:
            c.split_hi(x)
        wt(A, s_gr, j + (PRIME + 1))
        A.activation(gr[i][:, :], gr[i][:, :], ACT.Silu).then_inc(s_sl.h, 1)
        wt(A, s_m, j + (PRIME + 1))
        c.absorb(A)
        A.activation(mh[:, bass.ds(j * SEQ, SEQ)], ur[i][:, :], ACT.Copy).then_inc(s_mh.h, 1)
        if withmod:
            A.wait_ge(c.s_used.h, used + 3)
            c.absorb(A)
            A.activation(c.modraw[1][:, bass.ds(j * 4 + 16, 4)], c.ps[:, 6 + q % 2, 0:4], ACT.Copy).then_inc(s_md.h, 1)

    def blks(q, i=0, it=0):
        return [Blk(n0 + per * q + x, i, it) for x in range(per)]

    for eng, part in ((T, lambda j, q, b, u, m: pe(j, q, b, m)), (V, lambda j, q, b, u, m: ve(j, q, u, m)),
                      (A, lambda j, q, b, u, m: ac(j, q, b, u, m))):
        with eng.Fori(0, pairs // unroll, 1) as i:
            for q in range(unroll):
                part(i * unroll + q, q, blks(q, i, per * unroll), i * (per * unroll) + (n0 + per * q + PRIME), mod)
        for j in range(pairs, FT):
            first = n0 + per * pairs + 2 * (j - pairs)
            part(j, j, [Blk(first), Blk(first + 1)], first + PRIME, False)
    for s in (s_gr, s_ur, s_m, s_sl, s_mh, s_ml):
        s.n = PRIME + FT
    s_md.n = PRIME + (pairs if mod else 0)
    return [(lambda e, v: wt(e, v), s) for s in (s_ml, s_md)]



def block_two_layer(c, l, n0, V_):
    nc, T, V, A, S, io = c.nc, c.T, c.V, c.A, c.S, c.io
    both = l == 0
    nt_q = NT if both else TT
    nq = nt_q * P
    vec, modv, ps = c.vec, c.modv, c.ps
    L = f"l{l}_"

    def up(sem, ins):
        return sem.up(ins)

    V.wait_ge(c.s_a.h, c.s_a.n)
    mr = c.modraw[l][:, :].rearrange("p (t k) -> p t k", k=4)
    V.tensor_tensor(modv[:, l, :, :], mr[:, :, 0:2], mr[:, :, 2:4], ALU.add)
    V.drain()
    V.tensor_tensor(modv[:, l, :, :], modv[:, l, :, :],
                    vec[:, V_["b_mod"] + l * MT:V_["b_mod"] + (l + 1) * MT].unsqueeze(2).broadcast_to([P, MT, 2]),
                    ALU.add)
    V.drain()
    amul = c.ctx(L + "amul", [P, KT, 2])
    V.tensor_scalar(amul[:, :, :], modv[:, l, KT:2 * KT, :], 1.0, None, ALU.add)
    V.drain()
    up(c.s_v, V.tensor_tensor(amul[:, :, :], amul[:, :, :],
                              vec[:, V_["norm_g"] + l * KT:V_["norm_g"] + (l + 1) * KT].unsqueeze(2)
                              .broadcast_to([P, KT, 2]), ALU.mult))
    V.drain()

    c.norm_begin()
    for k in range(KT):
        c_src = (c.x[:, k, :], c.y[:, k, :])
        wt(A, c.s_ssq, c.s_ssq_base + k - 1)
        wt(A, c.s_x)
        A.activation(c.sq[:, k % 2, 0:SEQ], c_src[0], ACT.Square)
        up(c.s_sq, A.activation(c.sq[:, k % 2, SEQ:ALLT], c_src[1], ACT.Square))
        if k == 0:
            wt(T, c.s_x)
        c.sum_squares(k, KT, 0, 0, NT)
    c.rstd(0, NT, D_MODEL)
    c.broadcast_rstd(1, NT)

    outer = c.scope()
    h_hi = c.ctx(L + "h_hi", [P, KT, ALLT], F32R)
    h_lo = c.ctx(L + "h_lo", [P, KT, ALLT], F32R)
    h_end = c.offset
    tok = c.scope()
    ag = c.ctx(L + "ag", [P, 4, ALLT])
    spare = c.offset
    cq = c.ctx(L + "cq", [P, 2, ALLT])
    ckv = c.ctx(L + "ckv", [P, ALLT])
    kro = c.ctx(L + "kro", [P, NT, A_ROPE])
    stage1 = c.scope()
    tmp = c.ctx(L + "tmp", [P, 2, ALLT])
    hh0 = c.s_hh.n
    hv0 = c.s_v.n
    hl0 = c.s_hl.n
    for k in range(KT):
        if k >= 2:
            wt(V, c.s_hh, hh0 + k - 1)
        for lo, n, cond, src in ((0, SEQ, 0, c.x), (SEQ, CTX, 1, c.y)):
            ins = V.scalar_tensor_tensor(tmp[:, k % 2, lo:lo + n], src[:, k, :], amul[:, k, cond:cond + 1],
                                         c.RB[:, lo:lo + n], ALU.mult, ALU.mult)
        up(c.s_v, ins)
        wt(A, c.s_v, hv0 + k + 1)
        for lo, n, cond in ((0, SEQ, 0), (SEQ, CTX, 1)):
            ins = A.activation(h_hi[:, k, lo:lo + n], tmp[:, k % 2, lo:lo + n], ACT.Identity,
                               bias=modv[:, l, k, cond:cond + 1])
        up(c.s_hh, ins)
        wt(V, c.s_hh, hh0 + k + 1)
        for lo, n, cond in ((0, SEQ, 0), (SEQ, CTX, 1)):
            ins = V.scalar_tensor_tensor(h_lo[:, k, lo:lo + n], tmp[:, k % 2, lo:lo + n],
                                         modv[:, l, k, cond:cond + 1], h_hi[:, k, lo:lo + n].bitcast(F32),
                                         ALU.add, ALU.subtract)
        up(c.s_hl, ins)
    wt(T, c.s_hl)

    n = n0
    b = Blk(n)
    c.use(b)
    wh, wl = c.w_hi[:, b.slot, :], c.w_lo[:, b.slot, :]
    for t in range(NT):
        for k in range(KT):
            ts = slice(t * P, (t + 1) * P)
            ks = slice(k * A_ROPE, (k + 1) * A_ROPE)
            ins = c.mm3(ps[:, 6, t * A_ROPE:(t + 1) * A_ROPE], wh[:, ks], wl[:, ks],
                        h_hi[:, k, ts], h_lo[:, k, ts], k == 0, k == KT - 1, w_is_lhs=False)
    c.used(ins)
    c.split_hi(b)
    A.wait_ge(c.s_used.h, n + 1 + PRIME)
    up(c.s_a, A.activation(kro[:, :, :].rearrange("p t d -> p (t d)"), ps[:, 6, 0:NT * A_ROPE], ACT.Copy))
    kro_done = c.s_a.n
    n += 1
    tm = c.ctx(L + "tm", [P, NT, 512])
    wt(T, c.s_RB)
    for q in range(4):
        b = Blk(n + q)
        c.use(b)
        wh = c.w_hi[:, b.slot, :].rearrange("p (k n) -> p k n", k=2)
        wl = c.w_lo[:, b.slot, :].rearrange("p (k n) -> p k n", k=2)
        for k in range(2):
            kk = 2 * q + k
            for t in range(nt_q):
                ts = slice(t * P, (t + 1) * P)
                ins = c.mm3(ps[:, t, :], wh[:, k, :], wl[:, k, :], h_hi[:, kk, ts], h_lo[:, kk, ts],
                            kk == 0, kk == KT - 1, w_is_lhs=False)
        c.used(ins)
        c.split_hi(b)
    n += 4
    for t in range(nt_q):
        A.wait_ge(c.s_used.h, n + PRIME)
        up(c.s_a, A.activation(tm[:, t, :], ps[:, t, :], ACT.Copy))
    tm_done = c.s_a.n

    gu = c.ctx(L + "gu", [P, 2, ALLT])
    fg = c.ctx(L + "fg", [P, 2, ALLT])
    rows = (("cq", 0), ("cq", 1), ("ckv", 0), ("gg", 0), ("gg", 1), ("gu", 0), ("gu", 1), ("fg", 0), ("fg", 1),
            ("ag", 0), ("ag", 1), ("ag", 2), ("ag", 3))
    evac = [(c.s_a, tm_done), (c.s_a, kro_done)]
    sq_evac = {}
    for i, (what, kk) in enumerate(rows):
        b = Blk(n + i)
        bank = (6, 4)[i % 2]
        sem, v = evac[-2] if i >= 2 else (c.s_a, tm_done)
        wt(T, sem, v)
        c.use(b)
        wh = c.w_hi[:, b.slot, :].rearrange("p (k m) -> p k m", k=KT)
        wl = c.w_lo[:, b.slot, :].rearrange("p (k m) -> p k m", k=KT)
        wide = both or what in ("cq", "ckv")
        width = ALLT if (both or what == "ckv") else SEQ
        for lo, nn in ((0, SEQ), (SEQ, CTX))[:2 if width == ALLT else 1]:
            for k in range(KT):
                ins = c.mm3(c.flat(bank, lo, nn), wh[:, k, :], wl[:, k, :], h_hi[:, k, lo:lo + nn],
                            h_lo[:, k, lo:lo + nn], k == 0, k == KT - 1)
        c.used(ins)
        c.split_hi(b)
        done = n + i + 1 + PRIME
        src = c.flat(bank, 0, width)
        if what in ("cq", "ckv"):
            A.wait_ge(c.s_used.h, done)
            dst = cq[:, kk, 0:width] if what == "cq" else ckv[:, 0:width]
            gcol = (V_["q_a_g"] + 2 * l + kk) if what == "cq" else V_["kv_a_g"] + l
            A.activation(dst, src, ACT.Copy, scale=vec[:, gcol:gcol + 1])
            c.norm_begin() if kk == 0 else None
            wt(A, c.s_ssq)
            up(c.s_sq, A.activation(c.sq[:, kk % 2, 0:width], src, ACT.Square))
            evac.append((c.s_sq, c.s_sq.n))
            c.sum_squares(kk, 2 if what == "cq" else 1, 0, 0 if what == "cq" else 1, width // P)
            if what == "ckv" or kk == 1:
                c.rstd(0 if what == "cq" else 1, width // P, 256 if what == "cq" else 128,
                       row=1 if what == "cq" else 2)
        elif what == "gu":
            V.wait_ge(c.s_used.h, done)
            wt(V, c.s_a)
            up(c.s_v, V.tensor_tensor(gu[:, kk, 0:width], src, gu[:, kk, 0:width], ALU.mult))
            evac.append((c.s_v, c.s_v.n))
        else:
            dst = {"gg": gu, "fg": fg, "ag": ag}[what]
            A.wait_ge(c.s_used.h, done)
            up(c.s_a, A.activation(dst[:, kk, 0:width], src, ACT.Silu))
            evac.append((c.s_a, c.s_a.n))
    n += 13
    wt(T, c.s_a)
    wt(T, c.s_v)
    wt(V, c.s_a)
    wt(A, c.s_v)

    m_hi = nc.alloc_sbuf_tensor_at(L + "m_hi", [P, KT, ALLT], F32R, offset=h_end - 2 * KT * ALLT * 4)
    m_lo = nc.alloc_sbuf_tensor_at(L + "m_lo", [P, KT, ALLT], F32R, offset=h_end - KT * ALLT * 4)
    V.wait_ge(c.s_used.h, n + PRIME)
    A.wait_ge(c.s_used.h, n + PRIME)

    def split_out(kk, src, width):
        wt(A, c.s_v)
        up(c.s_hh, A.activation(m_hi[:, kk, 0:width], src, ACT.Copy))
        wt(V, c.s_hh)
        up(c.s_hl, V.tensor_tensor(m_lo[:, kk, 0:width], src, m_hi[:, kk, 0:width].bitcast(F32), ALU.subtract))

    ua = h_end - KT * ALLT * 4 - 4 * ALLT * 4
    ub = h_end - 4 * ALLT * 4
    at_ = lambda name, shape, off: nc.alloc_sbuf_tensor_at(L + name, shape, F32, offset=off)
    dft = [at_(f"dft{a}", [P, TT, SEQ], (ua, ub)[a]) for a in range(2)]
    dfc = [at_(f"dfc{a}", [P, 2, CTX], (ua, ub)[a] + TT * SEQ * 4) for a in range(2)]
    wfm = at_("wfm", [P, 2, 256], ua + (TT * SEQ + 2 * CTX) * 4)
    wsT = at_("wsT", [P, 4, P], ub + (TT * SEQ + 2 * CTX) * 4)
    dfd = c.ctx(L + "dfd", [P, 2, P])
    bsb = c.ctx(L + "bsb", [P, 2, P])
    glg = c.ctx(L + "glg", [P, HD])
    d_s1 = nc.alloc_semaphore(L + "d_s1")
    loads = [(dft[a][:, :, :], io["dft"][:, a]) for a in range(2)]
    loads += [(dfd[:, :, :].rearrange("p a n -> p (a n)"), io["dfd"]),
             (wfm[:, :, :].rearrange("p a n -> p (a n)"), io["wfmix"][l]),
             (wsT[:, :, :].rearrange("p a n -> p (a n)"), io["gws"][l]),
             (bsb[:, :, :].rearrange("p a n -> p (a n)"), io["gbs"][l]),
             (glg[:, :], io["glg"][l])]
    if both:
        loads += [(dfc[a][:, :, :], io["dfc"][:, a]) for a in range(2)]
    for d, s in loads:
        A.dma_start(d, s).then_inc(d_s1, 16)
    T.wait_ge(d_s1, 16 * len(loads))
    V.wait_ge(d_s1, 16 * len(loads))

    U = c.ctx(L + "U", [P, 2, 2, ALLT])
    u_done = [0, 0]
    for ft in range(2):
        fs = slice(ft * P, (ft + 1) * P)
        for a in range(2):
            bank = (0, 2)[a]
            if ft:
                wt(T, c.s_a, u_done[a])
            for t in range(TT):
                ins = T.matmul(ps[:, bank, :], tm[:, t, fs], dft[a][:, t, :], start=t == 0, stop=t == TT - 1)
            if both:
                for t in range(2):
                    ins = T.matmul(ps[:, bank + 1, 0:CTX], tm[:, TT + t, fs], dfc[a][:, t, :], start=t == 0, stop=t == 1)
            up(c.s_t, ins)
            wt(A, c.s_t)
            up(c.s_a, A.activation(U[:, a, ft, 0:nq], c.flat(bank, 0, nq), ACT.Copy))
            u_done[a] = c.s_a.n
    F_ = c.ctx(L + "F", [P, 2, ALLT])
    pieces = ((0, SEQ), (SEQ, CTX))[:2 if both else 1]
    wt(T, c.s_a)
    for ft in range(2):
        bank = (4, 6)[ft]
        for lo, nn in pieces:
            T.matmul(c.flat(bank, lo, nn), dfd[:, 0, :], U[:, 0, ft, lo:lo + nn], start=True, stop=False)
            ins = T.matmul(c.flat(bank, lo, nn), dfd[:, 1, :], U[:, 1, ft, lo:lo + nn], start=False, stop=True)
        up(c.s_t, ins)
        wt(A, c.s_t)
        up(c.s_a, A.activation(F_[:, ft, 0:nq], c.flat(bank, 0, nq), ACT.Copy))
    wt(T, c.s_a)
    for ft in range(2):
        bank = (0, 2)[ft]
        for lo, nn in pieces:
            for k in range(2):
                ins = T.matmul(c.flat(bank, lo, nn), wfm[:, k, ft * P:(ft + 1) * P], F_[:, k, lo:lo + nn],
                               start=k == 0, stop=k == 1)
        up(c.s_t, ins)
        wt(V, c.s_t)
        up(c.s_v, V.tensor_tensor(fg[:, ft, 0:nq], c.flat(bank, 0, nq), fg[:, ft, 0:nq], ALU.mult))
        split_out(ft, fg[:, ft, 0:nq], nq)

    st = c.ctx(L + "st", [P, 2, NT * 4])
    gv = tm[:, 0:nt_q, 256:512].rearrange("p t (h d) -> p t h d", h=4)
    sqv = c.ctx(L + "sqv", [P, NT, 4, HD])
    ng = nt_q * 4

    def groups(ap):
        return ap.rearrange("p (t h) -> p t h", h=4)

    def wide_(ap):
        return groups(ap).unsqueeze(3).broadcast_to([P, nt_q, 4, HD])

    V.tensor_reduce(groups(st[:, 0, 0:ng]), gv, AX.X, ALU.add)
    V.drain()
    V.tensor_scalar(st[:, 0, 0:ng], st[:, 0, 0:ng], 1.0 / HD, None, ALU.mult)
    V.drain()
    for t in range(nt_q):
        g4 = gv[:, t]
        V.tensor_tensor(g4, g4, st[:, 0, 4 * t:4 * t + 4].unsqueeze(2).broadcast_to([P, 4, HD]), ALU.subtract)
    V.drain()
    for t in range(nt_q):
        V.tensor_tensor(sqv[:, t], gv[:, t], gv[:, t], ALU.mult)
    V.drain()
    up(c.s_v, V.tensor_reduce(groups(st[:, 1, 0:ng]), sqv[:, 0:nt_q], AX.X, ALU.add))
    wt(A, c.s_v)
    up(c.s_a, A.activation(st[:, 1, 0:ng], st[:, 1, 0:ng], ACT.Sqrt, bias=EPS, scale=1.0 / HD))
    wt(V, c.s_a)
    V.reciprocal(st[:, 1, 0:ng], st[:, 1, 0:ng])
    V.drain()
    for t in range(nt_q):
        g4 = gv[:, t]
        V.tensor_tensor(g4, g4, st[:, 1, 4 * t:4 * t + 4].unsqueeze(2).broadcast_to([P, 4, HD]), ALU.mult)
    V.drain()
    for t in range(nt_q):
        g4 = gv[:, t]
        ins = V.tensor_tensor(g4, g4, glg[:, :].unsqueeze(1).broadcast_to([P, 4, HD]), ALU.mult)
    up(c.s_v, ins)
    wt(T, c.s_v)
    for pr in range(2):
        bank = (4, 6)[pr]
        for t in range(nt_q):
            for e in range(2):
                hd = 2 * pr + e
                ins = T.matmul(c.flat(bank, t * P, P)[HD * e:HD * e + HD], tm[:, t, 256 + hd * HD:256 + (hd + 1) * HD],
                               wsT[:, hd, :], start=True, stop=True)
        up(c.s_t, ins)
        wt(V, c.s_t)
        mixed = sqv[:, :, :, :].rearrange("p t h d -> p (t h d)")[:, pr * ALLT:pr * ALLT + nq]
        V.tensor_tensor(mixed.rearrange("p (t n) -> p t n", n=P), c.flat(bank, 0, nq).rearrange("p (t n) -> p t n", n=P),
                        bsb[:, pr, :].unsqueeze(1).broadcast_to([P, nt_q, P]), ALU.add)
        V.drain()
        up(c.s_v, V.tensor_tensor(mixed, mixed, gu[:, pr, 0:nq], ALU.mult))
        split_out(2 + pr, mixed, nq)
    wt(A, c.s_hl)
    wt(T, c.s_hl)
    c.close(stage1)

    kT = c.ctx(L + "kT", [A_QK, A_HEADS, ALLT])
    qT = c.ctx(L + "qT", [A_QK, A_HEADS, ALLT])
    vS = c.ctx(L + "vS", [P, NT, A_HEADS * A_V])
    stage2 = c.scope()
    gains = c.ctx(L + "gains", [P, 2, A_QK])
    rope = c.ctx(L + "rope", [P, 2, TT, A_ROPE])
    small = c.ctx(L + "small", [P, 2, A_HEADS])
    wuq = nc.alloc_sbuf_tensor_at(L + "wuq", [P, 2, A_HEADS * A_QK], F32, offset=ua)
    wukv = nc.alloc_sbuf_tensor_at(L + "wukv", [P, 1024], F32, offset=ua + 2 * ALLT * 4)
    work = nc.alloc_sbuf_tensor_at(L + "work", [P, 2, A_HEADS, A_QK], F32, offset=ub)
    wsq = nc.alloc_sbuf_tensor_at(L + "wsq", [P, A_HEADS, A_QK], F32, offset=ub + 2 * ALLT * 4)
    rtmp = c.ctx(L + "rtmp", [P, A_HEADS, A_ROPE])
    d_s2 = nc.alloc_semaphore(L + "d_s2")
    loads = [(wuq[:, :, :].rearrange("p a n -> p (a n)"), io["wuq"][l]), (wukv[:, :], io["wukv"][l]),
             (gains[:, :, :].rearrange("p a n -> p (a n)"), io["qkg"][l]),
             (rope[:, :, :, :].rearrange("p a b n -> p (a b n)"), io["rope"])]
    for d, s in loads:
        A.dma_start(d, s).then_inc(d_s2, 16)
    T.wait_ge(d_s2, 16 * len(loads))
    V.wait_ge(d_s2, 16 * len(loads))
    V.tensor_scalar(gains[:, 0, :], gains[:, 0, :], A_QK ** -0.5, None, ALU.mult)
    V.drain()

    jobs = [("k", t) for t in range(NT)] + [("q", t) for t in range(nt_q)]
    turned = []
    evicted = []
    for i, (what, t) in enumerate(jobs):
        bank = (0, 2)[i % 2]
        w = work[:, i % 2]
        wflat = w.rearrange("p h d -> p (h d)")
        ts = slice(t * P, (t + 1) * P)
        if i >= 2:
            wt(T, c.s_a, evicted[i - 2])
        if what == "k":
            for half in range(2):
                ins = T.matmul(ps[:, bank + half, :], ckv[:, ts], wukv[:, half * 512:(half + 1) * 512],
                               start=True, stop=True)
        else:
            for half in range(2):
                for k in range(2):
                    ins = T.matmul(ps[:, bank + half, 0:384], cq[:, k, ts], wuq[:, k, half * 384:(half + 1) * 384],
                                   start=k == 0, stop=k == 1)
        up(c.s_t, ins)
        wt(A, c.s_t)
        if i >= 2:
            wt(A, c.s_t, turned[i - 2])
        if what == "k":
            r = c.r_tok[:, 2, t:t + 1]
            A.activation(vS[:, t, :], ps[:, bank + 1, :], ACT.Copy, scale=r)
            up(c.s_a, A.activation(w[:, :, 0:A_NOPE], ps[:, bank, :].rearrange("p (h d) -> p h d", h=A_HEADS),
                                   ACT.Copy, scale=r))
            evicted.append(c.s_a.n)
            A.drain()
            A.activation(w[:, :, A_NOPE:A_QK], kro[:, t, :].unsqueeze(1).broadcast_to([P, A_HEADS, A_ROPE]), ACT.Copy)
            gain = gains[:, 1, :]
        else:
            r = c.r_tok[:, 1, t:t + 1]
            for half in range(2):
                ins = A.activation(wflat[:, half * 384:(half + 1) * 384], ps[:, bank + half, 0:384], ACT.Copy, scale=r)
            up(c.s_a, ins)
            evicted.append(c.s_a.n)
            gain = gains[:, 0, :]
        A.drain()
        if i:
            wt(A, c.s_v, reduced)
        up(c.s_a, A.activation(wsq[:, :, :], w, ACT.Square))
        wt(V, c.s_a)
        up(c.s_v, V.tensor_reduce(small[:, i % 2, :], wsq[:, :, :], AX.X, ALU.add))
        reduced = c.s_v.n
        wt(A, c.s_v)
        up(c.s_a, A.activation(small[:, i % 2, :], small[:, i % 2, :], ACT.Sqrt, bias=EPS, scale=1.0 / A_QK))
        wt(V, c.s_a)
        V.reciprocal(small[:, i % 2, :], small[:, i % 2, :])
        V.drain()
        V.tensor_tensor(w, w, small[:, i % 2, :].unsqueeze(2).broadcast_to([P, A_HEADS, A_QK]), ALU.mult)
        V.drain()
        ins = V.tensor_tensor(w, w, gain.unsqueeze(1).broadcast_to([P, A_HEADS, A_QK]), ALU.mult)
        if t < TT:
            V.drain()
            for a in range(2):
                for q in range(2):
                    dst = slice(16 * a + 8 * q, 16 * a + 8 * q + 8)
                    src = slice(A_NOPE + 16 * a + 8 * (1 - q), A_NOPE + 16 * a + 8 * (1 - q) + 8)
                    V.tensor_tensor(rtmp[:, :, dst], w[:, :, src],
                                    rope[:, 1, t, dst].unsqueeze(1).broadcast_to([P, A_HEADS, 8]), ALU.mult)
            V.drain()
            wr = w[:, :, A_NOPE:A_QK]
            V.tensor_tensor(wr, wr, rope[:, 0, t, :].unsqueeze(1).broadcast_to([P, A_HEADS, A_ROPE]), ALU.mult)
            V.drain()
            ins = V.tensor_tensor(wr, wr, rtmp[:, :, :], ALU.add)
        up(c.s_v, ins)
        wt(T, c.s_v)
        if i:
            wt(T, c.s_a, copied)
        for hd in range(A_HEADS):
            ins = T.transpose(ps[0:A_QK, 4 + hd // 4, (hd % 4) * P:(hd % 4 + 1) * P], w[:, hd, :], c.ident[:, :])
        up(c.s_t, ins)
        turned.append(c.s_t.n)
        wt(A, c.s_t)
        dst = (kT if what == "k" else qT)[:, :, ts]
        up(c.s_a, A.activation(dst, c.flat(4, 0, 1024)[0:A_QK].rearrange("p (h n) -> p h n", h=A_HEADS), ACT.Copy))
        copied = c.s_a.n
    wt(T, c.s_a)
    wt(V, c.s_a)
    wt(A, c.s_v)
    wt(V, c.s_t)
    wt(A, c.s_t)
    c.close(stage2)
    joint_attention(c, l, 0, TT, ALLT, 0, kT, qT, vS, ag, m_hi, m_lo, spare)
    if both:
        joint_attention(c, l, TT, NT - TT, CTX, SEQ, kT, qT, vS, ag, m_hi, m_lo, spare)
    c.close(tok)

    x0 = c.s_x.n
    with T.Fori(0, KT // RING, 1) as i:
        for u in range(RING):
            b = Blk(n + u, i, RING)
            c.use(b)
            wt(T, c.s_x, i * RING + (x0 + u - 1))
            wh = c.w_hi[:, b.slot, :].rearrange("p (k m) -> p k m", k=KT)
            wl = c.w_lo[:, b.slot, :].rearrange("p (k m) -> p k m", k=KT)
            for lo, nn in pieces:
                for k in range(KT):
                    ins = c.mm3(c.flat((0, 2)[u % 2], lo, nn), wh[:, k, :], wl[:, k, :],
                                m_hi[:, k, lo:lo + nn], m_lo[:, k, lo:lo + nn], k == 0, k == KT - 1)
            c.used(ins)
    for u in range(KT):
        c.split_hi(Blk(n + u))
        V.wait_ge(c.s_used.h, n + u + 1 + PRIME)
        bank = (0, 2)[u % 2]
        if both:
            V.scalar_tensor_tensor(c.y[:, u, :], ps[:, bank + 1, 0:CTX], modv[:, l, 2 * KT + u, 1:2], c.y[:, u, :],
                                   ALU.mult, ALU.add)
        c.s_x.up(V.scalar_tensor_tensor(c.x[:, u, :], ps[:, bank, :], modv[:, l, 2 * KT + u, 0:1], c.x[:, u, :],
                                        ALU.mult, ALU.add))
    wt(A, c.s_x)
    wt(T, c.s_x)
    c.close(outer)
    return n + KT


def joint_attention(c, l, t0, nqb, nk, k0, kT, qT, vS, ag, m_hi, m_lo, spare):
    nc, T, V, A = c.nc, c.T, c.V, c.A
    L = f"j{l}{t0}_"
    sc = c.scope()
    KTL = nk // P
    mk = lambda nme, e: Sem(nc, L + nme, e)
    s_q, s_exp, s_hi = (mk(x, A) for x in ("q", "exp", "hi"))
    s_mx, s_pt, s_on, s_g, s_lo = (mk(x, V) for x in ("mx", "pt", "on", "g", "lo"))
    s_qk, s_tr, s_pv, s_ot = (mk(x, T) for x in ("qk", "tr", "pv", "ot"))
    qc = [c.ctx(L + f"qc{i}", [A_QK, A_HEADS, P]) for i in range(1)]
    prob = [nc.alloc_sbuf_tensor_at(L + f"prob{i}", [P, nk], F32, offset=spare + i * ALLT * 4) for i in range(2)]
    probT = [nc.alloc_sbuf_tensor_at(L + "probT0", [P, nk], F32, offset=spare + 2 * ALLT * 4)[:, :], c.sq[:, 0, 0:nk]]
    nm = c.ctx(L + "nm", [P, A_HEADS])
    den = c.ctx(L + "den", [P, A_HEADS])
    rden = c.ctx(L + "rden", [P, A_HEADS])
    osb = c.ctx(L + "osb", [P, 512])
    gt = c.sq[:, 1, 0:512].rearrange("p (f n) -> p f n", f=4)
    cut = [(0, min(nk, 512))] + ([(512, nk - 512)] if nk > 512 else [])
    sbank, tbank, o_bank, ot_bank = (0, 2), 4, 6, 7

    with T.Fori(0, nqb, 1) as i:
        u = lambda s: i * 8 + (s + 1 + PRIME)

        def pv(s):
            wt(T, s_pt, u(s))
            if s == 0:
                wt(T, s_on, i + PRIME)
            for k in range(KTL):
                ins = T.matmul(c.ps[:, o_bank, s * A_V:(s + 1) * A_V], probT[s % 2][:, k * P:(k + 1) * P],
                               vS[:, k0 // P + k, s * A_V:(s + 1) * A_V], start=k == 0, stop=k == KTL - 1)
            ins.then_inc(s_pv.h, 1)

        def tr(s):
            wt(T, s_exp, u(s))
            wt(T, s_pt, u(s - 1))
            for k in range(KTL):
                ins = T.transpose(c.flat(tbank, k * P, P), prob[s % 2][:, k * P:(k + 1) * P], c.ident[:, :])
            ins.then_inc(s_tr.h, 1)

        for s in range(8):
            if s == 0:
                wt(T, s_q, i + (1 + PRIME))
            wt(T, s_exp, u(s - 2))
            for lo, nn in cut:
                ins = T.matmul(c.flat(sbank[s % 2], lo, nn), qc[0][:, s, :], kT[:, s, k0 + lo:k0 + lo + nn],
                               start=True, stop=True)
            ins.then_inc(s_qk.h, 1)
            if s >= 1:
                tr(s - 1)
            if s >= 2:
                pv(s - 2)
        tr(7)
        pv(6)
        pv(7)
        wt(T, s_on, i + (1 + PRIME))
        wt(T, s_g, i + PRIME)
        for b in range(4):
            ins = T.transpose(c.ps[:, ot_bank, b * P:(b + 1) * P], osb[:, b * P:(b + 1) * P], c.ident[:, :])
        ins.then_inc(s_ot.h, 1)

    with V.Fori(0, nqb, 1) as i:
        u = lambda s: i * 8 + (s + 1 + PRIME)

        def ptc(s):
            wt(V, s_tr, u(s))
            wt(V, s_pv, u(s - 2))
            V.tensor_copy(probT[s % 2][:, 0:nk], c.flat(tbank, 0, nk)).then_inc(s_pt.h, 1)
        for s in range(8):
            wt(V, s_qk, u(s))
            V.tensor_reduce(nm[:, s:s + 1], c.flat(sbank[s % 2], 0, nk), AX.X, ALU.max, negate=True).then_inc(s_mx.h, 1)
            if s >= 1:
                ptc(s - 1)
        ptc(7)
        wt(V, s_exp, u(7))
        V.reciprocal(rden[:, :], den[:, :])
        V.drain()
        wt(V, s_pv, u(7))
        wt(V, s_ot, i + PRIME)
        V.tensor_tensor(osb[:, :].rearrange("p (h d) -> p h d", h=A_HEADS),
                        c.ps[:, o_bank, :].rearrange("p (h d) -> p h d", h=A_HEADS),
                        rden[:, :].unsqueeze(2).broadcast_to([P, A_HEADS, A_V]), ALU.mult).then_inc(s_on.h, 1)
        wt(V, s_ot, i + (1 + PRIME))
        wt(V, s_lo, i + PRIME)
        cols = bass.ds(i * P + t0 * P, P)
        V.tensor_tensor(gt, c.ps[:, ot_bank, :].rearrange("p (f n) -> p f n", f=4), ag[:, :, cols],
                        ALU.mult).then_inc(s_g.h, 1)
        wt(V, s_hi, i + (1 + PRIME))
        V.tensor_tensor(m_lo[:, 4:8, cols], gt, m_hi[:, 4:8, cols].bitcast(F32),
                        ALU.subtract).then_inc(s_lo.h, 1)

    with A.Fori(0, nqb, 1) as i:
        u = lambda s: i * 8 + (s + 1 + PRIME)
        cols = bass.ds(i * P + t0 * P, P)
        wt(A, s_qk, u(-1))
        c.absorb(A)
        A.activation(qc[0][:, :, :], qT[:, :, cols], ACT.Copy).then_inc(s_q.h, 1)
        for s in range(8):
            wt(A, s_mx, u(s))
            wt(A, s_tr, u(s - 2))
            A.activation(prob[s % 2][:, :], c.flat(sbank[s % 2], 0, nk), ACT.Exp, bias=nm[:, s:s + 1],
                         accum_out=den[:, s:s + 1]).then_inc(s_exp.h, 1)
        wt(A, s_g, i + (1 + PRIME))
        c.absorb(A)
        A.activation(m_hi[:, 4:8, cols], gt, ACT.Copy).then_inc(s_hi.h, 1)
    for s in (s_exp, s_mx, s_pt, s_qk, s_tr, s_pv):
        s.n = PRIME + 8 * nqb
    for s in (s_q, s_hi, s_on, s_g, s_lo, s_ot):
        s.n = PRIME + nqb
    for e in (T, A):
        wt(e, s_lo)
    wt(V, s_pv)
    wt(V, s_hi)
    wt(A, s_pv)
    c.close(sc)


def build(nc, io, V_):
    c = Core(nc, io)
    T, V, A, G, S = c.T, c.V, c.A, c.G, c.S

    c.top = (nc.sbuf_base + 31) // 32 * 32
    c.offset = c.top

    def ctx(name, shape, dt=F32):
        size = int(np.prod(shape[1:])) * 4
        t = nc.alloc_sbuf_tensor_at(name, shape, dt, offset=c.offset)
        c.offset += (size + 31) // 32 * 32
        return t

    c.ctx = ctx
    c.scope = lambda: c.offset

    def close(mark):
        c.offset = mark
    c.close = close

    S.dma_start(c.vec[:, :], io["vec"]).then_inc(c.d_const, 16)
    S.dma_start(c.ident[:, :], io["ident"]).then_inc(c.d_const, 16)
    S.dma_start(c.slope[:, :], io["slope"]).then_inc(c.d_const, 16)
    d_x = [nc.alloc_semaphore(f"d_x{i}") for i in range(4)]
    for i in range(4):
        S.dma_start(c.x[:, 2 * i:2 * i + 2, :], io["x"][:, 2 * i:2 * i + 2, :]).then_inc(d_x[i], 16)
    V.memset(c.ones[:, :], 1.0).then_inc(c.s_v.h, 1)
    c.s_v.n += 1
    wt(T, c.s_v)
    for e in (T, V, A):
        e.wait_ge(c.d_const, 48)
    c1 = c.scope()
    cs = c.ctx("cs", [P, KT, 2])
    A.activation(cs[:, :, :], c.vec[:, V_["c"]:V_["c"] + 2 * KT].rearrange("p (k a) -> p k a", a=2), ACT.Silu)
    A.drain()
    c.s_a.up(A.activation(c.c4[:, :, 0:2], cs[:, :, :], ACT.Copy))
    wt(V, c.s_a)
    c.s_v.up(V.tensor_tensor(c.c4[:, :, 2:4], cs[:, :, :], c.c4[:, :, 0:2].bitcast(F32), ALU.subtract))
    wt(T, c.s_v)

    c.stream_loops()
    for b in range(LEAD):
        c.split_hi(Blk(b - LEAD))

    h = (c.ctx("h_hi", [P, KT, SEQ], F32R), c.ctx("h_lo", [P, KT, SEQ], F32R))
    vcol = lambda name, i=0: c.vec[:, V_[name] + i * KT:V_[name] + (i + 1) * KT]
    body = c.scope()

    c.norm_begin()
    c.s_hh_base = c.s_hh.n
    for k in range(KT):
        norm_tile(c, h, k, vcol("norm_mix", 0), natural, 16, d_x[k // 2])
        norm_tile_lo(c, h, k, vcol("norm_mix", 0), natural)
        c.sum_squares(k, KT, 0, 0, TT)
    norm_finish(c)
    n = 0
    ah, al = c.ctx("a_hi", [P, KT * SEQ], F32R), c.ctx("a_lo", [P, KT * SEQ], F32R)
    ready = window_attention(c, n, h, ah, al)
    n += 16
    contract_out(c, n, KT, (ah, al), natural, (h, vcol("norm_ffn", 0), natural), ready)
    norm_finish(c)
    n += KT
    c.close(body)

    def ffn(n, name, mod, nxt):
        mh, ml = c.ctx(name + "m_hi", [P, FT * SEQ], F32R), c.ctx(name + "m_lo", [P, FT * SEQ], F32R)
        ready = swiglu(c, n, name, h, mh, ml, mod)
        n += 2 * FT + (20 if mod else 0)
        contract_out(c, n, FT, (mh, ml), natural, nxt, ready)
        c.close(body)
        return n + FT

    n = ffn(n, "f0", False, (h, vcol("norm_mix", 1), residues))
    norm_finish(c)
    ah, al = c.ctx("b_hi", [P, KT * SEQ], F32R), c.ctx("b_lo", [P, KT * SEQ], F32R)
    ready = dilated_attention(c, n, h, ah, al)
    n += 96
    contract_out(c, n, KT, (ah, al), residues, (h, vcol("norm_ffn", 1), natural), ready)
    norm_finish(c)
    n += KT
    c.close(body)
    n = ffn(n, "f1", True, (None, None, natural))
    c.close(c1)
    c.rstd(0, TT, D_MODEL)
    c.broadcast_rstd(1, TT)
    for k in range(KT):
        c.s_x.up(V.scalar_tensor_tensor(c.x[:, k, :], c.x[:, k, :], vcol("norm_final")[:, k:k + 1], c.RB[:, 0:SEQ],
                                        ALU.mult, ALU.mult))
    c.y = c.ctx("y", [P, KT, CTX])
    d_y = nc.alloc_semaphore("d_y")
    A.wait_ge(c.s_x.h, c.s_x.n)
    A.dma_start(c.y[:, :, :], io["ctx"]).then_inc(d_y, 16)
    A.wait_ge(d_y, 16)
    V.wait_ge(d_y, 16)
    for l in range(2):
        n = block_two_layer(c, l, n, V_)
    assert n == len(PLAN), (n, len(PLAN))
    d_out = nc.alloc_semaphore("d_out")
    S.wait_ge(c.s_x.h, c.s_x.n)
    S.dma_start(io["out"], c.x[:, :, :]).then_inc(d_out, 16)
    S.wait_ge(d_out, 16)



def shape_constants():
    j = np.arange(P)
    k = np.arange(3 * P)
    rel = np.abs(k[None, :] - WIN - j[:, None]).astype(np.float64)
    dist0 = np.where(rel <= WIN, -rel, -BIG)
    t = 4 * j[:, None]
    keys = np.concatenate([DIL * np.arange(P) + r for r in range(DIL)])
    cols = []
    dj = np.abs(j[:, None] - j[None, :])
    own2 = np.where(dj <= 64, -4.0 * dj, -BIG)
    own3 = np.where(dj % 4 == 0, -4.0 * dj, -BIG)
    for r in range(DIL):
        d = np.abs(t + r - keys[None, :]).astype(np.float64)
        cols += [np.where(d <= 64, -d, -BIG), own2, own3]
    dist1 = np.concatenate(cols, axis=1)
    slope = lambda hd: 2.0 ** (-8.0 * (hd + 1) / 16) * 8.0
    row = [slope(4 * (2 * (tt // 4) + e) + tt % 4) for tt in range(8) for e in range(2)] + [slope(hd) for hd in range(16)]
    slopes = np.tile(np.array(row)[None, :], (P, 1))

    def dft(n, scale):
        a = np.arange(n)
        ang = 2 * np.pi * ((a[:, None] * a[None, :]) % n) / n
        m = np.stack([np.cos(ang), np.sin(ang)]) * scale
        return m.reshape(2, n // P, P, n).transpose(2, 0, 1, 3)
    a = np.arange(64)
    ang = 2 * np.pi * ((a[:, None] * a[None, :]) % 64) / 64
    bd = np.zeros((2, P, P))
    for g in range(2):
        s = slice(64 * g, 64 * g + 64)
        bd[0, s, s] = np.cos(ang) / 8.0
        bd[1, s, s] = -np.sin(ang) / 8.0
    half = A_ROPE // 2
    tok = np.arange(SEQ)
    inv = (10000.0 ** (-np.arange(0, half, 2, dtype=np.float32) / half)).astype(np.float32)
    ar = (tok // 64).astype(np.float32)[:, None] * inv[None, :]
    ac = (tok % 64).astype(np.float32)[:, None] * inv[None, :]
    angs = np.concatenate([ar, ar, ac, ac], -1).astype(np.float32)
    sign = np.repeat(np.array([-1.0, 1.0, -1.0, 1.0]), 8)
    rope = np.stack([np.cos(angs), np.sin(angs) * sign[None, :]])
    rope = rope.reshape(2, TT, P, A_ROPE).transpose(2, 0, 1, 3).reshape(P, -1)
    out = {"dist0": dist0, "dist1": dist1, "slope": slopes, "ident": np.eye(P), "dft": dft(SEQ, SEQ ** -0.5),
           "dfc": dft(CTX, CTX ** -0.5), "dfd": bd.transpose(1, 0, 2).reshape(P, -1), "rope": rope}
    return {n: np.ascontiguousarray(v, dtype=np.float32) for n, v in out.items()}


def lay_out(x):
    g = {n: np.asarray(v) for n, v in x.items()}
    colblk = lambda w, t: w[:, t * P:(t + 1) * P].reshape(KT, P, P).transpose(1, 0, 2).reshape(P, 1024)
    hcols = lambda hd: np.arange(hd * HD, (hd + 1) * HD)
    pair = lambda tt: (4 * (2 * (tt // 4)) + tt % 4, 4 * (2 * (tt // 4) + 1) + tt % 4)
    qa = np.concatenate([hcols(hd) for tt in range(8) for hd in pair(tt)])
    wa = g["w_qkv_a"][0]
    waq, wak, wav = wa[:, :1024][:, qa], wa[:, 1024:1280], wa[:, 1280:1536]
    woa = g["w_out_a"][0][qa, :]
    wb = g["w_qkv_b"][0].reshape(D_MODEL, 3, 3, 1024)
    win = g["w_in_2"]
    o = dict(f=0, fg=256, gu=512, gv=768, gg=1024, cq=1280, ckv=1536, kr=1664, ag=1696)
    tokcols = np.concatenate([np.arange(256), np.arange(o["gv"], o["gv"] + 256)])
    feat = np.concatenate([np.arange(o[nme], o[nme] + w) for nme, w in
                           (("cq", 256), ("ckv", 128), ("gg", 256), ("gu", 256), ("fg", 256), ("ag", 512))])
    blocks = []
    for kind, *w in PLAN:
        if kind == "ak":
            b = colblk(wak, w[0])
        elif kind == "av":
            b = colblk(wav, w[0])
        elif kind == "aq":
            b = colblk(waq, w[0])
        elif kind == "mod":
            b = colblk(g["w_mod_2"][w[0]], w[1])
        elif kind == "oa":
            b = woa[w[0] * P:(w[0] + 1) * P]
        elif kind == "ob":
            b = g["w_out_b"][0][w[0] * P:(w[0] + 1) * P]
        elif kind == "gate":
            b = colblk(g["w_gate"][w[0]], w[1])
        elif kind == "up":
            b = colblk(g["w_up"][w[0]], w[1])
        elif kind == "down":
            b = g["w_down"][w[0]][w[1] * P:(w[1] + 1) * P]
        elif kind in ("bq", "bk", "bv"):
            b = colblk(wb[:, w[0], "qkv".index(kind[1])], w[1])
        elif kind == "kr":
            b = np.zeros((P, 1024), np.float32)
            b[:, :KT * A_ROPE] = win[w[0]][:, o["kr"]:o["kr"] + 32].reshape(KT, P, 32).transpose(1, 0, 2).reshape(P, -1)
        elif kind == "tok":
            b = win[w[0]][:, tokcols][w[1] * 256:(w[1] + 1) * 256].reshape(2, P, 512).transpose(1, 0, 2).reshape(P, 1024)
        elif kind == "feat":
            b = colblk(win[w[0]][:, feat], w[1])
        elif kind == "out":
            b = colblk(g["w_out_2"][w[0]], w[1])
        blocks.append(b)
    arr = {"wstream": np.stack(blocks)}
    ft = lambda a: a.reshape(-1, P).T
    vec, V_ = [], {}

    def add(name, a):
        V_[name] = sum(v.shape[1] for v in vec)
        vec.append(a)
    add("norm_mix", ft(g["norm_mix"]))
    add("norm_ffn", ft(g["norm_ffn"]))
    add("norm_final", ft(g["norm_final"]))
    add("norm_g", ft(g["norm_g_2"]))
    add("b_mod", ft(g["b_mod_2"]))
    add("q_a_g", ft(g["q_a_g_2"]))
    add("kv_a_g", ft(g["kv_a_g_2"]))
    add("c", np.stack([ft(g["c_2"][0]), ft(g["c_ctx_2"])], axis=2).reshape(P, 2 * KT))
    arr["vec"] = np.concatenate(vec, axis=1)
    arr["x"] = g["x"][0].T.reshape(KT, P, SEQ).transpose(1, 0, 2)
    arr["ctx"] = g["ctx_2"][0].T.reshape(KT, P, CTX).transpose(1, 0, 2)
    arr["sinks"] = np.broadcast_to(np.concatenate(
        [np.tile(g["sink_a"][0][list(pair(tt))], 4) for tt in range(8)])[None, :], (P, 64))
    arr["wfmix"] = g["w_fmix_2"].reshape(2, 2, P, 256).transpose(0, 2, 1, 3).reshape(2, P, 512)
    arr["gws"] = g["g_ws_2"].transpose(0, 3, 1, 2).reshape(2, P, 512)
    arr["gbs"] = np.repeat(g["g_bs_2"].reshape(2, 2, 2, 1, P), HD, axis=3).reshape(2, 2, P, P).transpose(0, 2, 1, 3).reshape(2, P, 2 * P)
    arr["glg"] = np.broadcast_to(g["g_ln_g_2"][:, None, :], (2, P, HD))
    arr["wuq"] = g["w_uq_2"].reshape(2, 2, P, 768).transpose(0, 2, 1, 3).reshape(2, P, 1536)
    arr["wukv"] = g["w_ukv_2"].reshape(2, P, A_HEADS, 2, 64).transpose(0, 1, 3, 2, 4).reshape(2, P, 1024)
    arr["qkg"] = np.broadcast_to(np.stack([g["q_norm_g_2"], g["k_norm_g_2"]], 1)[:, None], (2, P, 2, A_QK)).reshape(2, P, 2 * A_QK)
    arr = {n: np.ascontiguousarray(v) for n, v in arr.items()}
    arr.update(shape_constants())
    return arr, V_


def kernel(**inputs):
    from concourse import bacc
    from concourse.bass_utils import run_bass_kernel_spmd
    arr, V_ = lay_out(inputs)
    nc = bacc.Bacc("TRN2", target_bir_lowering=False, num_devices=1)
    io = {n: nc.dram_tensor("in_" + n, a.shape, F32, kind="ExternalInput").ap() for n, a in arr.items()}
    io["out"] = nc.dram_tensor("out", (P, KT, SEQ), F32, kind="ExternalOutput").ap()
    build(nc, io, V_)
    r = run_bass_kernel_spmd(nc, [{"in_" + n: a for n, a in arr.items()}], core_ids=[0])
    o = r.results[0]["out"]
    return np.ascontiguousarray(o.transpose(1, 0, 2).reshape(D_MODEL, SEQ).T)[None]
```

```python
import numpy as np
from concourse import bass, mybir
from concourse.alu_op_type import AluOpType as ALU

F32 = mybir.dt.float32
F32R = mybir.dt.float32r
ACT = mybir.ActivationFunctionType
AX = mybir.AxisListType

P = 128
D_MODEL = 1024
KT = D_MODEL // P
SEQ = 512
TT = SEQ // P
CTX = 256
ALLT = SEQ + CTX
NT = ALLT // P
EPS = 1e-6
HD = 64
D_FF = 2816
FT = D_FF // P
WIN = 128
DIL = 4
MT = 3 * KT
A_HEADS, A_NOPE, A_ROPE, A_V = 8, 64, 32, 64
A_QK = A_NOPE + A_ROPE
BIG = 1e32
RING = 4
LEAD = 3
PRIME = 8


def stream_plan():
    s = []
    mod = [(0, t) for t in range(MT)]
    mod1 = [(1, t) for t in range(MT)]
    for m in range(2):
        s += [("ak", m), ("av", m)] + [("aq", 4 * m + i) for i in range(4)]
        s += [("mod", *mod1.pop(0)) for _ in range(2)]
    s += [("oa", t) for t in range(KT)]
    for j in range(FT):
        s += [("gate", 0, j), ("up", 0, j)]
    s += [("down", 0, j) for j in range(FT)]
    for p in range(8):
        for g in range(3):
            s += [("bq", g, p), ("bk", g, p), ("bv", g, p), ("mod", *mod.pop(0))]
    s += [("ob", t) for t in range(KT)]
    for j in range(FT):
        s += [("gate", 1, j), ("up", 1, j)]
        if mod1:
            s += [("mod", *mod1.pop(0))]
    s += [("down", 1, j) for j in range(FT)]
    for l in range(2):
        s += [("tok", l, b) for b in range(4)] + [("kr", l)]
        s += [("feat", l, t) for t in range(13)]
        s += [("out", l, t) for t in range(KT)]
    assert not mod and not mod1
    return s


PLAN = stream_plan()


class Blk:

    def __init__(self, const, i=0, per=0):
        assert per % RING == 0
        self.c, self.i, self.per = const, i, per
        self.slot = const % RING
        self.n = const + i * per if per else const
        self.round = const // RING + i * (per // RING) if per else const // RING

    def plus(self, k):
        return Blk(self.c + k, self.i, self.per)


class Sem:

    def __init__(self, nc, name, eng):
        self.h = nc.alloc_semaphore(name)
        eng.nop().then_inc(self.h, PRIME)
        self.n = PRIME

    def up(self, ins):
        ins.then_inc(self.h, 1)
        self.n += 1
        return self.n


def wt(eng, sem, value=None):
    eng.wait_ge(sem.h, sem.n if value is None else value)


class Core:

    def __init__(self, nc, io):
        self.nc, self.io = nc, io
        self.T, self.V, self.A, self.G, self.S = nc.tensor, nc.vector, nc.scalar, nc.gpsimd, nc.sync
        self.dummy = {}
        for name, eng in (("t", self.T), ("v", self.V), ("a", self.A), ("g", self.G)):
            self.dummy[id(eng)] = nc.alloc_semaphore("own_" + name)
        sb = self.sb
        self.ps = nc.alloc_psum_tensor("ps", [P, 8, 512], F32)
        off = (nc.sbuf_base + 31) // 32 * 32
        self.w_lo = nc.alloc_sbuf_tensor("w_lo", [P, RING, 1024], F32R)
        self.w_raw = nc.alloc_sbuf_tensor_at("w_raw", [P, RING, 1024], F32, offset=off)
        self.w_hi = sb("w_hi", [P, RING, 1024], F32R)
        self.x = sb("x", [P, KT, SEQ])
        self.y = sb("y", [P, KT, CTX])
        self.ident = sb("ident", [P, P])
        self.ones = sb("ones", [P, P])
        self.vec = sb("vec", [P, io["vec"].shape[1]])
        self.slope = sb("slope", [P, 32])
        self.c4 = sb("c4", [P, KT, 4], F32R)
        self.modraw = [sb(f"modraw{l}", [P, MT * 4]) for l in range(2)]
        self.modv = sb("modv", [P, 2, MT, 2])
        self.r_tok = sb("r_tok", [P, 3, NT])
        self.RB = sb("RB", [P, ALLT])
        self.sq = sb("sq", [P, 2, ALLT])
        self.d_raw = [nc.alloc_semaphore(f"d_raw{i}") for i in range(RING)]
        self.s_hi = Sem(nc, "s_hi", self.A)
        self.s_lo = Sem(nc, "s_lo", self.G)
        self.s_used = Sem(nc, "s_used", self.T)
        mk = lambda n, e: Sem(nc, n, e)
        self.s_x = mk("s_x", self.V)
        self.s_sq = mk("s_sq", self.A)
        self.s_ssq = mk("s_ssq", self.T)
        self.s_std = mk("s_std", self.A)
        self.s_rstd = mk("s_rstd", self.V)
        self.s_hh = mk("s_hh", self.A)
        self.s_hl = mk("s_hl", self.V)
        self.s_acc = mk("s_acc", self.T)
        self.s_v = mk("s_v", self.V)
        self.s_a = mk("s_a", self.A)
        self.s_t = mk("s_t", self.T)
        self.d_const = nc.alloc_semaphore("d_const")
        self.nsplit = 0

    def sb(self, name, shape, dt=F32):
        return self.nc.alloc_sbuf_tensor(name, shape, dt)

    def absorb(self, eng):
        eng.sem_inc(self.dummy[id(eng)])

    def stream_loops(self):
        nb = len(PLAN)
        w = self.io["wstream"]

        def load(b):
            self.S.wait_ge(self.s_used.h, b.n + 1 + PRIME - RING)
            self.S.dma_start(self.w_raw[:, b.slot, :], w[b.n] if isinstance(b.n, int) else
                             w[bass.ds(b.n, 1)].rearrange("a p n -> (a p) n")).then_inc(self.d_raw[b.slot], 16)

        def split_lo(b):
            self.G.wait_ge(self.s_hi.h, b.n + 1 + PRIME)
            self.G.tensor_tensor(self.w_lo[:, b.slot, :], self.w_raw[:, b.slot, :],
                                 self.w_hi[:, b.slot, :].bitcast(F32), ALU.subtract).then_inc(self.s_lo.h, 1)

        for eng, f in ((self.S, load), (self.G, split_lo)):
            with eng.Fori(0, nb // RING, 1) as i:
                for u in range(RING):
                    f(Blk(u, i, RING))
            for n in range(nb // RING * RING, nb):
                f(Blk(n))

    def split_hi(self, b):
        b = b.plus(LEAD)
        if b.per == 0 and b.c >= len(PLAN):
            return
        self.A.wait_ge(self.d_raw[b.slot], (b.round + 1) * 16)
        self.A.activation(self.w_hi[:, b.slot, :], self.w_raw[:, b.slot, :], ACT.Copy).then_inc(self.s_hi.h, 1)

    def use(self, b):
        self.T.wait_ge(self.s_lo.h, b.n + 1 + PRIME)

    def used(self, ins):
        ins.then_inc(self.s_used.h, 1)

    def mm3(self, out, wh, wl, ah, al, start, stop, w_is_lhs=True):
        T = self.T
        if w_is_lhs:
            T.matmul(out, wh, ah, start=start, stop=False)
            T.matmul(out, wh, al, start=False, stop=False)
            return T.matmul(out, wl, ah, start=False, stop=stop)
        T.matmul(out, ah, wh, start=start, stop=False)
        T.matmul(out, ah, wl, start=False, stop=False)
        return T.matmul(out, al, wh, start=False, stop=stop)

    def feat_chunk(self, b, out, h, ks, last=KT - 1):
        wh = self.w_hi[:, b.slot, :].rearrange("p (k m) -> p k m", k=KT)
        wl = self.w_lo[:, b.slot, :].rearrange("p (k m) -> p k m", k=KT)
        for k in ks:
            ins = self.mm3(out, wh[:, k, :], wl[:, k, :], h[0][:, k, :], h[1][:, k, :], k == 0, k == last)
        return ins

    def mod_chunk(self, b, out, ks):
        wh = self.w_hi[:, b.slot, :].rearrange("p (k m) -> p k m", k=KT)
        wl = self.w_lo[:, b.slot, :].rearrange("p (k m) -> p k m", k=KT)
        for k in ks:
            self.T.matmul(out[:, 0:4], wh[:, k, :], self.c4[:, k, :], start=k == 0, stop=False)
            ins = self.T.matmul(out[:, 0:2], wl[:, k, :], self.c4[:, k, 0:2], start=False, stop=k == KT - 1)
        return ins

    def sum_squares(self, n, ntiles, cols, bank, tiles):
        wt(self.T, self.s_sq, self.s_sq_base + n + 1)
        for t in range(tiles):
            ins = self.T.matmul(self.ps[:, bank, cols + t:cols + t + 1], self.sq[:, n % 2, t * P:(t + 1) * P],
                                self.ones[:, 0:1], start=(n == 0 and t == 0),
                                stop=(n == ntiles - 1 and t == tiles - 1), skip_group_check=True)
        self.s_ssq.up(ins)

    def norm_begin(self):
        self.s_ssq_base, self.s_sq_base = self.s_ssq.n, self.s_sq.n

    def rstd(self, bank, tiles, width, row=0):
        A, V = self.A, self.V
        wt(A, self.s_ssq)
        self.s_std.up(A.activation(self.r_tok[:, row, 0:tiles], self.ps[:, bank, 0:tiles], ACT.Sqrt,
                                   bias=EPS, scale=1.0 / width))
        wt(V, self.s_std)
        V.reciprocal(self.r_tok[:, row, 0:tiles], self.r_tok[:, row, 0:tiles]).then_inc(self.s_rstd.h, 1)
        self.s_rstd.n += 1
        V.drain()

    def sum_rows(self, n, ntiles, groups):
        wt(self.T, self.s_sq, self.s_sq_base + n + 1)
        for bank, src in groups:
            ins = self.T.matmul(self.flat(bank, 0, src.shape[-1]), self.ones[:, :], src, start=n == 0,
                                stop=n == ntiles - 1)
        self.s_ssq.up(ins)

    def rstd_rows(self, bank, n, dst):
        wt(self.A, self.s_ssq)
        self.s_std.up(self.A.activation(dst, self.flat(bank, 0, n), ACT.Sqrt, bias=EPS, scale=1.0 / D_MODEL))
        wt(self.V, self.s_std)
        self.s_rstd.up(self.V.reciprocal(dst, dst))
        self.V.drain()

    def flat(self, bank, start, n):
        return self.ps[:, :, :].rearrange("p b n -> p (b n)")[:, bank * 512 + start:bank * 512 + start + n]



def norm_tile(c, h, k, gain, order, sem_value, sem=None):
    A = c.A
    xin = order(c.x[:, k, :])
    A.wait_ge(sem if sem is not None else c.s_x.h, sem_value)
    c.s_hh.up(A.activation(h[0][:, k, :], xin, ACT.Copy, scale=gain[:, k:k + 1]))
    wt(A, c.s_ssq, c.s_ssq_base + k - 1)
    c.s_sq.up(A.activation(c.sq[:, k % 2, 0:SEQ], xin, ACT.Square))


def norm_tile_lo(c, h, k, gain, order):
    V = c.V
    wt(V, c.s_hh, c.s_hh_base + k + 1)
    c.s_hl.up(V.scalar_tensor_tensor(h[1][:, k, :], order(c.x[:, k, :]), gain[:, k:k + 1],
                                     h[0][:, k, :].bitcast(F32), ALU.mult, ALU.subtract))


def norm_finish(c):
    c.rstd_rows(0, SEQ, c.RB[:, 0:SEQ])
    wt(c.T, c.s_hl)
    wt(c.T, c.s_std)


def square_both(c, k):
    wt(c.A, c.s_ssq, c.s_ssq_base + k - 1)
    c.A.activation(c.sq[:, k % 2, 0:SEQ], c.x[:, k, :], ACT.Square)
    return c.A.activation(c.sq[:, k % 2, SEQ:ALLT], c.y[:, k, :], ACT.Square)


def context_norm(c):
    c.norm_begin()
    for k in range(KT):
        wt(c.A, c.s_ssq, c.s_ssq_base + k - 1)
        c.s_sq.up(c.A.activation(c.sq[:, k % 2, 0:CTX], c.y[:, k, :], ACT.Square))
        c.sum_rows(k, KT, [(2, c.sq[:, k % 2, 0:CTX])])
    c.rstd_rows(2, CTX, c.RB[:, SEQ:ALLT])
    wt(c.T, c.s_std)


def final_norm(c, gain):
    V, A = c.V, c.A
    mark = c.scope()
    RB1 = c.ctx("RB1", [P, SEQ])
    c.rstd_rows(0, SEQ, RB1[:, :])
    r2 = c.RB[:, 0:SEQ]
    V.tensor_tensor(r2, c.ps[:, 1, :], RB1[:, :], ALU.mult)
    V.drain()
    c.s_rstd.up(V.tensor_tensor(r2, r2, RB1[:, :], ALU.mult))
    wt(A, c.s_rstd)
    c.s_std.up(A.activation(r2, r2, ACT.Sqrt, bias=EPS, scale=1.0 / D_MODEL))
    for k in range(KT):
        c.s_x.up(V.scalar_tensor_tensor(c.x[:, k, :], c.x[:, k, :], gain[:, k:k + 1], RB1[:, :], ALU.mult, ALU.mult))
        if k == 1:
            wt(V, c.s_std)
            V.reciprocal(r2, r2)
    V.drain()
    c.close(mark)


def contract_out(c, n0, nb, act, order, nxt, ready):
    T, A, V = c.T, c.A, c.V
    ah, al = act

    def rows(b, m):
        return c.w_hi[:, b.slot, m * P:(m + 1) * P], c.w_lo[:, b.slot, m * P:(m + 1) * P]

    def outer(b, k, start):
        c.use(b)
        cols = bass.ds(k * SEQ, SEQ)
        for m in range(KT):
            wh, wl = rows(b, m)
            ins = c.mm3(c.ps[:, m, :], wh, wl, ah[:, cols], al[:, cols], start, False)
        c.used(ins)

    for e, v in ready:
        e(T, v)
    head = min(4, nb - 2)
    loops = (nb - 2 - head) // RING
    for k in range(head):
        outer(Blk(n0 + k), k, k == 0)
    if loops:
        with T.Fori(0, loops, 1) as i:
            for u in range(RING):
                outer(Blk(n0 + head + u, i, RING), i * RING + (head + u), False)
    for k in range(head + loops * RING, nb - 2):
        outer(Blk(n0 + k), k, False)
    for k in range(head):
        c.split_hi(Blk(n0 + k))
    if loops:
        with A.Fori(0, loops, 1) as i:
            for u in range(RING):
                c.split_hi(Blk(n0 + head + u, i, RING))
    for k in range(head + loops * RING, nb - 2):
        c.split_hi(Blk(n0 + k))
    b0, b1 = Blk(n0 + nb - 2), Blk(n0 + nb - 1)
    h, gain, norder = nxt
    sqg = None if h is not None else c.ctx("sqg", [P, 2, SEQ])

    def sums(m):
        return [(0, c.sq[:, m % 2, 0:SEQ])] + ([(1, sqg[:, m % 2, :])] if h is None else [])
    c.norm_begin()
    c.s_hh_base = c.s_hh.n
    x_base, acc_base = c.s_x.n, c.s_acc.n
    c.use(b0)
    c.use(b1)
    for m in range(KT):
        for b, k in ((b0, nb - 2), (b1, nb - 1)):
            wh, wl = rows(b, m)
            cols = slice(k * SEQ, (k + 1) * SEQ)
            ins = c.mm3(c.ps[:, m, :], wh, wl, ah[:, cols], al[:, cols], False, k == nb - 1)
            if m == KT - 1:
                c.used(ins)
        if m < KT - 1:
            c.s_acc.up(ins)
        if m >= 2:
            if m == 2:
                wt(T, c.s_x, x_base + 2)
            c.sum_rows(m - 2, KT, sums(m - 2))
    c.acc_last = c.s_used.h, n0 + nb + PRIME
    c.sum_rows(KT - 2, KT, sums(KT - 2))
    c.sum_rows(KT - 1, KT, sums(KT - 1))
    c.split_hi(b0)
    for m in range(KT):
        if m < KT - 1:
            wt(V, c.s_acc, acc_base + m + 1)
        else:
            V.wait_ge(*c.acc_last)
        c.s_x.up(V.tensor_tensor(order(c.x[:, m, :]), tokens(c.ps[:, m, :], order), order(c.x[:, m, :]), ALU.add))
        if h is not None:
            norm_tile(c, h, m, gain, norder, x_base + m + 1)
            if m >= 1:
                norm_tile_lo(c, h, m - 1, gain, norder)
        else:
            wt(A, c.s_x, x_base + m + 1)
            wt(A, c.s_ssq, c.s_ssq_base + m - 1)
            A.activation(c.sq[:, m % 2, 0:SEQ], c.x[:, m, :], ACT.Square)
            c.s_sq.up(A.activation(sqg[:, m % 2, :], c.x[:, m, :], ACT.Square, scale=gain[:, m:m + 1]))
    if h is not None:
        norm_tile_lo(c, h, KT - 1, gain, norder)
    c.split_hi(b1)
    c.s_used.n = n0 + nb + PRIME


def natural(ap):
    return ap


def residues(ap):
    return ap.rearrange("p (j r) -> p r j", r=DIL)


def tokens(ap, order):
    return ap if order is natural else ap.rearrange("p (r j) -> p r j", r=DIL)


class Attention:

    def __init__(self, c, name, nbuf, s_bank, t_bank, width, sink=None, bias=True):
        nc = c.nc
        self.c, self.nbuf, self.s_bank, self.t_bank, self.width, self.sink = c, nbuf, s_bank, t_bank, width, sink
        self.bias = bias
        mk = lambda n, e: Sem(nc, name + n, e)
        self.qk_, self.t_, self.pv_, self.ot_ = (mk(n, c.T) for n in ("qk", "t", "pv", "ot"))
        self.ttr_, self.sink_, self.on_, self.olo_ = (mk(n, c.V) for n in ("ttr", "sink", "on", "olo"))
        self.exp_, self.pt_, self.e8_, self.ohi_ = (mk(n, c.A) for n in ("exp", "pt", "e8", "ohi"))
        self.prob = [c.ctx(name + f"prob{i}", [P, width]) for i in range(2)]
        self.probT = [c.ctx(name + f"probT{i}", [P, width]) for i in range(2)]
        self.nm = [c.ctx(name + f"nm{i}", [P, 8]) for i in range(2)]
        self.den = [c.ctx(name + f"den{i}", [P, 8]) for i in range(2)]
        self.tmp8 = c.ctx(name + "tmp8", [P, 8])
        self.osb = c.ctx(name + "osb", [P, 512])

    def u(self, tile, s, sem):
        return tile * 8 + (s + 1 + PRIME)

    def qk(self, tile, s, pieces, extra=()):
        T = self.c.T
        for sem, v in extra:
            wt(T, sem, v)
        wt(T, self.ttr_, self.u(tile, s - self.nbuf, 0))
        for cols, q, k in pieces:
            ins = T.matmul(self.c.flat(self.s_bank + (s % self.nbuf), cols[0], cols[1]), q, k, start=True, stop=True)
        ins.then_inc(self.qk_.h, 1)

    def ttr(self, tile, s, par, n, bias):
        c = self.c
        V = c.V
        wt(V, self.qk_, self.u(tile, s, 0))
        wt(V, self.t_, self.u(tile, s - 2, 0))
        c.absorb(V)
        src = c.flat(self.s_bank + (s % self.nbuf), 0, n)
        V.tensor_tensor_reduce(self.prob[s % 2][:, 0:n], src, bias, -(HD ** -0.5), 3e38, ALU.add, ALU.min,
                               self.nm[par][:, s:s + 1]).then_inc(self.ttr_.h, 1)

    def exp(self, tile, s, par, n):
        A = self.c.A
        wt(A, self.ttr_, self.u(tile, s, 0))
        p = self.prob[s % 2][:, 0:n]
        A.activation(p, p, ACT.Exp, bias=self.nm[par][:, s:s + 1], scale=-1.0,
                     accum_out=self.den[par][:, s:s + 1]).then_inc(self.exp_.h, 1)

    def transpose(self, tile, s, n):
        c = self.c
        wt(c.T, self.exp_, self.u(tile, s, 0))
        wt(c.T, self.pt_, self.u(tile, s - self.nbuf, 0))
        for k in range(n // P):
            ins = c.T.transpose(c.flat(self.t_bank + (s % self.nbuf), k * P, P),
                                self.prob[s % 2][:, k * P:(k + 1) * P], c.ident[:, :])
        ins.then_inc(self.t_.h, 1)

    def copy_pt(self, tile, s, n):
        c = self.c
        wt(c.A, self.t_, self.u(tile, s, 0))
        wt(c.A, self.pv_, self.u(tile, s - 2, 0))
        c.A.activation(self.probT[s % 2][:, 0:n], c.flat(self.t_bank + (s % self.nbuf), 0, n),
                       ACT.Copy).then_inc(self.pt_.h, 1)

    def pv(self, tile, s, vs, col):
        c = self.c
        wt(c.T, self.pt_, self.u(tile, s, 0))
        if s == 0:
            wt(c.T, self.on_, tile + PRIME)
        for k, v in enumerate(vs):
            ins = c.T.matmul(c.flat(self.o_bank, col, HD), self.probT[s % 2][:, k * P:(k + 1) * P], v,
                             start=k == 0, stop=k == len(vs) - 1)
        ins.then_inc(self.pv_.h, 1)

    def norm_out(self, tile, par, perm):
        c = self.c
        V = c.V
        wt(V, self.exp_, self.u(tile, 7, 0))
        c.absorb(V)
        if self.sink is not None:
            V.tensor_tensor(self.tmp8[:, :], self.nm[par][:, :], self.sink(tile), ALU.add).then_inc(self.sink_.h, 1)
            wt(V, self.e8_, tile + 1 + PRIME)
            V.tensor_tensor(self.den[par][:, :], self.den[par][:, :], self.tmp8[:, :], ALU.add)
            V.drain()
        V.reciprocal(self.den[par][:, :], self.den[par][:, :])
        V.drain()
        wt(V, self.pv_, self.u(tile, 7, 0))
        wt(V, self.ot_, tile + PRIME)
        V.tensor_tensor(self.osb[:, :].rearrange("p (u d) -> p u d", u=8),
                        c.flat(self.o_bank, 0, 512).rearrange("p (u d) -> p u d", u=8),
                        perm(self.den[par][:, :]), ALU.mult).then_inc(self.on_.h, 1)

    def sink_exp(self, tile):
        c = self.c
        wt(c.A, self.sink_, tile + 1 + PRIME)
        c.A.activation(self.tmp8[:, :], self.tmp8[:, :], ACT.Exp).then_inc(self.e8_.h, 1)

    def turn(self, tile):
        c = self.c
        wt(c.T, self.on_, tile + 1 + PRIME)
        wt(c.T, self.olo_, tile + PRIME)
        for b in range(4):
            ins = c.T.transpose(c.flat(self.ot_bank, b * P, P), self.osb[:, b * P:(b + 1) * P], c.ident[:, :])
        ins.then_inc(self.ot_.h, 1)

    def out_hi(self, tile, dst):
        c = self.c
        wt(c.A, self.ot_, tile + 1 + PRIME)
        c.absorb(c.A)
        c.A.activation(dst[:, bass.ds(tile * 512, 512)], c.flat(self.ot_bank, 0, 512),
                       ACT.Copy).then_inc(self.ohi_.h, 1)

    def out_lo(self, tile, dst, hi):
        c = self.c
        wt(c.V, self.ohi_, tile + 1 + PRIME)
        cols = bass.ds(tile * 512, 512)
        c.V.tensor_tensor(dst[:, cols], c.flat(self.ot_bank, 0, 512), hi[:, cols].bitcast(F32),
                          ALU.subtract).then_inc(self.olo_.h, 1)

    def finish(self, tiles):
        for s in (self.qk_, self.t_, self.pv_, self.ttr_, self.exp_, self.pt_):
            s.n = PRIME + 8 * tiles
        for s in (self.ot_, self.on_, self.olo_, self.ohi_):
            s.n = PRIME + tiles


def turn_values(c, vt, vx, vT, bank, count):
    wt(c.T, vt, count)
    for t in range(TT):
        ins = c.T.transpose(c.ps[:, bank, t * P:(t + 1) * P], vT[:, t * P:(t + 1) * P], c.ident[:, :])
    ins.then_inc(vx.h, 1)


def window_attention(c, n0, h, ah, al):
    nc, T, V, A = c.nc, c.T, c.V, c.A
    dist = c.ctx("dist0", [P, 3 * P])
    bias = [[c.ctx(f"bias0_{i}{e}", [P, 3 * P]) for e in range(2)] for i in range(2)]
    kT = c.ctx("kT", [P, SEQ])
    vS = c.ctx("vS", [P, TT, P])
    qT = [c.ctx(f"qT{i}", [P, SEQ]) for i in range(2)]
    sinks = c.ctx("sinks", [P, 64])
    at = Attention(c, "wa_", 2, 2, 4, 3 * P, sink=lambda tile: sinks[:, bass.ds(tile * 8, 8)])
    at.o_bank, at.ot_bank = 0, 1
    pb = (6, 7)
    ev = Sem(nc, "wa_ev", V)
    em = Sem(nc, "wa_em", A)
    pj = Sem(nc, "wa_pj", T)
    bs = Sem(nc, "wa_bs", A)
    vT = c.ctx("vT", [P, SEQ])
    vt = Sem(nc, "wa_vt", V)
    vx = Sem(nc, "wa_vx", T)
    d_c = nc.alloc_semaphore("d_wa")
    c.A.dma_start(dist[:, :], c.io["dist0"]).then_inc(d_c, 16)
    c.A.dma_start(sinks[:, :], c.io["sinks"]).then_inc(d_c, 16)
    A.wait_ge(d_c, 32)
    V.wait_ge(d_c, 32)

    def keys(b):
        lo, hi = max(b - 1, 0), min(b + 1, TT - 1)
        return lo, hi - lo + 1

    def unit(s):
        b, e = s // 2, s % 2
        lo, nk = keys(b)
        return b, e, lo, nk, nk * P

    def chunk(b, m, cpos, ks):
        if ks[0] == 0:
            c.use(b)
            if cpos < 2:
                wt(T, em, m * 2 + (PRIME - 1 + cpos))
            elif cpos < 8:
                wt(T, ev, m * 6 + (PRIME + cpos - 1))
        bank = pb[cpos % 2]
        if cpos >= 6:
            ins = c.mod_chunk(b, c.ps[:, bank, :], ks)
        else:
            ins = c.feat_chunk(b, c.ps[:, bank, :], h, ks)
        if ks[-1] == KT - 1:
            c.used(ins)

    def blocks(m):
        return [Blk(n0 + u, m, 8) for u in range(8)]

    with T.Fori(0, 2, 1) as m:
        bl = blocks(m)
        for cpos in range(3):
            chunk(bl[cpos], m, cpos, range(KT))
        turn_values(c, vt, vx, vT, pb[1], m + (1 + PRIME))
        for i in range(4):
            tile = m * 4 + i
            for s in range(8):
                if i < 3:
                    chunk(bl[3 + i], m, 3 + i, [s])
                else:
                    chunk(bl[6 + s // 4], m, 6 + s // 4, [2 * (s % 4), 2 * (s % 4) + 1])
                b, e, lo, nk, n = unit(s)
                rows = slice(HD * e, HD * e + HD)
                at.qk(tile, s, [((0, n), qT[i % 2][rows, b * P:(b + 1) * P], kT[rows, lo * P:lo * P + n])],
                      extra=[(ev, m * 6 + (PRIME + 3 + i))] if s == 0 else ())
                if s >= 1:
                    at.transpose(tile, s - 1, unit(s - 1)[4])
                if s >= 2:
                    b2, e2, lo2, nk2, _ = unit(s - 2)
                    at.pv(tile, s - 2, [vS[:, lo2 + k, HD * e2:HD * e2 + HD] for k in range(nk2)], (s - 2) * HD)
                if s == 3 and i > 0:
                    at.turn(m * 4 + (i - 1))
            at.transpose(tile, 7, unit(7)[4])
            for s in (6, 7):
                b2, e2, lo2, nk2, _ = unit(s)
                at.pv(tile, s, [vS[:, lo2 + k, HD * e2:HD * e2 + HD] for k in range(nk2)], s * HD)
        at.turn(m * 4 + 3)

    with V.Fori(0, 2, 1) as m:
        def evac(cpos):
            V.wait_ge(c.s_used.h, m * 8 + (n0 + cpos + 1 + PRIME))
            bank = pb[cpos % 2]
            if cpos == 0:
                ins = V.tensor_tensor(kT[:, :], c.ps[:, bank, :], c.RB[:, 0:SEQ], ALU.mult)
            elif cpos == 1:
                V.tensor_tensor(vT[:, :], c.ps[:, bank, :], c.RB[:, 0:SEQ], ALU.mult).then_inc(vt.h, 1)
                wt(V, vx, m + (1 + PRIME))
                ins = V.tensor_copy(vS[:, :, :].rearrange("p t n -> p (t n)"), c.ps[:, bank, :])
            else:
                ins = V.tensor_tensor(qT[cpos % 2][:, :], c.ps[:, bank, :], c.RB[:, 0:SEQ], ALU.mult)
            ins.then_inc(ev.h, 1)
        for cpos in range(3):
            evac(cpos)
        for i in range(4):
            tile = m * 4 + i
            for s in range(8):
                b, e, lo, nk, n = unit(s)
                if s == 0:
                    wt(V, bs, m * 4 + (i + 1 + PRIME))
                off = P * (lo - b + 1)
                at.ttr(tile, s, i % 2, n, bias[i % 2][e][:, off:off + n])
                if s == 6 and i > 0:
                    at.out_lo(m * 4 + (i - 1), al, ah)
            if i < 3:
                evac(3 + i)
            at.norm_out(tile, i % 2, lambda r: r.unsqueeze(2).broadcast_to([P, 8, HD]))
        at.out_lo(m * 4 + 3, al, ah)

    with A.Fori(0, 2, 1) as m:
        bl = blocks(m)

        def make_bias(i):
            wt(A, at.ttr_, at.u(m * 4 + i, -9, 0))
            c.absorb(A)
            for e in range(2):
                ins = A.activation(bias[i % 2][e][:, :], dist[:, :], ACT.Copy,
                                   scale=c.slope[:, bass.ds((m * 4 + i) * 2 + e, 1)])
            ins.then_inc(bs.h, 1)
        for cpos in range(3):
            c.split_hi(bl[cpos])
        make_bias(0)
        for i in range(4):
            tile = m * 4 + i
            if i < 3:
                c.split_hi(bl[3 + i])
                make_bias(i + 1)
            for s in range(8):
                at.exp(tile, s, i % 2, unit(s)[4])
                if s >= 1:
                    at.copy_pt(tile, s - 1, unit(s - 1)[4])
                if s == 5 and i > 0:
                    at.out_hi(m * 4 + (i - 1), ah)
                if i == 3 and s in (3, 7):
                    c.split_hi(bl[6 + s // 4])
            at.copy_pt(tile, 7, unit(7)[4])
            at.sink_exp(tile)
        for q in range(2):
            A.wait_ge(c.s_used.h, m * 8 + (n0 + 6 + q + 1 + PRIME))
            c.absorb(A)
            A.activation(c.modraw[1][:, bass.ds((m * 2 + q) * 4, 4)], c.ps[:, pb[q], 0:4], ACT.Copy).then_inc(em.h, 1)
        at.out_hi(m * 4 + 3, ah)
    at.finish(8)
    ev.n, em.n, bs.n = PRIME + 12, PRIME + 4, PRIME + 8
    return [(lambda e, v: wt(e, v), s) for s in (at.olo_, ev, em)]


def dilated_attention(c, n0, h, ah, al):
    nc, T, V, A = c.nc, c.T, c.V, c.A
    W1 = SEQ
    NK = W1 + 2 * P
    dist = c.ctx("dist1", [P, DIL * NK])
    bias = [c.ctx(f"bias1_{i}", [P, NK]) for i in range(2)]
    qT = [[c.ctx(f"dqT{i}{g}", [P, SEQ]) for g in range(3)] for i in range(2)]
    kT = [[c.ctx(f"dkT{i}{g}", [P, SEQ]) for g in range(3)] for i in range(2)]
    vS = [[c.ctx(f"dvS{i}{g}", [P, DIL, P]) for g in range(3)] for i in range(2)]
    at = Attention(c, "da_", 1, 2, 4, NK)
    at.o_bank, at.ot_bank = 0, 1
    pb = (6, 7)
    vT = c.ctx("dvT", [P, SEQ])
    ev = Sem(nc, "da_ev", V)
    vt = Sem(nc, "da_vt", V)
    vx = Sem(nc, "da_vx", T)
    em = Sem(nc, "da_em", A)
    bs = Sem(nc, "da_bs", A)
    d_c = nc.alloc_semaphore("d_da")
    A.wait_ge(c.s_x.h, c.s_x.n)
    c.A.dma_start(dist[:, :], c.io["dist1"]).then_inc(d_c, 16)
    A.wait_ge(d_c, 16)

    def tokens_of(s):
        e, r = s // 4, s % 4
        return e, r, slice(HD * e, HD * e + HD)

    def pe(j, par, bl, proj, attn):
        tile = j - 1
        q, k, v = qT[1 - par], kT[1 - par], vS[1 - par]
        for s in range(12):
            if proj:
                b, bank = bl[s], pb[s % 2]
                c.use(b)
                g2, what2 = (s - 2) // 4, (s - 2) % 4
                if what2 == 3:
                    wt(T, em, j * 3 + (PRIME + g2 + 1))
                else:
                    wt(T, ev, j * 9 + (PRIME + g2 * 3 + what2 + 1))
                if s % 4 == 3:
                    ins = c.mod_chunk(b, c.ps[:, bank, :], range(KT))
                else:
                    ins = c.feat_chunk(b, c.ps[:, bank, :], h, range(KT))
                c.used(ins)
                if s % 4 == 3:
                    turn_values(c, vt, vx, vT, pb[(s - 1) % 2], j * 3 + (s // 4 + 1 + PRIME))
            if not attn:
                continue
            if s < 8:
                e, r, rows = tokens_of(s)
                own = slice(r * P, (r + 1) * P)
                at.qk(tile, s, [((0, W1), q[0][rows, own], k[0][rows, :]),
                                ((W1, P), q[1][rows, own], k[1][rows, own]),
                                ((W1 + P, P), q[2][rows, own], k[2][rows, own])],
                      extra=[(ev, tile * 9 + (9 + PRIME))] if s == 0 else ())
            if 1 <= s <= 8:
                at.transpose(tile, s - 1, NK)
            if 2 <= s <= 9:
                e, r, _ = tokens_of(s - 2)
                cols = slice(HD * e, HD * e + HD)
                at.pv(tile, s - 2, [v[0][:, t, cols] for t in range(DIL)] + [v[1][:, r, cols], v[2][:, r, cols]],
                      (2 * r + e) * HD)
            if s == 11:
                at.turn(tile)

    def ve(j, par, proj, attn):
        tile = j - 1
        for s in range(12):
            if proj and s % 4 == 3:
                wt(V, vx, j * 3 + (s // 4 + 1 + PRIME))
                V.tensor_copy(vS[par][s // 4][:, :, :].rearrange("p t n -> p (t n)"),
                              c.ps[:, pb[(s - 1) % 2], :]).then_inc(ev.h, 1)
            elif proj:
                V.wait_ge(c.s_used.h, j * 12 + (n0 + s + 1 + PRIME))
                g, what = s // 4, s % 4
                src = c.ps[:, pb[s % 2], :]
                if what == 2:
                    V.tensor_tensor(vT[:, :], src, c.RB[:, 0:SEQ], ALU.mult).then_inc(vt.h, 1)
                else:
                    V.tensor_tensor((qT, kT)[what][par][g][:, :], src, c.RB[:, 0:SEQ], ALU.mult).then_inc(ev.h, 1)
            if attn and s < 8:
                e, r, _ = tokens_of(s)
                wt(V, bs, at.u(tile, s, 0))
                at.ttr(tile, s, 1 - par, NK, bias[s % 2][:, :])
            if attn and s == 10:
                at.norm_out(tile, 1 - par, lambda d: d.rearrange("p (e r) -> p r e", e=2).unsqueeze(3)
                            .broadcast_to([P, 4, 2, HD]))
        if attn:
            at.out_lo(tile, al, ah)

    def ac(j, par, bl, proj, attn):
        tile = j - 1

        def make_bias(s):
            e, r, _ = tokens_of(s)
            wt(A, at.ttr_, at.u(tile, s - 2, 0))
            c.absorb(A)
            A.activation(bias[s % 2][:, :], dist[:, r * NK:(r + 1) * NK], ACT.Copy,
                         scale=c.slope[:, bass.ds(tile * 2 + (16 + e), 1)]).then_inc(bs.h, 1)
        for s in range(12):
            if proj:
                c.split_hi(bl[s])
            if proj and s % 4 == 3:
                A.wait_ge(c.s_used.h, j * 12 + (n0 + s + 1 + PRIME))
                c.absorb(A)
                A.activation(c.modraw[0][:, bass.ds((j * 3 + s // 4) * 4, 4)], c.ps[:, pb[s % 2], 0:4],
                             ACT.Copy).then_inc(em.h, 1)
            if attn and s == 0:
                make_bias(0)
                make_bias(1)
            if attn and s < 8:
                at.exp(tile, s, 1 - par, NK)
            if attn and s < 6:
                make_bias(s + 2)
            if attn and 1 <= s <= 8:
                at.copy_pt(tile, s - 1, NK)
        if attn:
            at.out_hi(tile, ah)

    for eng, part in ((T, pe),
                      (V, lambda j, par, bl, proj, attn: ve(j, par, proj, attn)),
                      (A, ac)):
        part(0, 0, [Blk(n0 + u) for u in range(12)], True, False)
        with eng.Fori(0, 3, 1) as i:
            for q in range(2):
                part(i * 2 + (q + 1), (q + 1) % 2, [Blk(n0 + 12 * (q + 1) + u, i, 24) for u in range(12)],
                     True, True)
        part(7, 1, [Blk(n0 + 84 + u) for u in range(12)], True, True)
        part(8, 0, None, False, True)
    at.finish(8)
    ev.n, em.n, bs.n = PRIME + 72, PRIME + 24, PRIME + 64
    return [(lambda e, v: wt(e, v), s) for s in (at.olo_, ev, em)]


def swiglu(c, n0, name, h, mh, ml, mod):
    nc, T, V, A = c.nc, c.T, c.V, c.A
    per = 3 if mod else 2
    pairs = 20 if mod else FT
    unroll = 4 if mod else 2
    gr = [c.ctx(name + f"gr{i}", [P, SEQ]) for i in range(2)]
    ur = [c.ctx(name + f"ur{i}", [P, SEQ]) for i in range(2)]
    s_gr, s_ur, s_m = (Sem(nc, name + x, V) for x in ("s_gr", "s_ur", "s_m"))
    s_sl, s_mh, s_md = (Sem(nc, name + x, A) for x in ("s_sl", "s_mh", "s_md"))
    s_ml = Sem(nc, name + "s_ml", V)

    def pe(j, q, b, withmod):
        g_bank, u_bank = 2 + 2 * (q % 2), 3 + 2 * (q % 2)
        c.use(b[0])
        wt(T, s_gr, j + (PRIME - 1))
        c.used(c.feat_chunk(b[0], c.ps[:, g_bank, :], h, range(KT)))
        c.use(b[1])
        wt(T, s_ur, j + (PRIME - 1))
        c.used(c.feat_chunk(b[1], c.ps[:, u_bank, :], h, range(KT)))
        if withmod:
            c.use(b[2])
            wt(T, s_md, j + (PRIME - 1))
            c.used(c.mod_chunk(b[2], c.ps[:, 6 + q % 2, :], range(KT)))

    def ve(j, q, used, withmod):
        i = q % 2
        V.wait_ge(c.s_used.h, used + 1)
        wt(V, s_m, j + (PRIME - 1))
        V.tensor_tensor(gr[i][:, :], c.ps[:, 2 + 2 * i, :], c.RB[:, 0:SEQ], ALU.mult).then_inc(s_gr.h, 1)
        V.wait_ge(c.s_used.h, used + 2)
        V.tensor_tensor(ur[i][:, :], c.ps[:, 3 + 2 * i, :], c.RB[:, 0:SEQ], ALU.mult).then_inc(s_ur.h, 1)
        wt(V, s_sl, j + (PRIME + 1))
        wt(V, s_ur, j + (PRIME + 1))
        V.tensor_tensor(ur[i][:, :], gr[i][:, :], ur[i][:, :], ALU.mult).then_inc(s_m.h, 1)
        wt(V, s_mh, j + (PRIME + 1))
        cols = bass.ds(j * SEQ, SEQ)
        V.tensor_tensor(ml[:, cols], ur[i][:, :], mh[:, cols].bitcast(F32), ALU.subtract).then_inc(s_ml.h, 1)

    def ac(j, q, b, used, withmod):
        i = q % 2
        c.split_hi(b[0])
        wt(A, s_gr, j + (PRIME + 1))
        A.activation(gr[i][:, :], gr[i][:, :], ACT.Silu).then_inc(s_sl.h, 1)
        c.split_hi(b[1])
        wt(A, s_m, j + (PRIME + 1))
        c.absorb(A)
        A.activation(mh[:, bass.ds(j * SEQ, SEQ)], ur[i][:, :], ACT.Copy).then_inc(s_mh.h, 1)
        if withmod:
            A.wait_ge(c.s_used.h, used + 3)
            c.absorb(A)
            A.activation(c.modraw[1][:, bass.ds(j * 4 + 16, 4)], c.ps[:, 6 + q % 2, 0:4], ACT.Copy).then_inc(s_md.h, 1)
            c.split_hi(b[2])

    def blks(q, i=0, it=0):
        return [Blk(n0 + per * q + x, i, it) for x in range(per)]

    for eng, part in ((T, lambda j, q, b, u, m: pe(j, q, b, m)), (V, lambda j, q, b, u, m: ve(j, q, u, m)),
                      (A, lambda j, q, b, u, m: ac(j, q, b, u, m))):
        with eng.Fori(0, pairs // unroll, 1) as i:
            for q in range(unroll):
                part(i * unroll + q, q, blks(q, i, per * unroll), i * (per * unroll) + (n0 + per * q + PRIME), mod)
        for j in range(pairs, FT):
            first = n0 + per * pairs + 2 * (j - pairs)
            part(j, j, [Blk(first), Blk(first + 1)], first + PRIME, False)
    for s in (s_gr, s_ur, s_m, s_sl, s_mh, s_ml):
        s.n = PRIME + FT
    s_md.n = PRIME + (pairs if mod else 0)
    return [(lambda e, v: wt(e, v), s) for s in (s_ml, s_md)]



def block_two_layer(c, l, n0, V_):
    nc, T, V, A, S, io = c.nc, c.T, c.V, c.A, c.S, c.io
    both = l == 0
    nt_q = NT if both else TT
    nq = nt_q * P
    vec, modv, ps = c.vec, c.modv, c.ps
    L = f"l{l}_"

    def up(sem, ins):
        return sem.up(ins)

    V.wait_ge(c.s_a.h, c.s_a.n)
    mr = c.modraw[l][:, :].rearrange("p (t k) -> p t k", k=4)
    V.tensor_tensor(modv[:, l, :, :], mr[:, :, 0:2], mr[:, :, 2:4], ALU.add)
    V.drain()
    V.tensor_tensor(modv[:, l, :, :], modv[:, l, :, :],
                    vec[:, V_["b_mod"] + l * MT:V_["b_mod"] + (l + 1) * MT].unsqueeze(2).broadcast_to([P, MT, 2]),
                    ALU.add)
    V.drain()
    amul = c.ctx(L + "amul", [P, KT, 2])
    V.tensor_scalar(amul[:, :, :], modv[:, l, KT:2 * KT, :], 1.0, None, ALU.add)
    V.drain()
    up(c.s_v, V.tensor_tensor(amul[:, :, :], amul[:, :, :],
                              vec[:, V_["norm_g"] + l * KT:V_["norm_g"] + (l + 1) * KT].unsqueeze(2)
                              .broadcast_to([P, KT, 2]), ALU.mult))
    V.drain()

    outer = c.scope()
    h_hi = c.ctx(L + "h_hi", [P, KT, ALLT], F32R)
    h_lo = c.ctx(L + "h_lo", [P, KT, ALLT], F32R)
    h_end = c.offset
    tok = c.scope()
    ag = c.ctx(L + "ag", [P, 4, ALLT])
    spare = c.offset
    cq = c.ctx(L + "cq", [P, 2, ALLT])
    ckv = c.ctx(L + "ckv", [P, ALLT])
    kro = c.ctx(L + "kro", [P, NT, A_ROPE])
    stage1 = c.scope()
    tmp = c.ctx(L + "tmp", [P, 3, ALLT])
    sqv = nc.alloc_sbuf_tensor_at(L + "sqv", [P, NT, 4, HD], F32, offset=stage1)
    dft = [c.ctx(L + f"dft{a}", [P, TT, SEQ]) for a in range(2)]
    dfc = [c.ctx(L + f"dfc{a}", [P, 2, CTX]) for a in range(2)]
    wfm = c.ctx(L + "wfm", [P, 2, 256])
    wsT = c.ctx(L + "wsT", [P, 4, P])
    dfd = c.ctx(L + "dfd", [P, 2, P])
    bsb = c.ctx(L + "bsb", [P, 2, P])
    glg = c.ctx(L + "glg", [P, HD])
    st = c.ctx(L + "st", [P, 2, NT * 4])
    after = c.scope()
    c.close(stage1 + (2 * A_HEADS * ALLT + NT * A_HEADS * A_V) * 4)
    gains = c.ctx(L + "gains", [P, 2, A_QK])
    gcol = c.ctx(L + "gcol", [P, 2])
    rope = c.ctx(L + "rope", [P, 2, TT, A_ROPE])
    rtab = c.ctx(L + "rtab", [P, 2, 2, TT, A_ROPE])
    small = c.ctx(L + "small", [P, 2, A_HEADS])
    rtmp = c.ctx(L + "rtmp", [P, A_HEADS, A_ROPE])
    c.close(after)
    d_s1, d_s2 = nc.alloc_semaphore(L + "d_s1"), nc.alloc_semaphore(L + "d_s2")
    loads2 = [(glg[:, :], io["glg"][l]), (bsb[:, :, :].rearrange("p a n -> p (a n)"), io["gbs"][l]),
              (gains[:, :, :].rearrange("p a n -> p (a n)"), io["qkg"][l]), (gcol[0:A_NOPE, :], io["qkgT"][l]),
              (rope[:, :, :, :].rearrange("p a b n -> p (a b n)"), io["rope"])]
    loads = [(dft[a][:, :, :], io["dft"][:, a]) for a in range(2)]
    loads += [(dfd[:, :, :].rearrange("p a n -> p (a n)"), io["dfd"]),
              (wfm[:, :, :].rearrange("p a n -> p (a n)"), io["wfmix"][l]),
              (wsT[:, :, :].rearrange("p a n -> p (a n)"), io["gws"][l])]
    if both:
        loads += [(dfc[a][:, :, :], io["dfc"][:, a]) for a in range(2)]
    for sem, some in ((d_s2, loads2), (d_s1, loads)):
        for d, src in some:
            A.dma_start(d, src).then_inc(sem, 16)
    hh0, hv0, hl0 = c.s_hh.n, c.s_v.n, c.s_hl.n
    parts = ((0, SEQ, 0, c.x), (SEQ, CTX, 1, c.y))

    def h_lo_of(k):
        wt(V, c.s_hh, hh0 + k + 1)
        for lo, n, cond, _ in parts:
            ins = V.scalar_tensor_tensor(h_lo[:, k, lo:lo + n], tmp[:, k % 3, lo:lo + n],
                                         modv[:, l, k, cond:cond + 1], h_hi[:, k, lo:lo + n].bitcast(F32),
                                         ALU.add, ALU.subtract)
        up(c.s_hl, ins)

    for k in range(KT):
        if k >= 3:
            wt(V, c.s_hl, hl0 + k - 2)
        for lo, n, cond, src in parts:
            ins = V.scalar_tensor_tensor(tmp[:, k % 3, lo:lo + n], src[:, k, :], amul[:, k, cond:cond + 1],
                                         c.RB[:, lo:lo + n], ALU.mult, ALU.mult)
        up(c.s_v, ins)
        wt(A, c.s_v, hv0 + k + 1)
        for lo, n, cond, _ in parts:
            ins = A.activation(h_hi[:, k, lo:lo + n], tmp[:, k % 3, lo:lo + n], ACT.Identity,
                               bias=modv[:, l, k, cond:cond + 1])
        up(c.s_hh, ins)
        if k:
            h_lo_of(k - 1)
    h_lo_of(KT - 1)

    n = n0
    tm = c.ctx(L + "tm", [P, NT, 512])
    for q in range(4):
        b = Blk(n + q)
        c.use(b)
        wt(T, c.s_hl, hl0 + 2 * q + 2)
        wh = c.w_hi[:, b.slot, :].rearrange("p (k n) -> p k n", k=2)
        wl = c.w_lo[:, b.slot, :].rearrange("p (k n) -> p k n", k=2)
        for k in range(2):
            kk = 2 * q + k
            for t in range(nt_q):
                ts = slice(t * P, (t + 1) * P)
                ins = c.mm3(ps[:, t, :], wh[:, k, :], wl[:, k, :], h_hi[:, kk, ts], h_lo[:, kk, ts],
                            kk == 0, kk == KT - 1, w_is_lhs=False)
        c.used(ins)
        c.split_hi(b)
    n += 4
    for t in range(nt_q):
        A.wait_ge(c.s_used.h, n + PRIME)
        up(c.s_a, A.activation(tm[:, t, :], ps[:, t, :], ACT.Copy))
    tm_done = c.s_a.n

    b = Blk(n)
    c.use(b)
    for lo, nn in ((0, SEQ), (SEQ, CTX)):
        for k in range(KT):
            ks = slice(k * A_ROPE, (k + 1) * A_ROPE)
            ins = c.mm3(c.flat(6, lo, nn)[0:A_ROPE], c.w_hi[:, b.slot, ks], c.w_lo[:, b.slot, ks],
                        h_hi[:, k, lo:lo + nn], h_lo[:, k, lo:lo + nn], k == 0, k == KT - 1)
    c.used(ins)
    c.split_hi(b)
    A.wait_ge(c.s_used.h, n + 1 + PRIME)
    krT = c.sq[0:A_ROPE, 1, :]
    up(c.s_a, A.activation(krT, c.flat(6, 0, ALLT)[0:A_ROPE], ACT.Copy))
    kro_done = c.s_a.n
    n += 1

    def turn_rope():
        wt(T, c.s_a, kro_done)
        for t in range(NT):
            ins = T.transpose(ps[:, 0, t * A_ROPE:(t + 1) * A_ROPE], krT[:, t * P:(t + 1) * P],
                              c.ident[0:A_ROPE, 0:A_ROPE])
        up(c.s_t, ins)
        wt(A, c.s_t)
        up(c.s_a, A.activation(kro[:, :, :].rearrange("p t d -> p (t d)"), ps[:, 0, 0:NT * A_ROPE], ACT.Copy))

    gv = tm[:, 0:nt_q, 256:512].rearrange("p t (h d) -> p t h d", h=4)
    ng = nt_q * 4

    def groups(ap):
        return ap.rearrange("p (t h) -> p t h", h=4)

    def wide_(ap):
        return groups(ap).unsqueeze(3).broadcast_to([P, nt_q, 4, HD])

    V.wait_ge(c.s_a.h, tm_done)
    V.tensor_reduce(groups(st[:, 0, 0:ng]), gv, AX.X, ALU.add)
    V.drain()
    V.tensor_scalar(st[:, 0, 0:ng], st[:, 0, 0:ng], 1.0 / HD, None, ALU.mult)
    V.drain()
    for t in range(nt_q):
        g4 = gv[:, t]
        V.tensor_tensor(g4, g4, st[:, 0, 4 * t:4 * t + 4].unsqueeze(2).broadcast_to([P, 4, HD]), ALU.subtract)
    V.drain()
    for t in range(nt_q):
        V.tensor_tensor(sqv[:, t], gv[:, t], gv[:, t], ALU.mult)
    V.drain()
    up(c.s_v, V.tensor_reduce(groups(st[:, 1, 0:ng]), sqv[:, 0:nt_q], AX.X, ALU.add))
    gate_sum = c.s_v.n

    def gate_norm():
        wt(A, c.s_v, gate_sum)
        up(c.s_a, A.activation(st[:, 1, 0:ng], st[:, 1, 0:ng], ACT.Sqrt, bias=EPS, scale=1.0 / HD))
        wt(V, c.s_a)
        V.reciprocal(st[:, 1, 0:ng], st[:, 1, 0:ng])
        V.drain()
        for t in range(nt_q):
            g4 = gv[:, t]
            V.tensor_tensor(g4, g4, st[:, 1, 4 * t:4 * t + 4].unsqueeze(2).broadcast_to([P, 4, HD]), ALU.mult)
        V.drain()
        V.wait_ge(d_s2, 16 * len(loads2))
        for t in range(nt_q):
            g4 = gv[:, t]
            ins = V.tensor_tensor(g4, g4, glg[:, :].unsqueeze(1).broadcast_to([P, 4, HD]), ALU.mult)
        up(c.s_v, ins)
        done = c.s_v.n
        V.tensor_scalar(gains[:, 0, :], gains[:, 0, :], A_QK ** -0.5, None, ALU.mult)
        V.tensor_scalar(gcol[0:A_NOPE, 0:1], gcol[0:A_NOPE, 0:1], A_QK ** -0.5, None, ALU.mult)
        V.memset(gcol[A_NOPE:A_QK, :], 1.0)
        V.drain()
        for w_ in range(2):
            V.tensor_tensor(rtab[:, w_, 0], rope[:, 0], gains[:, w_, A_NOPE:A_QK].unsqueeze(1)
                            .broadcast_to([P, TT, A_ROPE]), ALU.mult)
            for q in range(4):
                d0, g0 = 8 * q, A_NOPE + 8 * (q ^ 1)
                ins = V.tensor_tensor(rtab[:, w_, 1, :, d0:d0 + 8], rope[:, 1, :, d0:d0 + 8],
                                      gains[:, w_, g0:g0 + 8].unsqueeze(1).broadcast_to([P, TT, 8]), ALU.mult)
        up(c.s_v, ins)
        return done

    gu = c.ctx(L + "gu", [P, 2, ALLT])
    fg = c.ctx(L + "fg", [P, 2, ALLT])
    rows = (("cq", 0), ("cq", 1), ("ckv", 0), ("gg", 0), ("gg", 1), ("gu", 0), ("gu", 1), ("fg", 0), ("fg", 1),
            ("ag", 0), ("ag", 1), ("ag", 2), ("ag", 3))
    evac = []
    for i, (what, kk) in enumerate(rows):
        b = Blk(n + i)
        bank = (4, 6)[i % 2]
        if i == 3:
            gate_done = gate_norm()
        sem, v = evac[-2] if i >= 2 else (c.s_a, (tm_done, kro_done)[i])
        wt(T, sem, v)
        c.use(b)
        wh = c.w_hi[:, b.slot, :].rearrange("p (k m) -> p k m", k=KT)
        wl = c.w_lo[:, b.slot, :].rearrange("p (k m) -> p k m", k=KT)
        width = ALLT if (both or what == "ckv") else SEQ
        for lo, nn in ((0, SEQ), (SEQ, CTX))[:2 if width == ALLT else 1]:
            for k in range(KT):
                ins = c.mm3(c.flat(bank, lo, nn), wh[:, k, :], wl[:, k, :], h_hi[:, k, lo:lo + nn],
                            h_lo[:, k, lo:lo + nn], k == 0, k == KT - 1)
        c.used(ins)
        c.split_hi(b)
        if i == 0:
            turn_rope()
        done = n + i + 1 + PRIME
        src = c.flat(bank, 0, width)
        if what in ("cq", "ckv"):
            A.wait_ge(c.s_used.h, done)
            dst = cq[:, kk, 0:width] if what == "cq" else ckv[:, 0:width]
            gain_at = (V_["q_a_g"] + 2 * l + kk) if what == "cq" else V_["kv_a_g"] + l
            A.activation(dst, src, ACT.Copy, scale=vec[:, gain_at:gain_at + 1])
            c.norm_begin() if kk == 0 else None
            wt(A, c.s_ssq)
            up(c.s_sq, A.activation(c.sq[:, kk % 2, 0:width], src, ACT.Square))
            evac.append((c.s_sq, c.s_sq.n))
            c.sum_squares(kk, 2 if what == "cq" else 1, 0, 0 if what == "cq" else 1, width // P)
            if what == "ckv" or kk == 1:
                c.rstd(0 if what == "cq" else 1, width // P, 256 if what == "cq" else 128,
                       row=1 if what == "cq" else 2)
        elif what == "gu":
            V.wait_ge(c.s_used.h, done)
            wt(V, c.s_a)
            up(c.s_v, V.tensor_tensor(gu[:, kk, 0:width], src, gu[:, kk, 0:width], ALU.mult))
            evac.append((c.s_v, c.s_v.n))
        else:
            dst = {"gg": gu, "fg": fg, "ag": ag}[what]
            A.wait_ge(c.s_used.h, done)
            up(c.s_a, A.activation(dst[:, kk, 0:width], src, ACT.Silu))
            evac.append((c.s_a, c.s_a.n))
    n += 13
    wt(T, c.s_a)
    wt(T, c.s_v)
    wt(V, c.s_a)
    wt(A, c.s_v)

    m_hi = nc.alloc_sbuf_tensor_at(L + "m_hi", [P, KT, ALLT], F32R, offset=h_end - 2 * KT * ALLT * 4)
    m_lo = nc.alloc_sbuf_tensor_at(L + "m_lo", [P, KT, ALLT], F32R, offset=h_end - KT * ALLT * 4)
    V.wait_ge(c.s_used.h, n + PRIME)
    A.wait_ge(c.s_used.h, n + PRIME)

    def split_out(kk, src, width):
        wt(A, c.s_v)
        up(c.s_hh, A.activation(m_hi[:, kk, 0:width], src, ACT.Copy))
        wt(V, c.s_hh)
        up(c.s_hl, V.tensor_tensor(m_lo[:, kk, 0:width], src, m_hi[:, kk, 0:width].bitcast(F32), ALU.subtract))

    at_ = lambda name, shape, off: nc.alloc_sbuf_tensor_at(L + name, shape, F32, offset=off)
    ua = h_end - KT * ALLT * 4 - 4 * ALLT * 4
    ub = h_end - 4 * ALLT * 4
    U = at_("U", [P, 2, 2, ALLT], ua)
    F_ = at_("F", [P, 2, ALLT], ub)
    wuq = at_("wuq", [P, 2, A_HEADS * A_QK], ub + 2 * ALLT * 4)
    d_uq, d_ukv = nc.alloc_semaphore(L + "d_uq"), nc.alloc_semaphore(L + "d_ukv")
    A.dma_start(wuq[:, :, :].rearrange("p a n -> p (a n)"), io["wuq"][l]).then_inc(d_uq, 16)
    T.wait_ge(d_s1, 16 * len(loads))

    u_done = [0, 0]
    for ft in range(2):
        fs = slice(ft * P, (ft + 1) * P)
        for a in range(2):
            bank = (0, 2)[a]
            if ft:
                wt(T, c.s_a, u_done[a])
            for t in range(TT):
                ins = T.matmul(ps[:, bank, :], tm[:, t, fs], dft[a][:, t, :], start=t == 0, stop=t == TT - 1)
            if both:
                for t in range(2):
                    ins = T.matmul(ps[:, bank + 1, 0:CTX], tm[:, TT + t, fs], dfc[a][:, t, :], start=t == 0, stop=t == 1)
            up(c.s_t, ins)
            wt(A, c.s_t)
            up(c.s_a, A.activation(U[:, a, ft, 0:nq], c.flat(bank, 0, nq), ACT.Copy))
            u_done[a] = c.s_a.n
    pieces = ((0, SEQ), (SEQ, CTX))[:2 if both else 1]
    wt(T, c.s_a)
    for ft in range(2):
        bank = (4, 6)[ft]
        for lo, nn in pieces:
            T.matmul(c.flat(bank, lo, nn), dfd[:, 0, :], U[:, 0, ft, lo:lo + nn], start=True, stop=False)
            ins = T.matmul(c.flat(bank, lo, nn), dfd[:, 1, :], U[:, 1, ft, lo:lo + nn], start=False, stop=True)
        up(c.s_t, ins)
        wt(A, c.s_t)
        up(c.s_a, A.activation(F_[:, ft, 0:nq], c.flat(bank, 0, nq), ACT.Copy))
    wt(T, c.s_a)
    wukv = at_("wukv", [P, 1024], ua)
    A.dma_start(wukv[:, :], io["wukv"][l]).then_inc(d_ukv, 16)
    fm_read = []
    for ft in range(2):
        bank = (0, 2)[ft]
        for lo, nn in pieces:
            for k in range(2):
                ins = T.matmul(c.flat(bank, lo, nn), wfm[:, k, ft * P:(ft + 1) * P], F_[:, k, lo:lo + nn],
                               start=k == 0, stop=k == 1)
        up(c.s_t, ins)
        wt(V, c.s_t)
        up(c.s_v, V.tensor_tensor(fg[:, ft, 0:nq], c.flat(bank, 0, nq), fg[:, ft, 0:nq], ALU.mult))
        fm_read.append(c.s_v.n)
        split_out(ft, fg[:, ft, 0:nq], nq)

    wt(T, c.s_v, gate_done)
    mix_read = []
    for pr in range(2):
        bank = (4, 6)[pr]
        for t in range(nt_q):
            for e in range(2):
                hd = 2 * pr + e
                ins = T.matmul(c.flat(bank, t * P, P)[HD * e:HD * e + HD], tm[:, t, 256 + hd * HD:256 + (hd + 1) * HD],
                               wsT[:, hd, :], start=True, stop=True)
        up(c.s_t, ins)
        wt(V, c.s_t)
        mixed = sqv[:, :, :, :].rearrange("p t h d -> p (t h d)")[:, pr * ALLT:pr * ALLT + nq]
        V.tensor_tensor(mixed.rearrange("p (t n) -> p t n", n=P), c.flat(bank, 0, nq).rearrange("p (t n) -> p t n", n=P),
                        bsb[:, pr, :].unsqueeze(1).broadcast_to([P, nt_q, P]), ALU.add)
        V.drain()
        up(c.s_v, V.tensor_tensor(mixed, mixed, gu[:, pr, 0:nq], ALU.mult))
        mix_read.append(c.s_v.n)
        split_out(2 + pr, mixed, nq)
    wt(A, c.s_hl)
    c.close(stage1)

    kT = c.ctx(L + "kT", [A_QK, A_HEADS, ALLT])
    qT = c.ctx(L + "qT", [A_QK, A_HEADS, ALLT])
    vS = c.ctx(L + "vS", [P, NT, A_HEADS * A_V])
    stage2 = c.scope()
    work = [at_(f"work{i}", [P, A_HEADS, A_QK], (ub, ub + ALLT * 4, ua + 4096)[i]) for i in range(3)]
    flatw = [w[:, :, :].rearrange("p h d -> p (h d)") for w in work]
    wsq = [c.RB[:, :], c.sq[:, 1, :]]
    heads = lambda ap: ap.rearrange("p (h d) -> p h d", h=A_HEADS)
    T.wait_ge(d_uq, 16)
    T.wait_ge(d_ukv, 16)
    jobs = [("k", t) for t in range(NT)] + [("q", t) for t in range(nt_q)]
    nj = len(jobs)
    pj_, evac_, sum_, std_, fin_, turn_, out_ = ([0] * nj for _ in range(7))

    def project(i):
        what, t = jobs[i]
        bank, ts = (0, 2)[i % 2], slice(t * P, (t + 1) * P)
        if i >= 2:
            wt(T, c.s_a, evac_[i - 2])
        else:
            wt(T, c.s_v, fm_read[i])
        if what == "k":
            for half in range(2):
                ins = T.matmul(ps[:, bank + half, :], ckv[:, ts], wukv[:, half * 512:(half + 1) * 512],
                               start=True, stop=True)
        else:
            for half in range(2):
                for k in range(2):
                    ins = T.matmul(ps[:, bank + half, 0:384], cq[:, k, ts], wuq[:, k, half * 384:(half + 1) * 384],
                                   start=k == 0, stop=k == 1)
        pj_[i] = up(c.s_t, ins)

    def turn_heads(i):
        wt(T, c.s_v, fin_[i])
        if i >= 2:
            wt(T, c.s_a, out_[i - 2])
        else:
            wt(T, c.s_v, mix_read[i])
        for hd in range(A_HEADS):
            ins = T.transpose(c.flat((4, 6)[i % 2], hd * P, P)[0:A_QK], work[i % 3][:, hd, :], c.ident[:, :])
        turn_[i] = up(c.s_t, ins)

    def evacuate(i):
        what, t = jobs[i]
        bank, w = (0, 2)[i % 2], work[i % 3]
        wt(A, c.s_t, pj_[i])
        if i >= 3:
            wt(A, c.s_t, turn_[i - 3])
        if what == "k":
            r = c.r_tok[:, 2, t:t + 1]
            A.activation(w[:, :, A_NOPE:A_QK], kro[:, t, :].unsqueeze(1).broadcast_to([P, A_HEADS, A_ROPE]), ACT.Copy)
            A.activation(vS[:, t, :], ps[:, bank + 1, :], ACT.Copy, scale=r)
            evac_[i] = up(c.s_a, A.activation(w[:, :, 0:A_NOPE], heads(ps[:, bank, :]), ACT.Copy, scale=r))
        else:
            r = c.r_tok[:, 1, t:t + 1]
            for half in range(2):
                ins = A.activation(flatw[i % 3][:, half * 384:(half + 1) * 384], ps[:, bank + half, 0:384],
                                   ACT.Copy, scale=r)
            evac_[i] = up(c.s_a, ins)
        A.drain()
        if i >= 2:
            wt(A, c.s_v, sum_[i - 2])
        up(c.s_a, A.activation(wsq[i % 2], flatw[i % 3], ACT.Square))

    def finish_job(i):
        what, t = jobs[i]
        w, w_, sm = work[i % 3], 0 if what == "q" else 1, small[:, i % 2, :]
        wt(V, c.s_a, std_[i])
        V.reciprocal(sm, sm)
        V.drain()
        V.tensor_tensor(w[:, :, :], w[:, :, :], sm.unsqueeze(2).broadcast_to([P, A_HEADS, A_QK]), ALU.mult)
        V.drain()
        wr = w[:, :, A_NOPE:A_QK]
        if t < TT:
            wr4 = wr.rearrange("p h (a x) -> p h a x", a=2)
            rt4 = rtmp[:, :, :].rearrange("p h (a x) -> p h a x", a=2)
            tab = rtab[:, w_, 1, t, :].rearrange("p (a x) -> p a x", a=2)
            for q in range(2):
                a0, b0 = 8 * q, 8 * (1 - q)
                V.tensor_tensor(rt4[:, :, :, a0:a0 + 8], wr4[:, :, :, b0:b0 + 8],
                                tab[:, :, a0:a0 + 8].unsqueeze(1).broadcast_to([P, A_HEADS, 2, 8]), ALU.mult)
            V.drain()
            V.tensor_tensor(wr, wr, rtab[:, w_, 0, t, :].unsqueeze(1).broadcast_to([P, A_HEADS, A_ROPE]), ALU.mult)
            V.drain()
            ins = V.tensor_tensor(wr, wr, rtmp[:, :, :], ALU.add)
        else:
            ins = V.tensor_tensor(wr, wr, gains[:, w_, A_NOPE:A_QK].unsqueeze(1).broadcast_to([P, A_HEADS, A_ROPE]),
                                  ALU.mult)
        fin_[i] = up(c.s_v, ins)

    def copy_out(i):
        what, t = jobs[i]
        w_ = 0 if what == "q" else 1
        wt(A, c.s_t, turn_[i])
        src = c.flat((4, 6)[i % 2], 0, 1024)[0:A_QK].rearrange("p (h n) -> p h n", h=A_HEADS)
        out_[i] = up(c.s_a, A.activation((kT if what == "k" else qT)[:, :, t * P:(t + 1) * P], src, ACT.Copy,
                                         scale=gcol[0:A_QK, w_:w_ + 1]))

    for i in range(nj + 2):
        if i < nj:
            project(i)
        if i >= 2:
            turn_heads(i - 2)
        if i < nj:
            evacuate(i)
            squared = c.s_a.n
        if 1 <= i <= nj:
            finish_job(i - 1)
        if i < nj:
            wt(V, c.s_a, squared)
            sum_[i] = up(c.s_v, V.tensor_reduce(small[:, i % 2, :], heads(wsq[i % 2]), AX.X, ALU.add))
        if i >= 2:
            copy_out(i - 2)
        if i < nj:
            wt(A, c.s_v, sum_[i])
            std_[i] = up(c.s_a, A.activation(small[:, i % 2, :], small[:, i % 2, :], ACT.Sqrt, bias=EPS,
                                             scale=1.0 / A_QK))
    wt(T, c.s_a)
    wt(V, c.s_a)
    wt(A, c.s_v)
    wt(V, c.s_t)
    wt(A, c.s_t)
    c.close(stage2)
    joint_attention(c, l, 0, TT, ALLT, 0, kT, qT, vS, ag, m_hi, m_lo, spare)
    if both:
        joint_attention(c, l, TT, NT - TT, CTX, SEQ, kT, qT, vS, ag, m_hi, m_lo, spare)
    c.close(tok)

    x0 = c.s_x.n
    sums = lambda k: [(4, c.sq[:, k % 2, 0:SEQ]), (5, c.sq[:, k % 2, SEQ:ALLT])]
    if both:
        c.norm_begin()
    for u in range(KT):
        b, bank = Blk(n + u), (0, 2)[u % 2]
        c.use(b)
        wt(T, c.s_x, x0 + u - 1)
        for lo, nn in pieces:
            for k in range(KT):
                wh = c.w_hi[:, b.slot, k * P:(k + 1) * P]
                wl = c.w_lo[:, b.slot, k * P:(k + 1) * P]
                ins = c.mm3(c.flat(bank, lo, nn), wh, wl, m_hi[:, k, lo:lo + nn], m_lo[:, k, lo:lo + nn],
                            k == 0, k == KT - 1)
        c.used(ins)
        c.split_hi(b)
        V.wait_ge(c.s_used.h, n + u + 1 + PRIME)
        if both:
            V.scalar_tensor_tensor(c.y[:, u, :], ps[:, bank + 1, 0:CTX], modv[:, l, 2 * KT + u, 1:2], c.y[:, u, :],
                                   ALU.mult, ALU.add)
        c.s_x.up(V.scalar_tensor_tensor(c.x[:, u, :], ps[:, bank, :], modv[:, l, 2 * KT + u, 0:1], c.x[:, u, :],
                                        ALU.mult, ALU.add))
        if both:
            wt(A, c.s_x)
            c.s_sq.up(square_both(c, u))
            if u:
                c.sum_rows(u - 1, KT, sums(u - 1))
    if both:
        c.sum_rows(KT - 1, KT, sums(KT - 1))
        c.rstd_rows(4, ALLT, c.RB[:, :])
        wt(T, c.s_std)
    wt(A, c.s_x)
    wt(T, c.s_x)
    c.close(outer)
    return n + KT


def joint_attention(c, l, t0, nqb, nk, k0, kT, qT, vS, ag, m_hi, m_lo, spare):
    nc, T, V, A = c.nc, c.T, c.V, c.A
    L = f"j{l}{t0}_"
    sc = c.scope()
    KTL = nk // P
    mk = lambda nme, e: Sem(nc, L + nme, e)
    s_q, s_exp, s_hi = (mk(x, A) for x in ("q", "exp", "hi"))
    s_mx, s_pt, s_on, s_g, s_lo = (mk(x, V) for x in ("mx", "pt", "on", "g", "lo"))
    s_qk, s_tr, s_pv, s_ot = (mk(x, T) for x in ("qk", "tr", "pv", "ot"))
    qc = [c.ctx(L + f"qc{i}", [A_QK, A_HEADS, P]) for i in range(1)]
    prob = [nc.alloc_sbuf_tensor_at(L + f"prob{i}", [P, nk], F32, offset=spare + i * ALLT * 4) for i in range(2)]
    probT = [nc.alloc_sbuf_tensor_at(L + "probT0", [P, nk], F32, offset=spare + 2 * ALLT * 4)[:, :], c.sq[:, 0, 0:nk]]
    nm = c.ctx(L + "nm", [P, A_HEADS])
    den = c.ctx(L + "den", [P, A_HEADS])
    rden = c.ctx(L + "rden", [P, A_HEADS])
    osb = c.ctx(L + "osb", [P, 512])
    gt = c.sq[:, 1, 0:512].rearrange("p (f n) -> p f n", f=4)
    cut = [(0, min(nk, 512))] + ([(512, nk - 512)] if nk > 512 else [])
    sbank, tbank, o_bank, ot_bank = (0, 2), 4, 6, 7

    with T.Fori(0, nqb, 1) as i:
        u = lambda s: i * 8 + (s + 1 + PRIME)

        def pv(s):
            wt(T, s_pt, u(s))
            if s == 0:
                wt(T, s_on, i + PRIME)
            for k in range(KTL):
                ins = T.matmul(c.ps[:, o_bank, s * A_V:(s + 1) * A_V], probT[s % 2][:, k * P:(k + 1) * P],
                               vS[:, k0 // P + k, s * A_V:(s + 1) * A_V], start=k == 0, stop=k == KTL - 1)
            ins.then_inc(s_pv.h, 1)

        def tr(s):
            wt(T, s_exp, u(s))
            wt(T, s_pt, u(s - 1))
            for k in range(KTL):
                ins = T.transpose(c.flat(tbank, k * P, P), prob[s % 2][:, k * P:(k + 1) * P], c.ident[:, :])
            ins.then_inc(s_tr.h, 1)

        for s in range(8):
            if s == 0:
                wt(T, s_q, i + (1 + PRIME))
            wt(T, s_exp, u(s - 2))
            for lo, nn in cut:
                ins = T.matmul(c.flat(sbank[s % 2], lo, nn), qc[0][:, s, :], kT[:, s, k0 + lo:k0 + lo + nn],
                               start=True, stop=True)
            ins.then_inc(s_qk.h, 1)
            if s >= 1:
                tr(s - 1)
            if s >= 2:
                pv(s - 2)
        tr(7)
        pv(6)
        pv(7)
        wt(T, s_on, i + (1 + PRIME))
        wt(T, s_g, i + PRIME)
        for b in range(4):
            ins = T.transpose(c.ps[:, ot_bank, b * P:(b + 1) * P], osb[:, b * P:(b + 1) * P], c.ident[:, :])
        ins.then_inc(s_ot.h, 1)

    with V.Fori(0, nqb, 1) as i:
        u = lambda s: i * 8 + (s + 1 + PRIME)

        def ptc(s):
            wt(V, s_tr, u(s))
            wt(V, s_pv, u(s - 2))
            V.tensor_copy(probT[s % 2][:, 0:nk], c.flat(tbank, 0, nk)).then_inc(s_pt.h, 1)
        for s in range(8):
            wt(V, s_qk, u(s))
            V.tensor_reduce(nm[:, s:s + 1], c.flat(sbank[s % 2], 0, nk), AX.X, ALU.max, negate=True).then_inc(s_mx.h, 1)
            if s >= 1:
                ptc(s - 1)
        ptc(7)
        wt(V, s_exp, u(7))
        V.reciprocal(rden[:, :], den[:, :])
        V.drain()
        wt(V, s_pv, u(7))
        wt(V, s_ot, i + PRIME)
        V.tensor_tensor(osb[:, :].rearrange("p (h d) -> p h d", h=A_HEADS),
                        c.ps[:, o_bank, :].rearrange("p (h d) -> p h d", h=A_HEADS),
                        rden[:, :].unsqueeze(2).broadcast_to([P, A_HEADS, A_V]), ALU.mult).then_inc(s_on.h, 1)
        wt(V, s_ot, i + (1 + PRIME))
        wt(V, s_lo, i + PRIME)
        cols = bass.ds(i * P + t0 * P, P)
        V.tensor_tensor(gt, c.ps[:, ot_bank, :].rearrange("p (f n) -> p f n", f=4), ag[:, :, cols],
                        ALU.mult).then_inc(s_g.h, 1)
        wt(V, s_hi, i + (1 + PRIME))
        V.tensor_tensor(m_lo[:, 4:8, cols], gt, m_hi[:, 4:8, cols].bitcast(F32),
                        ALU.subtract).then_inc(s_lo.h, 1)

    with A.Fori(0, nqb, 1) as i:
        u = lambda s: i * 8 + (s + 1 + PRIME)
        cols = bass.ds(i * P + t0 * P, P)
        wt(A, s_qk, u(-1))
        c.absorb(A)
        A.activation(qc[0][:, :, :], qT[:, :, cols], ACT.Copy).then_inc(s_q.h, 1)
        for s in range(8):
            wt(A, s_mx, u(s))
            wt(A, s_tr, u(s - 2))
            A.activation(prob[s % 2][:, :], c.flat(sbank[s % 2], 0, nk), ACT.Exp, bias=nm[:, s:s + 1],
                         accum_out=den[:, s:s + 1]).then_inc(s_exp.h, 1)
        wt(A, s_g, i + (1 + PRIME))
        c.absorb(A)
        A.activation(m_hi[:, 4:8, cols], gt, ACT.Copy).then_inc(s_hi.h, 1)
    for s in (s_exp, s_mx, s_pt, s_qk, s_tr, s_pv):
        s.n = PRIME + 8 * nqb
    for s in (s_q, s_hi, s_on, s_g, s_lo, s_ot):
        s.n = PRIME + nqb
    for e in (T, A):
        wt(e, s_lo)
    wt(V, s_pv)
    wt(V, s_hi)
    wt(A, s_pv)
    c.close(sc)


def build(nc, io, V_):
    c = Core(nc, io)
    T, V, A, G, S = c.T, c.V, c.A, c.G, c.S

    c.top = (nc.sbuf_base + 31) // 32 * 32
    c.offset = c.top

    def ctx(name, shape, dt=F32):
        size = int(np.prod(shape[1:])) * 4
        t = nc.alloc_sbuf_tensor_at(name, shape, dt, offset=c.offset)
        c.offset += (size + 31) // 32 * 32
        return t

    c.ctx = ctx
    c.scope = lambda: c.offset

    def close(mark):
        c.offset = mark
    c.close = close

    S.dma_start(c.vec[:, :], io["vec"]).then_inc(c.d_const, 16)
    S.dma_start(c.ident[:, :], io["ident"]).then_inc(c.d_const, 16)
    S.dma_start(c.slope[:, :], io["slope"]).then_inc(c.d_const, 16)
    d_x = [nc.alloc_semaphore(f"d_x{i}") for i in range(4)]
    for i in range(4):
        S.dma_start(c.x[:, 2 * i:2 * i + 2, :], io["x"][:, 2 * i:2 * i + 2, :]).then_inc(d_x[i], 16)
    d_y = nc.alloc_semaphore("d_y")
    S.dma_start(c.y[:, :, :], io["ctx"]).then_inc(d_y, 16)
    V.memset(c.ones[:, :], 1.0).then_inc(c.s_v.h, 1)
    c.s_v.n += 1
    wt(T, c.s_v)
    for e in (T, V, A):
        e.wait_ge(c.d_const, 48)
    c1 = c.scope()
    cs = c.ctx("cs", [P, KT, 2])
    A.activation(cs[:, :, :], c.vec[:, V_["c"]:V_["c"] + 2 * KT].rearrange("p (k a) -> p k a", a=2), ACT.Silu)
    A.drain()
    c.s_a.up(A.activation(c.c4[:, :, 0:2], cs[:, :, :], ACT.Copy))
    wt(V, c.s_a)
    c.s_v.up(V.tensor_tensor(c.c4[:, :, 2:4], cs[:, :, :], c.c4[:, :, 0:2].bitcast(F32), ALU.subtract))
    wt(T, c.s_v)

    c.stream_loops()
    for b in range(LEAD):
        c.split_hi(Blk(b - LEAD))

    h = (c.ctx("h_hi", [P, KT, SEQ], F32R), c.ctx("h_lo", [P, KT, SEQ], F32R))
    vcol = lambda name, i=0: c.vec[:, V_[name] + i * KT:V_[name] + (i + 1) * KT]
    body = c.scope()

    c.norm_begin()
    c.s_hh_base = c.s_hh.n
    for k in range(KT):
        norm_tile(c, h, k, vcol("norm_mix", 0), natural, 16, d_x[k // 2])
        norm_tile_lo(c, h, k, vcol("norm_mix", 0), natural)
        c.sum_rows(k, KT, [(0, c.sq[:, k % 2, 0:SEQ])])
    norm_finish(c)
    A.wait_ge(d_y, 16)
    V.wait_ge(d_y, 16)
    context_norm(c)
    n = 0
    ah, al = c.ctx("a_hi", [P, KT * SEQ], F32R), c.ctx("a_lo", [P, KT * SEQ], F32R)
    ready = window_attention(c, n, h, ah, al)
    n += 16
    contract_out(c, n, KT, (ah, al), natural, (h, vcol("norm_ffn", 0), natural), ready)
    norm_finish(c)
    n += KT
    c.close(body)

    def ffn(n, name, mod, nxt):
        mh, ml = c.ctx(name + "m_hi", [P, FT * SEQ], F32R), c.ctx(name + "m_lo", [P, FT * SEQ], F32R)
        ready = swiglu(c, n, name, h, mh, ml, mod)
        n += 2 * FT + (20 if mod else 0)
        contract_out(c, n, FT, (mh, ml), natural, nxt, ready)
        c.close(body)
        return n + FT

    n = ffn(n, "f0", False, (h, vcol("norm_mix", 1), residues))
    norm_finish(c)
    ah, al = c.ctx("b_hi", [P, KT * SEQ], F32R), c.ctx("b_lo", [P, KT * SEQ], F32R)
    ready = dilated_attention(c, n, h, ah, al)
    n += 96
    contract_out(c, n, KT, (ah, al), residues, (h, vcol("norm_ffn", 1), natural), ready)
    norm_finish(c)
    n += KT
    c.close(body)
    n = ffn(n, "f1", True, (None, vcol("norm_final"), natural))
    c.close(c1)
    final_norm(c, vcol("norm_final"))
    for l in range(2):
        n = block_two_layer(c, l, n, V_)
    assert n == len(PLAN), (n, len(PLAN))
    d_out = nc.alloc_semaphore("d_out")
    S.wait_ge(c.s_x.h, c.s_x.n)
    S.dma_start(io["out"], c.x[:, :, :]).then_inc(d_out, 16)
    S.wait_ge(d_out, 16)



def shape_constants():
    j = np.arange(P)
    k = np.arange(3 * P)
    rel = np.abs(k[None, :] - WIN - j[:, None]).astype(np.float64)
    dist0 = np.where(rel <= WIN, -rel, -BIG)
    t = 4 * j[:, None]
    keys = np.concatenate([DIL * np.arange(P) + r for r in range(DIL)])
    cols = []
    dj = np.abs(j[:, None] - j[None, :])
    own2 = np.where(dj <= 64, -4.0 * dj, -BIG)
    own3 = np.where(dj % 4 == 0, -4.0 * dj, -BIG)
    for r in range(DIL):
        d = np.abs(t + r - keys[None, :]).astype(np.float64)
        cols += [np.where(d <= 64, -d, -BIG), own2, own3]
    dist1 = np.concatenate(cols, axis=1)
    slope = lambda hd: 2.0 ** (-8.0 * (hd + 1) / 16) * 8.0
    row = [slope(4 * (2 * (tt // 4) + e) + tt % 4) for tt in range(8) for e in range(2)] + [slope(hd) for hd in range(16)]
    slopes = np.tile(np.array(row)[None, :], (P, 1))

    def dft(n, scale):
        a = np.arange(n)
        ang = 2 * np.pi * ((a[:, None] * a[None, :]) % n) / n
        m = np.stack([np.cos(ang), np.sin(ang)]) * scale
        return m.reshape(2, n // P, P, n).transpose(2, 0, 1, 3)
    a = np.arange(64)
    ang = 2 * np.pi * ((a[:, None] * a[None, :]) % 64) / 64
    bd = np.zeros((2, P, P))
    for g in range(2):
        s = slice(64 * g, 64 * g + 64)
        bd[0, s, s] = np.cos(ang) / 8.0
        bd[1, s, s] = -np.sin(ang) / 8.0
    half = A_ROPE // 2
    tok = np.arange(SEQ)
    inv = (10000.0 ** (-np.arange(0, half, 2, dtype=np.float32) / half)).astype(np.float32)
    ar = (tok // 64).astype(np.float32)[:, None] * inv[None, :]
    ac = (tok % 64).astype(np.float32)[:, None] * inv[None, :]
    angs = np.concatenate([ar, ar, ac, ac], -1).astype(np.float32)
    sign = np.repeat(np.array([-1.0, 1.0, -1.0, 1.0]), 8)
    rope = np.stack([np.cos(angs), np.sin(angs) * sign[None, :]])
    rope = rope.reshape(2, TT, P, A_ROPE).transpose(2, 0, 1, 3).reshape(P, -1)
    out = {"dist0": dist0, "dist1": dist1, "slope": slopes, "ident": np.eye(P), "dft": dft(SEQ, SEQ ** -0.5),
           "dfc": dft(CTX, CTX ** -0.5), "dfd": bd.transpose(1, 0, 2).reshape(P, -1), "rope": rope}
    return {n: np.ascontiguousarray(v, dtype=np.float32) for n, v in out.items()}


def lay_out(x):
    g = {n: np.asarray(v) for n, v in x.items()}
    colblk = lambda w, t: w[:, t * P:(t + 1) * P].reshape(KT, P, P).transpose(1, 0, 2).reshape(P, 1024)
    hcols = lambda hd: np.arange(hd * HD, (hd + 1) * HD)
    pair = lambda tt: (4 * (2 * (tt // 4)) + tt % 4, 4 * (2 * (tt // 4) + 1) + tt % 4)
    qa = np.concatenate([hcols(hd) for tt in range(8) for hd in pair(tt)])
    wa = g["w_qkv_a"][0]
    waq, wak, wav = wa[:, :1024][:, qa], wa[:, 1024:1280], wa[:, 1280:1536]
    woa = g["w_out_a"][0][qa, :]
    wb = g["w_qkv_b"][0].reshape(D_MODEL, 3, 3, 1024)
    win = g["w_in_2"]
    o = dict(f=0, fg=256, gu=512, gv=768, gg=1024, cq=1280, ckv=1536, kr=1664, ag=1696)
    tokcols = np.concatenate([np.arange(256), np.arange(o["gv"], o["gv"] + 256)])
    feat = np.concatenate([np.arange(o[nme], o[nme] + w) for nme, w in
                           (("cq", 256), ("ckv", 128), ("gg", 256), ("gu", 256), ("fg", 256), ("ag", 512))])
    blocks = []
    for kind, *w in PLAN:
        if kind == "ak":
            b = colblk(wak, w[0])
        elif kind == "av":
            b = colblk(wav, w[0])
        elif kind == "aq":
            b = colblk(waq, w[0])
        elif kind == "mod":
            b = colblk(g["w_mod_2"][w[0]], w[1])
        elif kind == "oa":
            b = woa[w[0] * P:(w[0] + 1) * P]
        elif kind == "ob":
            b = g["w_out_b"][0][w[0] * P:(w[0] + 1) * P]
        elif kind == "gate":
            b = colblk(g["w_gate"][w[0]], w[1])
        elif kind == "up":
            b = colblk(g["w_up"][w[0]], w[1])
        elif kind == "down":
            b = g["w_down"][w[0]][w[1] * P:(w[1] + 1) * P]
        elif kind in ("bq", "bk", "bv"):
            b = colblk(wb[:, w[0], "qkv".index(kind[1])], w[1])
        elif kind == "kr":
            b = np.zeros((P, 1024), np.float32)
            b[:, :KT * A_ROPE] = win[w[0]][:, o["kr"]:o["kr"] + 32].reshape(KT, P, 32).transpose(1, 0, 2).reshape(P, -1)
        elif kind == "tok":
            b = win[w[0]][:, tokcols][w[1] * 256:(w[1] + 1) * 256].reshape(2, P, 512).transpose(1, 0, 2).reshape(P, 1024)
        elif kind == "feat":
            b = colblk(win[w[0]][:, feat], w[1])
        elif kind == "out":
            b = colblk(g["w_out_2"][w[0]], w[1])
        blocks.append(b)
    arr = {"wstream": np.stack(blocks)}
    ft = lambda a: a.reshape(-1, P).T
    vec, V_ = [], {}

    def add(name, a):
        V_[name] = sum(v.shape[1] for v in vec)
        vec.append(a)
    add("norm_mix", ft(g["norm_mix"]))
    add("norm_ffn", ft(g["norm_ffn"]))
    add("norm_final", ft(g["norm_final"]))
    add("norm_g", ft(g["norm_g_2"]))
    add("b_mod", ft(g["b_mod_2"]))
    add("q_a_g", ft(g["q_a_g_2"]))
    add("kv_a_g", ft(g["kv_a_g_2"]))
    add("c", np.stack([ft(g["c_2"][0]), ft(g["c_ctx_2"])], axis=2).reshape(P, 2 * KT))
    arr["vec"] = np.concatenate(vec, axis=1)
    arr["x"] = g["x"][0].T.reshape(KT, P, SEQ).transpose(1, 0, 2)
    arr["ctx"] = g["ctx_2"][0].T.reshape(KT, P, CTX).transpose(1, 0, 2)
    arr["sinks"] = np.broadcast_to(np.concatenate(
        [np.tile(g["sink_a"][0][list(pair(tt))], 4) for tt in range(8)])[None, :], (P, 64))
    arr["wfmix"] = g["w_fmix_2"].reshape(2, 2, P, 256).transpose(0, 2, 1, 3).reshape(2, P, 512)
    arr["gws"] = g["g_ws_2"].transpose(0, 3, 1, 2).reshape(2, P, 512)
    arr["gbs"] = np.repeat(g["g_bs_2"].reshape(2, 2, 2, 1, P), HD, axis=3).reshape(2, 2, P, P).transpose(0, 2, 1, 3).reshape(2, P, 2 * P)
    arr["glg"] = np.broadcast_to(g["g_ln_g_2"][:, None, :], (2, P, HD))
    arr["wuq"] = g["w_uq_2"].reshape(2, 2, P, 768).transpose(0, 2, 1, 3).reshape(2, P, 1536)
    arr["wukv"] = g["w_ukv_2"].reshape(2, P, A_HEADS, 2, 64).transpose(0, 1, 3, 2, 4).reshape(2, P, 1024)
    arr["qkg"] = np.broadcast_to(np.stack([g["q_norm_g_2"], g["k_norm_g_2"]], 1)[:, None], (2, P, 2, A_QK)).reshape(2, P, 2 * A_QK)
    arr["qkgT"] = np.stack([g["q_norm_g_2"], g["k_norm_g_2"]], 2)[:, :A_NOPE]
    arr = {n: np.ascontiguousarray(v) for n, v in arr.items()}
    arr.update(shape_constants())
    return arr, V_


def kernel(**inputs):
    from concourse import bacc
    from concourse.bass_utils import run_bass_kernel_spmd
    arr, V_ = lay_out(inputs)
    nc = bacc.Bacc("TRN2", target_bir_lowering=False, num_devices=1)
    io = {n: nc.dram_tensor("in_" + n, a.shape, F32, kind="ExternalInput").ap() for n, a in arr.items()}
    io["out"] = nc.dram_tensor("out", (P, KT, SEQ), F32, kind="ExternalOutput").ap()
    build(nc, io, V_)
    r = run_bass_kernel_spmd(nc, [{"in_" + n: a for n, a in arr.items()}], core_ids=[0])
    o = r.results[0]["out"]
    return np.ascontiguousarray(o.transpose(1, 0, 2).reshape(D_MODEL, SEQ).T)[None]
```

```python
import numpy as np
from concourse import bass, mybir
from concourse.alu_op_type import AluOpType as ALU

F32 = mybir.dt.float32
F32R = mybir.dt.float32r
ACT = mybir.ActivationFunctionType
AX = mybir.AxisListType

P = 128
D_MODEL = 1024
KT = D_MODEL // P
SEQ = 512
TT = SEQ // P
CTX = 256
ALLT = SEQ + CTX
NT = ALLT // P
EPS = 1e-6
HD = 64
D_FF = 2816
FT = D_FF // P
WIN = 128
DIL = 4
MT = 3 * KT
A_HEADS, A_NOPE, A_ROPE, A_V = 8, 64, 32, 64
A_QK = A_NOPE + A_ROPE
BIG = 1e32
RING = 4
LEAD = 3
MROWS = 5
PRIME = 8


def stream_plan():
    s = []
    mod = [(0, t) for t in range(MT)]
    mod1 = [(1, t) for t in range(MT)]
    for m in range(2):
        s += [("ak", m), ("av", m)] + [("aq", 4 * m + i) for i in range(4)]
        s += [("mod", *mod1.pop(0)) for _ in range(2)]
    s += [("oa", t) for t in range(KT)]
    for j in range(FT):
        s += [("gate", 0, j), ("up", 0, j)]
    s += [("down", 0, j) for j in range(FT)]
    for p in range(8):
        for g in range(3):
            s += [("bq", g, p), ("bk", g, p), ("bv", g, p), ("mod", *mod.pop(0))]
    s += [("ob", t) for t in range(KT)]
    for j in range(FT):
        if j < MROWS * 4:
            s += [("modrow", j // 4, j % 4)]
        s += [("gate", 1, j), ("up", 1, j)]
    s += [("down", 1, j) for j in range(FT)]
    for l in range(2):
        s += [("tok", l, b) for b in range(4)] + [("kr", l)]
        s += [("feat", l, t) for t in range(13)]
        s += [("out", l, t) for t in range(KT)]
    assert not mod and len(mod1) == 4 * MROWS
    return s


PLAN = stream_plan()


class Blk:

    def __init__(self, const, i=0, per=0):
        assert per % RING == 0
        self.c, self.i, self.per = const, i, per
        self.slot = const % RING
        self.n = const + i * per if per else const
        self.round = const // RING + i * (per // RING) if per else const // RING

    def plus(self, k):
        return Blk(self.c + k, self.i, self.per)


class Sem:

    def __init__(self, nc, name, eng):
        self.h = nc.alloc_semaphore(name)
        eng.nop().then_inc(self.h, PRIME)
        self.n = PRIME

    def up(self, ins):
        ins.then_inc(self.h, 1)
        self.n += 1
        return self.n


def wt(eng, sem, value=None):
    eng.wait_ge(sem.h, sem.n if value is None else value)


class Core:

    def __init__(self, nc, io):
        self.nc, self.io = nc, io
        self.T, self.V, self.A, self.G, self.S = nc.tensor, nc.vector, nc.scalar, nc.gpsimd, nc.sync
        self.dummy = {}
        for name, eng in (("t", self.T), ("v", self.V), ("a", self.A), ("g", self.G)):
            self.dummy[id(eng)] = nc.alloc_semaphore("own_" + name)
        sb = self.sb
        self.ps = nc.alloc_psum_tensor("ps", [P, 8, 512], F32)
        off = (nc.sbuf_base + 31) // 32 * 32
        self.w_lo = nc.alloc_sbuf_tensor("w_lo", [P, RING, 1024], F32R)
        self.w_raw = nc.alloc_sbuf_tensor_at("w_raw", [P, RING, 1024], F32, offset=off)
        self.w_hi = sb("w_hi", [P, RING, 1024], F32R)
        self.x = sb("x", [P, KT, SEQ])
        self.y = sb("y", [P, KT, CTX])
        self.ident = sb("ident", [P, P])
        self.ones = sb("ones", [P, P])
        self.vec = sb("vec", [P, io["vec"].shape[1]])
        self.slope = sb("slope", [P, 32])
        self.c4 = sb("c4", [P, KT, 4], F32R)
        self.modraw = [sb(f"modraw{l}", [P, MT * 4]) for l in range(2)]
        self.modv = sb("modv", [P, 2, MT, 2])
        self.amul = sb("amul", [P, 2, KT, 2])
        self.r_tok = sb("r_tok", [P, 3, NT])
        self.RB1 = sb("RB1", [P, SEQ])
        self.RB = sb("RB", [P, ALLT])
        self.sq = sb("sq", [P, 2, ALLT])
        self.d_raw = [nc.alloc_semaphore(f"d_raw{i}") for i in range(RING)]
        self.s_hi = Sem(nc, "s_hi", self.A)
        self.s_lo = Sem(nc, "s_lo", self.G)
        self.s_used = Sem(nc, "s_used", self.T)
        mk = lambda n, e: Sem(nc, n, e)
        self.s_x = mk("s_x", self.V)
        self.s_sq = mk("s_sq", self.A)
        self.s_ssq = mk("s_ssq", self.T)
        self.s_std = mk("s_std", self.A)
        self.s_rstd = mk("s_rstd", self.V)
        self.s_hh = mk("s_hh", self.A)
        self.s_hl = mk("s_hl", self.V)
        self.s_acc = mk("s_acc", self.T)
        self.s_v = mk("s_v", self.V)
        self.s_a = mk("s_a", self.A)
        self.s_t = mk("s_t", self.T)
        self.d_const = nc.alloc_semaphore("d_const")
        self.prime_all()

    def prime_all(self):
        T, V, A = self.T, self.V, self.A
        names = [(p + n, e) for p in ("wa_", "da_")
                 for e, ns in ((T, "qk t pv ot vx"), (V, "ttr sink on olo ev vt"), (A, "exp pt e8 ohi em bs"))
                 for n in ns.split()]
        names += [(p + n, e) for p in ("f0", "f1") for e, ns in ((V, "s_gr s_ur s_m s_ml"), (A, "s_sl s_mh s_md"))
                  for n in ns.split()]
        names += [("f1s_mt", A), ("f1s_mx", T)]
        names += [(p + n, e) for p in ("j00_", "j04_", "j10_")
                  for e, ns in ((A, "q exp hi"), (V, "mx pt on g lo"), (T, "qk tr pv ot")) for n in ns.split()]
        self.primed = {n: Sem(self.nc, n, e) for n, e in names}

    def sem(self, name, eng):
        return self.primed[name]

    def sb(self, name, shape, dt=F32):
        return self.nc.alloc_sbuf_tensor(name, shape, dt)

    def absorb(self, eng):
        eng.sem_inc(self.dummy[id(eng)])

    def stream_loops(self):
        nb = len(PLAN)
        w = self.io["wstream"]

        def load(b):
            self.S.wait_ge(self.s_used.h, b.n + 1 + PRIME - RING)
            self.S.dma_start(self.w_raw[:, b.slot, :], w[b.n] if isinstance(b.n, int) else
                             w[bass.ds(b.n, 1)].rearrange("a p n -> (a p) n")).then_inc(self.d_raw[b.slot], 16)

        def split_lo(b):
            self.G.wait_ge(self.s_hi.h, b.n + 1 + PRIME)
            self.G.tensor_tensor(self.w_lo[:, b.slot, :], self.w_raw[:, b.slot, :],
                                 self.w_hi[:, b.slot, :].bitcast(F32), ALU.subtract).then_inc(self.s_lo.h, 1)

        for eng, f in ((self.S, load), (self.G, split_lo)):
            with eng.Fori(0, nb // RING, 1) as i:
                for u in range(RING):
                    f(Blk(u, i, RING))
            for n in range(nb // RING * RING, nb):
                f(Blk(n))

    def split_hi(self, b):
        b = b.plus(LEAD)
        if b.per == 0 and b.c >= len(PLAN):
            return
        self.A.wait_ge(self.d_raw[b.slot], (b.round + 1) * 16)
        self.A.activation(self.w_hi[:, b.slot, :], self.w_raw[:, b.slot, :], ACT.Copy).then_inc(self.s_hi.h, 1)

    def use(self, b):
        self.T.wait_ge(self.s_lo.h, b.n + 1 + PRIME)

    def used(self, ins):
        ins.then_inc(self.s_used.h, 1)

    def mm3(self, out, wh, wl, ah, al, start, stop, w_is_lhs=True):
        T = self.T
        if w_is_lhs:
            T.matmul(out, wh, ah, start=start, stop=False)
            T.matmul(out, wh, al, start=False, stop=False)
            return T.matmul(out, wl, ah, start=False, stop=stop)
        T.matmul(out, ah, wh, start=start, stop=False)
        T.matmul(out, ah, wl, start=False, stop=False)
        return T.matmul(out, al, wh, start=False, stop=stop)

    def feat_chunk(self, b, out, h, ks, last=KT - 1):
        wh = self.w_hi[:, b.slot, :].rearrange("p (k m) -> p k m", k=KT)
        wl = self.w_lo[:, b.slot, :].rearrange("p (k m) -> p k m", k=KT)
        for k in ks:
            ins = self.mm3(out, wh[:, k, :], wl[:, k, :], h[0][:, k, :], h[1][:, k, :], k == 0, k == last)
        return ins

    def mod_chunk(self, b, out, ks):
        wh = self.w_hi[:, b.slot, :].rearrange("p (k m) -> p k m", k=KT)
        wl = self.w_lo[:, b.slot, :].rearrange("p (k m) -> p k m", k=KT)
        for k in ks:
            self.T.matmul(out[:, 0:4], wh[:, k, :], self.c4[:, k, :], start=k == 0, stop=False)
            ins = self.T.matmul(out[:, 0:2], wl[:, k, :], self.c4[:, k, 0:2], start=False, stop=k == KT - 1)
        return ins

    def sum_squares(self, n, ntiles, cols, bank, tiles):
        wt(self.T, self.s_sq, self.s_sq_base + n + 1)
        for t in range(tiles):
            ins = self.T.matmul(self.ps[:, bank, cols + t:cols + t + 1], self.sq[:, n % 2, t * P:(t + 1) * P],
                                self.ones[:, 0:1], start=(n == 0 and t == 0),
                                stop=(n == ntiles - 1 and t == tiles - 1), skip_group_check=True)
        self.s_ssq.up(ins)

    def norm_begin(self):
        self.s_ssq_base, self.s_sq_base = self.s_ssq.n, self.s_sq.n

    def rstd(self, bank, tiles, width, row=0):
        A, V = self.A, self.V
        wt(A, self.s_ssq)
        self.s_std.up(A.activation(self.r_tok[:, row, 0:tiles], self.ps[:, bank, 0:tiles], ACT.Sqrt,
                                   bias=EPS, scale=1.0 / width))
        wt(V, self.s_std)
        V.reciprocal(self.r_tok[:, row, 0:tiles], self.r_tok[:, row, 0:tiles]).then_inc(self.s_rstd.h, 1)
        self.s_rstd.n += 1
        V.drain()

    def sum_rows(self, n, ntiles, groups):
        wt(self.T, self.s_sq, self.s_sq_base + n + 1)
        for bank, src in groups:
            ins = self.T.matmul(self.flat(bank, 0, src.shape[-1]), self.ones[:, :], src, start=n == 0,
                                stop=n == ntiles - 1)
        self.s_ssq.up(ins)

    def sum_over_partitions(self, groups):
        wt(self.T, self.s_v)
        for bank, src in groups:
            ins = self.T.matmul(self.flat(bank, 0, src.shape[-1]), self.ones[:, :], src, start=True, stop=True)
        self.s_ssq.up(ins)

    def rstd_rows(self, bank, n, dst, summed=None):
        wt(self.A, self.s_ssq, summed)
        self.s_std.up(self.A.activation(dst, self.flat(bank, 0, n), ACT.Sqrt, bias=EPS, scale=1.0 / D_MODEL))
        wt(self.V, self.s_std)
        self.s_rstd.up(self.V.reciprocal(dst, dst))
        self.V.drain()

    def flat(self, bank, start, n):
        return self.ps[:, :, :].rearrange("p b n -> p (b n)")[:, bank * 512 + start:bank * 512 + start + n]



def norm_tile(c, h, k, gain, order, sem_value, sem=None):
    A = c.A
    xin = order(c.x[:, k, :])
    A.wait_ge(sem if sem is not None else c.s_x.h, sem_value)
    c.s_hh.up(A.activation(h[0][:, k, :], xin, ACT.Copy, scale=gain[:, k:k + 1]))
    wt(A, c.s_ssq, c.s_ssq_base + k - 1)
    c.s_sq.up(A.activation(c.sq[:, k % 2, 0:SEQ], xin, ACT.Square))


def norm_tile_lo(c, h, k, gain, order):
    V = c.V
    wt(V, c.s_hh, c.s_hh_base + k + 1)
    c.s_hl.up(V.scalar_tensor_tensor(h[1][:, k, :], order(c.x[:, k, :]), gain[:, k:k + 1],
                                     h[0][:, k, :].bitcast(F32), ALU.mult, ALU.subtract))


def norm_finish(c):
    c.rstd_rows(0, SEQ, c.RB[:, 0:SEQ])
    wt(c.T, c.s_hl)


def context_sums(c):
    c.norm_begin()
    for k in range(KT):
        wt(c.A, c.s_ssq, c.s_ssq_base + k - 1)
        c.s_sq.up(c.A.activation(c.sq[:, k % 2, 0:CTX], c.y[:, k, :], ACT.Square))
        c.sum_rows(k, KT, [(2, c.sq[:, k % 2, 0:CTX])])


def final_norm(c, gain):
    V, A = c.V, c.A
    RB1, r12 = c.RB1[:, :], c.RB[:, 0:SEQ]
    wt(V, c.s_ssq)
    V.tensor_scalar(RB1, c.ps[:, 0, :], EPS / D_MODEL, EPS * EPS, ALU.mult, ALU.add)
    V.drain()
    c.s_rstd.up(V.scalar_tensor_tensor(r12, c.ps[:, 1, :], 1.0 / D_MODEL, RB1, ALU.mult, ALU.add))
    wt(A, c.s_rstd)
    c.s_std.up(A.activation(r12, r12, ACT.Sqrt))
    wt(V, c.s_std)
    c.s_std.up(A.activation(RB1, c.ps[:, 0, :], ACT.Sqrt, bias=EPS, scale=1.0 / D_MODEL))
    V.reciprocal(r12, r12)
    V.drain()

    def update():
        wt(V, c.s_std)
        V.reciprocal(RB1, RB1)
        V.drain()
        for k in range(KT):
            c.s_x.up(V.scalar_tensor_tensor(c.x[:, k, :], c.x[:, k, :], gain[:, k:k + 1], RB1, ALU.mult, ALU.mult))

    return update


def contract_out(c, n0, nb, act, order, nxt, ready):
    T, A, V = c.T, c.A, c.V
    ah, al = act

    def rows(b, m):
        return c.w_hi[:, b.slot, m * P:(m + 1) * P], c.w_lo[:, b.slot, m * P:(m + 1) * P]

    start_waits, first_banks, late_at, late_waits, last_waits = ready

    def outer(b, k, start):
        c.use(b)
        cols = bass.ds(k * SEQ, SEQ)
        for i, m in enumerate(first_banks if start else range(KT)):
            if start and i == late_at:
                for sem, v in late_waits:
                    wt(T, sem, v)
            wh, wl = rows(b, m)
            ins = c.mm3(c.ps[:, m, :], wh, wl, ah[:, cols], al[:, cols], start, False)
        c.used(ins)

    for sem, v in start_waits:
        wt(T, sem, v)
    held = 2 if nxt[0] is not None else 3
    head = min(4, nb - held)
    loops = (nb - held - head) // RING
    for k in range(head):
        outer(Blk(n0 + k), k, k == 0)
    if loops:
        with T.Fori(0, loops, 1) as i:
            for u in range(RING):
                outer(Blk(n0 + head + u, i, RING), i * RING + (head + u), False)
    for k in range(head + loops * RING, nb - held):
        outer(Blk(n0 + k), k, False)
    for k in range(head):
        c.split_hi(Blk(n0 + k))
    if loops:
        with A.Fori(0, loops, 1) as i:
            for u in range(RING):
                c.split_hi(Blk(n0 + head + u, i, RING))
    for k in range(head + loops * RING, nb - held):
        c.split_hi(Blk(n0 + k))
    last = [(Blk(n0 + k), k) for k in range(nb - held, nb)]
    h, gain, norder = nxt
    sqg = None if h is not None else c.ctx("sqg", [P, 2, SEQ])

    def sums(m):
        return [(0, c.sq[:, m % 2, 0:SEQ])]
    c.norm_begin()
    c.s_hh_base = c.s_hh.n
    x_base, acc_base = c.s_x.n, c.s_acc.n
    for sem, v in last_waits:
        wt(T, sem, v)
    for b, _ in last:
        c.use(b)
    for m in range(KT):
        for b, k in last:
            wh, wl = rows(b, m)
            cols = slice(k * SEQ, (k + 1) * SEQ)
            ins = c.mm3(c.ps[:, m, :], wh, wl, ah[:, cols], al[:, cols], False, k == nb - 1)
            if m == KT - 1:
                c.used(ins)
        if m < KT - 1:
            c.s_acc.up(ins)
        if m >= 2:
            if m == 2:
                wt(T, c.s_x, x_base + 2)
            if h is not None:
                c.sum_rows(m - 2, KT, sums(m - 2))
    c.acc_last = c.s_used.h, n0 + nb + PRIME
    if h is not None:
        c.sum_rows(KT - 2, KT, sums(KT - 2))
        c.sum_rows(KT - 1, KT, sums(KT - 1))
    c.split_hi(last[0][0])
    acc, add_base = (c.RB[:, 0:SEQ], c.RB1[:, :]), c.s_v.n

    def add_squares(j):
        wt(V, c.s_sq, c.s_sq_base + j + 1)
        wt(V, c.s_v, add_base + j - 1)
        V.tensor_tensor(acc[0], acc[0], c.sq[:, j % 2, 0:SEQ], ALU.add)
        c.s_v.up(V.tensor_tensor(acc[1], acc[1], sqg[:, j % 2, :], ALU.add))
    for m in range(KT):
        if m < KT - 1:
            wt(V, c.s_acc, acc_base + m + 1)
        else:
            V.wait_ge(*c.acc_last)
        c.s_x.up(V.tensor_tensor(order(c.x[:, m, :]), tokens(c.ps[:, m, :], order), order(c.x[:, m, :]), ALU.add))
        if h is not None:
            norm_tile(c, h, m, gain, norder, x_base + m + 1)
            if m >= 1:
                norm_tile_lo(c, h, m - 1, gain, norder)
        else:
            wt(A, c.s_x, x_base + m + 1)
            if m >= 3:
                wt(A, c.s_v, add_base + m - 2)
            to = acc if m == 0 else (c.sq[:, m % 2, 0:SEQ], sqg[:, m % 2, :])
            A.activation(to[0], c.x[:, m, :], ACT.Square)
            c.s_sq.up(A.activation(to[1], c.x[:, m, :], ACT.Square, scale=gain[:, m:m + 1]))
            if m >= 2:
                add_squares(m - 1)
    if h is not None:
        norm_tile_lo(c, h, KT - 1, gain, norder)
    else:
        add_squares(KT - 1)
        c.sum_over_partitions([(0, acc[0]), (1, acc[1])])
    for b, _ in last[1:]:
        c.split_hi(b)
    c.s_used.n = n0 + nb + PRIME


def natural(ap):
    return ap


def residues(ap):
    return ap.rearrange("p (j r) -> p r j", r=DIL)


def tokens(ap, order):
    return ap if order is natural else ap.rearrange("p (r j) -> p r j", r=DIL)


class Attention:

    def __init__(self, c, name, nbuf, s_bank, t_bank, width, sink=None):
        self.c, self.nbuf, self.s_bank, self.t_bank, self.width, self.sink = c, nbuf, s_bank, t_bank, width, sink
        mk = lambda n, e: c.sem(name + n, e)
        self.qk_, self.t_, self.pv_, self.ot_ = (mk(n, c.T) for n in ("qk", "t", "pv", "ot"))
        self.ttr_, self.sink_, self.on_, self.olo_ = (mk(n, c.V) for n in ("ttr", "sink", "on", "olo"))
        self.exp_, self.pt_, self.e8_, self.ohi_ = (mk(n, c.A) for n in ("exp", "pt", "e8", "ohi"))
        self.prob = [c.ctx(name + f"prob{i}", [P, width]) for i in range(2)]
        self.probT = [c.ctx(name + f"probT{i}", [P, width]) for i in range(2)]
        self.nm = [c.ctx(name + f"nm{i}", [P, 8]) for i in range(2)]
        self.den = [c.ctx(name + f"den{i}", [P, 8]) for i in range(2)]
        self.tmp8 = c.ctx(name + "tmp8", [P, 8])
        self.osb = c.ctx(name + "osb", [P, 512])

    def u(self, tile, s):
        return tile * 8 + (s + 1 + PRIME)

    def qk(self, tile, s, pieces, extra=()):
        T = self.c.T
        for sem, v in extra:
            wt(T, sem, v)
        wt(T, self.ttr_, self.u(tile, s - self.nbuf))
        for cols, q, k in pieces:
            ins = T.matmul(self.c.flat(self.s_bank + (s % self.nbuf), cols[0], cols[1]), q, k, start=True, stop=True)
        ins.then_inc(self.qk_.h, 1)

    def ttr(self, tile, s, par, n, bias):
        c = self.c
        V = c.V
        wt(V, self.qk_, self.u(tile, s))
        wt(V, self.t_, self.u(tile, s - 2))
        c.absorb(V)
        src = c.flat(self.s_bank + (s % self.nbuf), 0, n)
        V.tensor_tensor_reduce(self.prob[s % 2][:, 0:n], src, bias, -(HD ** -0.5), 3e38, ALU.add, ALU.min,
                               self.nm[par][:, s:s + 1]).then_inc(self.ttr_.h, 1)

    def exp(self, tile, s, par, n):
        A = self.c.A
        wt(A, self.ttr_, self.u(tile, s))
        p = self.prob[s % 2][:, 0:n]
        A.activation(p, p, ACT.Exp, bias=self.nm[par][:, s:s + 1], scale=-1.0,
                     accum_out=self.den[par][:, s:s + 1]).then_inc(self.exp_.h, 1)

    def transpose(self, tile, s, n):
        c = self.c
        wt(c.T, self.exp_, self.u(tile, s))
        wt(c.T, self.pt_, self.u(tile, s - self.nbuf))
        for k in range(n // P):
            ins = c.T.transpose(c.flat(self.t_bank + (s % self.nbuf), k * P, P),
                                self.prob[s % 2][:, k * P:(k + 1) * P], c.ident[:, :])
        ins.then_inc(self.t_.h, 1)

    def copy_pt(self, tile, s, n):
        c = self.c
        wt(c.A, self.t_, self.u(tile, s))
        wt(c.A, self.pv_, self.u(tile, s - 2))
        c.A.activation(self.probT[s % 2][:, 0:n], c.flat(self.t_bank + (s % self.nbuf), 0, n),
                       ACT.Copy).then_inc(self.pt_.h, 1)

    def pv(self, tile, s, vs, col):
        c = self.c
        wt(c.T, self.pt_, self.u(tile, s))
        if s == 0:
            wt(c.T, self.on_, tile + PRIME)
        for k, v in enumerate(vs):
            ins = c.T.matmul(c.flat(self.o_bank, col, HD), self.probT[s % 2][:, k * P:(k + 1) * P], v,
                             start=k == 0, stop=k == len(vs) - 1)
        ins.then_inc(self.pv_.h, 1)

    def norm_out(self, tile, par, perm):
        c = self.c
        V = c.V
        wt(V, self.exp_, self.u(tile, 7))
        c.absorb(V)
        if self.sink is not None:
            V.tensor_tensor(self.tmp8[:, :], self.nm[par][:, :], self.sink(tile), ALU.add).then_inc(self.sink_.h, 1)
            wt(V, self.e8_, tile + 1 + PRIME)
            V.tensor_tensor(self.den[par][:, :], self.den[par][:, :], self.tmp8[:, :], ALU.add)
            V.drain()
        V.reciprocal(self.den[par][:, :], self.den[par][:, :])
        V.drain()
        wt(V, self.pv_, self.u(tile, 7))
        wt(V, self.ot_, tile + PRIME)
        V.tensor_tensor(self.osb[:, :].rearrange("p (u d) -> p u d", u=8),
                        c.flat(self.o_bank, 0, 512).rearrange("p (u d) -> p u d", u=8),
                        perm(self.den[par][:, :]), ALU.mult).then_inc(self.on_.h, 1)

    def sink_exp(self, tile):
        c = self.c
        wt(c.A, self.sink_, tile + 1 + PRIME)
        c.A.activation(self.tmp8[:, :], self.tmp8[:, :], ACT.Exp).then_inc(self.e8_.h, 1)

    def turn(self, tile):
        c = self.c
        wt(c.T, self.on_, tile + 1 + PRIME)
        wt(c.T, self.olo_, tile + PRIME)
        for b in range(4):
            ins = c.T.transpose(c.flat(self.ot_bank, b * P, P), self.osb[:, b * P:(b + 1) * P], c.ident[:, :])
        ins.then_inc(self.ot_.h, 1)

    def out_hi(self, tile, dst):
        c = self.c
        wt(c.A, self.ot_, tile + 1 + PRIME)
        c.absorb(c.A)
        c.A.activation(dst[:, bass.ds(tile * 512, 512)], c.flat(self.ot_bank, 0, 512),
                       ACT.Copy).then_inc(self.ohi_.h, 1)

    def out_lo(self, tile, dst, hi):
        c = self.c
        wt(c.V, self.ohi_, tile + 1 + PRIME)
        cols = bass.ds(tile * 512, 512)
        c.V.tensor_tensor(dst[:, cols], c.flat(self.ot_bank, 0, 512), hi[:, cols].bitcast(F32),
                          ALU.subtract).then_inc(self.olo_.h, 1)

    def finish(self, tiles):
        for s in (self.qk_, self.t_, self.pv_, self.ttr_, self.exp_, self.pt_):
            s.n = PRIME + 8 * tiles
        for s in (self.ot_, self.on_, self.olo_, self.ohi_):
            s.n = PRIME + tiles


def turn_values(c, vt, vx, vT, bank, count):
    wt(c.T, vt, count)
    for t in range(TT):
        ins = c.T.transpose(c.ps[:, bank, t * P:(t + 1) * P], vT[:, t * P:(t + 1) * P], c.ident[:, :])
    ins.then_inc(vx.h, 1)


def window_attention(c, n0, h, ah, al):
    nc, T, V, A = c.nc, c.T, c.V, c.A
    dist = c.ctx("dist0", [P, 3 * P])
    bias = [[c.ctx(f"bias0_{i}{e}", [P, 3 * P]) for e in range(2)] for i in range(2)]
    kT = c.ctx("kT", [P, SEQ])
    vS = c.ctx("vS", [P, TT, P])
    qT = [c.ctx(f"qT{i}", [P, SEQ]) for i in range(2)]
    sinks = c.ctx("sinks", [P, 64])
    at = Attention(c, "wa_", 2, 2, 4, 3 * P, sink=lambda tile: sinks[:, bass.ds(tile * 8, 8)])
    at.o_bank, at.ot_bank = 0, 1
    pb = (6, 7)
    ev = c.sem("wa_ev", V)
    em = c.sem("wa_em", A)
    bs = c.sem("wa_bs", A)
    vT = c.ctx("vT", [P, SEQ])
    vt = c.sem("wa_vt", V)
    vx = c.sem("wa_vx", T)
    d_c = nc.alloc_semaphore("d_wa")
    c.A.dma_start(dist[:, :], c.io["dist0"]).then_inc(d_c, 16)
    c.A.dma_start(sinks[:, :], c.io["sinks"]).then_inc(d_c, 16)
    A.wait_ge(d_c, 32)
    V.wait_ge(d_c, 32)

    def keys(b):
        lo, hi = max(b - 1, 0), min(b + 1, TT - 1)
        return lo, hi - lo + 1

    def unit(s):
        b, e = s // 2, s % 2
        lo, nk = keys(b)
        return b, e, lo, nk, nk * P

    def chunk(b, m, cpos, ks):
        if ks[0] == 0:
            c.use(b)
            if cpos < 2:
                wt(T, em, m * 2 + (PRIME - 1 + cpos))
            elif cpos < 8:
                wt(T, ev, m * 6 + (PRIME + cpos - 1))
        bank = pb[cpos % 2]
        if cpos >= 6:
            ins = c.mod_chunk(b, c.ps[:, bank, :], ks)
        else:
            ins = c.feat_chunk(b, c.ps[:, bank, :], h, ks)
        if ks[-1] == KT - 1:
            c.used(ins)

    def blocks(m):
        return [Blk(n0 + u, m, 8) for u in range(8)]

    with T.Fori(0, 2, 1) as m:
        bl = blocks(m)
        for cpos in range(3):
            chunk(bl[cpos], m, cpos, range(KT))
        turn_values(c, vt, vx, vT, pb[1], m + (1 + PRIME))
        for i in range(4):
            tile = m * 4 + i
            for s in range(8):
                if i < 3:
                    chunk(bl[3 + i], m, 3 + i, [s])
                else:
                    chunk(bl[6 + s // 4], m, 6 + s // 4, [2 * (s % 4), 2 * (s % 4) + 1])
                b, e, lo, nk, n = unit(s)
                rows = slice(HD * e, HD * e + HD)
                at.qk(tile, s, [((0, n), qT[i % 2][rows, b * P:(b + 1) * P], kT[rows, lo * P:lo * P + n])],
                      extra=[(ev, m * 6 + (PRIME + 3 + i))] if s == 0 else ())
                if s >= 1:
                    at.transpose(tile, s - 1, unit(s - 1)[4])
                if s >= 2:
                    _, e2, lo2, nk2, _ = unit(s - 2)
                    at.pv(tile, s - 2, [vS[:, lo2 + k, HD * e2:HD * e2 + HD] for k in range(nk2)], (s - 2) * HD)
                if s == 3 and i > 0:
                    at.turn(m * 4 + (i - 1))
            at.transpose(tile, 7, unit(7)[4])
            for s in (6, 7):
                _, e2, lo2, nk2, _ = unit(s)
                at.pv(tile, s, [vS[:, lo2 + k, HD * e2:HD * e2 + HD] for k in range(nk2)], s * HD)
        at.turn(m * 4 + 3)

    with V.Fori(0, 2, 1) as m:
        def evac(cpos):
            V.wait_ge(c.s_used.h, m * 8 + (n0 + cpos + 1 + PRIME))
            bank = pb[cpos % 2]
            if cpos == 0:
                ins = V.tensor_tensor(kT[:, :], c.ps[:, bank, :], c.RB[:, 0:SEQ], ALU.mult)
            elif cpos == 1:
                V.tensor_tensor(vT[:, :], c.ps[:, bank, :], c.RB[:, 0:SEQ], ALU.mult).then_inc(vt.h, 1)
                wt(V, vx, m + (1 + PRIME))
                ins = V.tensor_copy(vS[:, :, :].rearrange("p t n -> p (t n)"), c.ps[:, bank, :])
            else:
                ins = V.tensor_tensor(qT[cpos % 2][:, :], c.ps[:, bank, :], c.RB[:, 0:SEQ], ALU.mult)
            ins.then_inc(ev.h, 1)
        for cpos in range(3):
            evac(cpos)
        for i in range(4):
            tile = m * 4 + i
            for s in range(8):
                b, e, lo, nk, n = unit(s)
                if s == 0:
                    wt(V, bs, m * 4 + (i + 1 + PRIME))
                off = P * (lo - b + 1)
                at.ttr(tile, s, i % 2, n, bias[i % 2][e][:, off:off + n])
                if s == 6 and i > 0:
                    at.out_lo(m * 4 + (i - 1), al, ah)
            if i < 3:
                evac(3 + i)
            at.norm_out(tile, i % 2, lambda r: r.unsqueeze(2).broadcast_to([P, 8, HD]))
        at.out_lo(m * 4 + 3, al, ah)

    with A.Fori(0, 2, 1) as m:
        bl = blocks(m)

        def make_bias(i):
            wt(A, at.ttr_, at.u(m * 4 + i, -9))
            c.absorb(A)
            for e in range(2):
                ins = A.activation(bias[i % 2][e][:, :], dist[:, :], ACT.Copy,
                                   scale=c.slope[:, bass.ds((m * 4 + i) * 2 + e, 1)])
            ins.then_inc(bs.h, 1)
        for cpos in range(3):
            c.split_hi(bl[cpos])
        make_bias(0)
        for i in range(4):
            tile = m * 4 + i
            if i < 3:
                c.split_hi(bl[3 + i])
                make_bias(i + 1)
            for s in range(8):
                at.exp(tile, s, i % 2, unit(s)[4])
                if s >= 1:
                    at.copy_pt(tile, s - 1, unit(s - 1)[4])
                if s == 5 and i > 0:
                    at.out_hi(m * 4 + (i - 1), ah)
                if i == 3 and s in (3, 7):
                    c.split_hi(bl[6 + s // 4])
            at.copy_pt(tile, 7, unit(7)[4])
            at.sink_exp(tile)
        for q in range(2):
            A.wait_ge(c.s_used.h, m * 8 + (n0 + 6 + q + 1 + PRIME))
            c.absorb(A)
            A.activation(c.modraw[1][:, bass.ds((m * 2 + q) * 4, 4)], c.ps[:, pb[q], 0:4], ACT.Copy).then_inc(em.h, 1)
        at.out_hi(m * 4 + 3, ah)
    at.finish(8)
    ev.n, em.n, bs.n = PRIME + 12, PRIME + 4, PRIME + 8
    olo = at.olo_
    return [(ev, ev.n), (em, em.n), (olo, olo.n - 1)], (2, 3, 4, 5, 6, 7, 0, 1), 6, [(olo, olo.n)], []


def dilated_attention(c, n0, h, ah, al):
    nc, T, V, A = c.nc, c.T, c.V, c.A
    W1 = SEQ
    NK = W1 + 2 * P
    dist = c.ctx("dist1", [P, DIL * NK])
    bias = [c.ctx(f"bias1_{i}", [P, NK]) for i in range(2)]
    qT = [[c.ctx(f"dqT{i}{g}", [P, SEQ]) for g in range(3)] for i in range(2)]
    kT = [[c.ctx(f"dkT{i}{g}", [P, SEQ]) for g in range(3)] for i in range(2)]
    vS = [[c.ctx(f"dvS{i}{g}", [P, DIL, P]) for g in range(3)] for i in range(2)]
    at = Attention(c, "da_", 1, 2, 4, NK)
    at.o_bank, at.ot_bank = 0, 1
    pb = (6, 7)
    vT = c.ctx("dvT", [P, SEQ])
    ev = c.sem("da_ev", V)
    vt = c.sem("da_vt", V)
    vx = c.sem("da_vx", T)
    em = c.sem("da_em", A)
    bs = c.sem("da_bs", A)
    d_c = nc.alloc_semaphore("d_da")
    A.wait_ge(c.s_x.h, c.s_x.n)
    c.A.dma_start(dist[:, :], c.io["dist1"]).then_inc(d_c, 16)
    A.wait_ge(d_c, 16)

    def tokens_of(s):
        e, r = s // 4, s % 4
        return e, r, slice(HD * e, HD * e + HD)

    def pe(j, par, bl, proj, attn):
        tile = j - 1
        q, k, v = qT[1 - par], kT[1 - par], vS[1 - par]
        for s in range(12):
            if proj:
                b, bank = bl[s], pb[s % 2]
                c.use(b)
                g2, what2 = (s - 2) // 4, (s - 2) % 4
                if what2 == 3:
                    wt(T, em, j * 3 + (PRIME + g2 + 1))
                else:
                    wt(T, ev, j * 9 + (PRIME + g2 * 3 + what2 + 1))
                if s % 4 == 3:
                    ins = c.mod_chunk(b, c.ps[:, bank, :], range(KT))
                else:
                    ins = c.feat_chunk(b, c.ps[:, bank, :], h, range(KT))
                c.used(ins)
                if s % 4 == 3:
                    turn_values(c, vt, vx, vT, pb[(s - 1) % 2], j * 3 + (s // 4 + 1 + PRIME))
            if not attn:
                continue
            if s < 8:
                e, r, rows = tokens_of(s)
                own = slice(r * P, (r + 1) * P)
                at.qk(tile, s, [((0, W1), q[0][rows, own], k[0][rows, :]),
                                ((W1, P), q[1][rows, own], k[1][rows, own]),
                                ((W1 + P, P), q[2][rows, own], k[2][rows, own])],
                      extra=[(ev, tile * 9 + (9 + PRIME))] if s == 0 else ())
            if 1 <= s <= 8:
                at.transpose(tile, s - 1, NK)
            if 2 <= s <= 9:
                e, r, _ = tokens_of(s - 2)
                cols = slice(HD * e, HD * e + HD)
                at.pv(tile, s - 2, [v[0][:, t, cols] for t in range(DIL)] + [v[1][:, r, cols], v[2][:, r, cols]],
                      (2 * r + e) * HD)
            if s == 11:
                at.turn(tile)

    def ve(j, par, proj, attn):
        tile = j - 1
        for s in range(12):
            if proj and s % 4 == 3:
                wt(V, vx, j * 3 + (s // 4 + 1 + PRIME))
                V.tensor_copy(vS[par][s // 4][:, :, :].rearrange("p t n -> p (t n)"),
                              c.ps[:, pb[(s - 1) % 2], :]).then_inc(ev.h, 1)
            elif proj:
                V.wait_ge(c.s_used.h, j * 12 + (n0 + s + 1 + PRIME))
                g, what = s // 4, s % 4
                src = c.ps[:, pb[s % 2], :]
                if what == 2:
                    V.tensor_tensor(vT[:, :], src, c.RB[:, 0:SEQ], ALU.mult).then_inc(vt.h, 1)
                else:
                    V.tensor_tensor((qT, kT)[what][par][g][:, :], src, c.RB[:, 0:SEQ], ALU.mult).then_inc(ev.h, 1)
            if attn and s < 8:
                e, r, _ = tokens_of(s)
                wt(V, bs, at.u(tile, s))
                at.ttr(tile, s, 1 - par, NK, bias[s % 2][:, :])
            if attn and s == 10:
                at.norm_out(tile, 1 - par, lambda d: d.rearrange("p (e r) -> p r e", e=2).unsqueeze(3)
                            .broadcast_to([P, 4, 2, HD]))
        if attn:
            at.out_lo(tile, al, ah)

    def ac(j, par, bl, proj, attn):
        tile = j - 1

        def make_bias(s):
            e, r, _ = tokens_of(s)
            wt(A, at.ttr_, at.u(tile, s - 2))
            c.absorb(A)
            A.activation(bias[s % 2][:, :], dist[:, r * NK:(r + 1) * NK], ACT.Copy,
                         scale=c.slope[:, bass.ds(tile * 2 + (16 + e), 1)]).then_inc(bs.h, 1)
        for s in range(12):
            if proj:
                c.split_hi(bl[s])
            if proj and s % 4 == 3:
                A.wait_ge(c.s_used.h, j * 12 + (n0 + s + 1 + PRIME))
                c.absorb(A)
                A.activation(c.modraw[0][:, bass.ds((j * 3 + s // 4) * 4, 4)], c.ps[:, pb[s % 2], 0:4],
                             ACT.Copy).then_inc(em.h, 1)
            if attn and s == 0:
                make_bias(0)
                make_bias(1)
            if attn and s < 8:
                at.exp(tile, s, 1 - par, NK)
            if attn and s < 6:
                make_bias(s + 2)
            if attn and 1 <= s <= 8:
                at.copy_pt(tile, s - 1, NK)
        if attn:
            at.out_hi(tile, ah)

    for eng, part in ((T, pe),
                      (V, lambda j, par, bl, proj, attn: ve(j, par, proj, attn)),
                      (A, ac)):
        part(0, 0, [Blk(n0 + u) for u in range(12)], True, False)
        with eng.Fori(0, 3, 1) as i:
            for q in range(2):
                part(i * 2 + (q + 1), (q + 1) % 2, [Blk(n0 + 12 * (q + 1) + u, i, 24) for u in range(12)],
                     True, True)
        part(7, 1, [Blk(n0 + 84 + u) for u in range(12)], True, True)
        part(8, 0, None, False, True)
    at.finish(8)
    ev.n, em.n, bs.n = PRIME + 72, PRIME + 24, PRIME + 64
    olo = at.olo_
    return [(ev, ev.n), (em, em.n), (olo, olo.n - 1)], (2, 3, 4, 5, 6, 7, 0, 1), 6, [(olo, olo.n)], []


def swiglu(c, n0, name, h, mh, ml, mod):
    nc, T, V, A = c.nc, c.T, c.V, c.A
    per = 3 if mod else 2
    pairs = 4 * MROWS if mod else FT
    pos = 1 if mod else 0
    unroll = 4 if mod else 2
    gr = [c.ctx(name + f"gr{i}", [P, SEQ]) for i in range(2)]
    ur = [c.ctx(name + f"ur{i}", [P, SEQ]) for i in range(2)]
    s_gr, s_ur, s_m = (c.sem(name + x, V) for x in ("s_gr", "s_ur", "s_m"))
    s_sl, s_mh, s_md = (c.sem(name + x, A) for x in ("s_sl", "s_mh", "s_md"))
    s_ml = c.sem(name + "s_ml", V)

    if mod:
        mrow = c.ctx(name + "mrow", [4, SEQ])
        s_mt, s_mx = c.sem(name + "s_mt", A), c.sem(name + "s_mx", T)

    def pe(j, q, b, withmod, group):
        g_bank, u_bank = 2 + 2 * (q % 2), 3 + 2 * (q % 2)
        if withmod:
            c.use(b[0])
            for k in range(2):
                kk, cols = 2 * q + k, slice(k * SEQ, (k + 1) * SEQ)
                T.matmul(c.ps[0:4, 6, :], c.c4[:, kk, :], c.w_hi[:, b[0].slot, cols], start=kk == 0, stop=False)
                ins = T.matmul(c.ps[0:2, 6, :], c.c4[:, kk, 0:2], c.w_lo[:, b[0].slot, cols], start=False,
                               stop=kk == KT - 1)
            c.used(ins)
            b = b[1:]
        c.use(b[0])
        wt(T, s_gr, j + (PRIME - 1))
        c.used(c.feat_chunk(b[0], c.ps[:, g_bank, :], h, range(KT)))
        c.use(b[1])
        wt(T, s_ur, j + (PRIME - 1))
        c.used(c.feat_chunk(b[1], c.ps[:, u_bank, :], h, range(KT)))
        if withmod and q == 3:
            wt(T, s_mt, group + (1 + PRIME))
            wt(T, s_md, group + PRIME)
            c.absorb(T)
            for t in range(4):
                ins = T.transpose(c.ps[:, 7, 4 * t:4 * t + 4], mrow[:, t * P:(t + 1) * P], c.ident[0:4, 0:4])
            ins.then_inc(s_mx.h, 1)

    def ve(j, q, used, withmod):
        i = q % 2
        used = used + (pos if withmod else 0)
        V.wait_ge(c.s_used.h, used + 1)
        wt(V, s_m, j + (PRIME - 1))
        V.tensor_tensor(gr[i][:, :], c.ps[:, 2 + 2 * i, :], c.RB[:, 0:SEQ], ALU.mult).then_inc(s_gr.h, 1)
        V.wait_ge(c.s_used.h, used + 2)
        V.tensor_tensor(ur[i][:, :], c.ps[:, 3 + 2 * i, :], c.RB[:, 0:SEQ], ALU.mult).then_inc(s_ur.h, 1)
        wt(V, s_sl, j + (PRIME + 1))
        wt(V, s_ur, j + (PRIME + 1))
        V.tensor_tensor(ur[i][:, :], gr[i][:, :], ur[i][:, :], ALU.mult).then_inc(s_m.h, 1)
        wt(V, s_mh, j + (PRIME + 1))
        cols = bass.ds(j * SEQ, SEQ)
        V.tensor_tensor(ml[:, cols], ur[i][:, :], mh[:, cols].bitcast(F32), ALU.subtract).then_inc(s_ml.h, 1)

    def ac(j, q, b, used, withmod, group):
        i = q % 2
        c.split_hi(b[0])
        if withmod and q == 3:
            A.wait_ge(c.s_used.h, used + 1)
            A.activation(mrow[:, :], c.ps[0:4, 6, :], ACT.Copy).then_inc(s_mt.h, 1)
        if withmod:
            c.split_hi(b[1])
            b = b[1:]
        wt(A, s_gr, j + (PRIME + 1))
        A.activation(gr[i][:, :], gr[i][:, :], ACT.Silu).then_inc(s_sl.h, 1)
        c.split_hi(b[1])
        wt(A, s_m, j + (PRIME + 1))
        c.absorb(A)
        A.activation(mh[:, bass.ds(j * SEQ, SEQ)], ur[i][:, :], ACT.Copy).then_inc(s_mh.h, 1)
        if withmod and q == 3:
            wt(A, s_mx, group + (1 + PRIME))
            c.absorb(A)
            A.activation(c.modraw[1][:, bass.ds(group * 16 + 4 * (MT - 4 * MROWS), 16)], c.ps[:, 7, 0:16],
                         ACT.Copy).then_inc(s_md.h, 1)

    def blks(q, i=0, it=0):
        return [Blk(n0 + per * q + x, i, it) for x in range(per)]

    for eng, part in ((T, lambda j, q, b, u, m, g: pe(j, q, b, m, g)), (V, lambda j, q, b, u, m, g: ve(j, q, u, m)),
                      (A, ac)):
        with eng.Fori(0, pairs // unroll, 1) as i:
            for q in range(unroll):
                part(i * unroll + q, q, blks(q, i, per * unroll), i * (per * unroll) + (n0 + per * q + PRIME), mod, i)
        for j in range(pairs, FT):
            first = n0 + per * pairs + 2 * (j - pairs)
            part(j, j, [Blk(first), Blk(first + 1)], first + PRIME, False, 0)
    for s in (s_gr, s_ur, s_m, s_sl, s_mh, s_ml):
        s.n = PRIME + FT
    s_md.n = PRIME + (MROWS if mod else 0)
    return ([(s_ml, s_ml.n - 2), (s_md, s_md.n)], (0, 1, 6, 7, 2, 3, 4, 5), 4, [(s_gr, s_gr.n), (s_ur, s_ur.n)],
            [(s_ml, s_ml.n)])



def modulation(c, l, V_):
    V, vec, modv, amul = c.V, c.vec, c.modv, c.amul[:, l, :, :]
    mr = c.modraw[l][:, :].rearrange("p (t k) -> p t k", k=4)
    V.tensor_tensor(modv[:, l, :, :], mr[:, :, 0:2], mr[:, :, 2:4], ALU.add)
    V.drain()
    V.tensor_tensor(modv[:, l, :, :], modv[:, l, :, :],
                    vec[:, V_["b_mod"] + l * MT:V_["b_mod"] + (l + 1) * MT].unsqueeze(2).broadcast_to([P, MT, 2]),
                    ALU.add)
    V.drain()
    V.tensor_scalar(amul, modv[:, l, KT:2 * KT, :], 1.0, None, ALU.add)
    V.drain()
    V.tensor_tensor(amul, amul, vec[:, V_["norm_g"] + l * KT:V_["norm_g"] + (l + 1) * KT].unsqueeze(2)
                    .broadcast_to([P, KT, 2]), ALU.mult)
    V.drain()
    if l == 0:
        V.tensor_tensor(amul[:, :, 0], amul[:, :, 0], vec[:, V_["norm_final"]:V_["norm_final"] + KT], ALU.mult)
        V.drain()

def block_two_layer(c, l, n0, V_, update):
    nc, T, V, A, io = c.nc, c.T, c.V, c.A, c.io
    both = l == 0
    nt_q = NT if both else TT
    nq = nt_q * P
    vec, modv, ps = c.vec, c.modv, c.ps
    L = f"l{l}_"

    def up(sem, ins):
        return sem.up(ins)

    outer = c.scope()
    h_hi = c.ctx(L + "h_hi", [P, KT, ALLT], F32R)
    h_lo = c.ctx(L + "h_lo", [P, KT, ALLT], F32R)
    h_end = c.offset
    tok = c.scope()
    ag = c.ctx(L + "ag", [P, 4, ALLT])
    spare = c.offset
    cq = c.ctx(L + "cq", [P, 2, ALLT])
    ckv = c.ctx(L + "ckv", [P, ALLT])
    kro = c.ctx(L + "kro", [P, NT, A_ROPE])
    stage1 = c.scope()
    tmp = c.ctx(L + "tmp", [P, 3, ALLT])
    sqv = nc.alloc_sbuf_tensor_at(L + "sqv", [P, NT, 4, HD], F32, offset=stage1)
    dft = [c.ctx(L + f"dft{a}", [P, TT, SEQ]) for a in range(2)]
    dfc = [c.ctx(L + f"dfc{a}", [P, 2, CTX]) for a in range(2)]
    wfm = c.ctx(L + "wfm", [P, 2, 256])
    wsT = c.ctx(L + "wsT", [P, 4, P])
    dfd = c.ctx(L + "dfd", [P, 2, P])
    bsb = c.ctx(L + "bsb", [P, 2, P])
    glg = c.ctx(L + "glg", [P, HD])
    st = c.ctx(L + "st", [P, 2, NT * 4])
    after = c.scope()
    c.close(stage1 + (2 * A_HEADS * ALLT + NT * A_HEADS * A_V) * 4)
    gains = c.ctx(L + "gains", [P, 2, A_QK])
    gcol = c.ctx(L + "gcol", [P, 2])
    rope = c.ctx(L + "rope", [P, 2, TT, A_ROPE])
    rtab = c.ctx(L + "rtab", [P, 2, 2, TT, A_ROPE])
    small = c.ctx(L + "small", [P, 2, A_HEADS])
    rtmp = c.ctx(L + "rtmp", [P, A_HEADS, A_ROPE])
    c.close(after)
    d_s1, d_s2 = nc.alloc_semaphore(L + "d_s1"), nc.alloc_semaphore(L + "d_s2")
    loads2 = [(glg[:, :], io["glg"][l]), (bsb[:, :, :].rearrange("p a n -> p (a n)"), io["gbs"][l]),
              (gains[:, :, :].rearrange("p a n -> p (a n)"), io["qkg"][l]), (gcol[0:A_NOPE, :], io["qkgT"][l]),
              (rope[:, :, :, :].rearrange("p a b n -> p (a b n)"), io["rope"])]
    loads = [(dft[a][:, :, :], io["dft"][:, a]) for a in range(2)]
    loads += [(dfd[:, :, :].rearrange("p a n -> p (a n)"), io["dfd"]),
              (wfm[:, :, :].rearrange("p a n -> p (a n)"), io["wfmix"][l]),
              (wsT[:, :, :].rearrange("p a n -> p (a n)"), io["gws"][l])]
    if both:
        loads += [(dfc[a][:, :, :], io["dfc"][:, a]) for a in range(2)]
    for sem, some in ((d_s2, loads2), (d_s1, loads)):
        for d, src in some:
            A.dma_start(d, src).then_inc(sem, 16)
    hh0, hv0, hl0 = c.s_hh.n, c.s_v.n, c.s_hl.n
    parts = ((0, SEQ, 0, c.x), (SEQ, CTX, 1, c.y))

    def h_lo_of(k):
        wt(V, c.s_hh, hh0 + k + 1)
        for lo, n, cond, _ in parts:
            ins = V.scalar_tensor_tensor(h_lo[:, k, lo:lo + n], tmp[:, k % 3, lo:lo + n],
                                         modv[:, l, k, cond:cond + 1], h_hi[:, k, lo:lo + n].bitcast(F32),
                                         ALU.add, ALU.subtract)
        up(c.s_hl, ins)

    for k in range(KT):
        if k >= 3:
            wt(V, c.s_hl, hl0 + k - 2)
        for lo, n, cond, src in parts:
            ins = V.scalar_tensor_tensor(tmp[:, k % 3, lo:lo + n], src[:, k, :], c.amul[:, l, k, cond:cond + 1],
                                         c.RB[:, lo:lo + n], ALU.mult, ALU.mult)
        up(c.s_v, ins)
        wt(A, c.s_v, hv0 + k + 1)
        for lo, n, cond, _ in parts:
            ins = A.activation(h_hi[:, k, lo:lo + n], tmp[:, k % 3, lo:lo + n], ACT.Identity,
                               bias=modv[:, l, k, cond:cond + 1])
        up(c.s_hh, ins)
        if k:
            h_lo_of(k - 1)
    h_lo_of(KT - 1)
    if update:
        update()

    n = n0
    tm = c.ctx(L + "tm", [P, NT, 512])
    for q in range(4):
        b = Blk(n + q)
        c.use(b)
        wh = c.w_hi[:, b.slot, :].rearrange("p (k n) -> p k n", k=2)
        wl = c.w_lo[:, b.slot, :].rearrange("p (k n) -> p k n", k=2)
        for k in range(2):
            kk = 2 * q + k
            wt(T, c.s_hl, hl0 + kk + 1)
            for t in range(nt_q):
                ts = slice(t * P, (t + 1) * P)
                ins = c.mm3(ps[:, t, :], wh[:, k, :], wl[:, k, :], h_hi[:, kk, ts], h_lo[:, kk, ts],
                            kk == 0, kk == KT - 1, w_is_lhs=False)
        c.used(ins)
        c.split_hi(b)
    n += 4
    for t in range(nt_q):
        A.wait_ge(c.s_used.h, n + PRIME)
        up(c.s_a, A.activation(tm[:, t, :], ps[:, t, :], ACT.Copy))
    tm_done = c.s_a.n

    b = Blk(n)
    c.use(b)
    for lo, nn in ((0, SEQ), (SEQ, CTX)):
        for k in range(KT):
            ks = slice(k * A_ROPE, (k + 1) * A_ROPE)
            ins = c.mm3(c.flat(6, lo, nn)[0:A_ROPE], c.w_hi[:, b.slot, ks], c.w_lo[:, b.slot, ks],
                        h_hi[:, k, lo:lo + nn], h_lo[:, k, lo:lo + nn], k == 0, k == KT - 1)
    c.used(ins)
    c.split_hi(b)
    A.wait_ge(c.s_used.h, n + 1 + PRIME)
    krT = c.sq[0:A_ROPE, 1, :]
    up(c.s_a, A.activation(krT, c.flat(6, 0, ALLT)[0:A_ROPE], ACT.Copy))
    kro_done = c.s_a.n
    n += 1

    def turn_rope():
        wt(T, c.s_a, kro_done)
        for t in range(NT):
            ins = T.transpose(ps[:, 0, t * A_ROPE:(t + 1) * A_ROPE], krT[:, t * P:(t + 1) * P],
                              c.ident[0:A_ROPE, 0:A_ROPE])
        up(c.s_t, ins)
        wt(A, c.s_t)
        up(c.s_a, A.activation(kro[:, :, :].rearrange("p t d -> p (t d)"), ps[:, 0, 0:NT * A_ROPE], ACT.Copy))

    gv = tm[:, 0:nt_q, 256:512].rearrange("p t (h d) -> p t h d", h=4)
    ng = nt_q * 4

    def groups(ap):
        return ap.rearrange("p (t h) -> p t h", h=4)

    V.wait_ge(c.s_a.h, tm_done)
    V.tensor_reduce(groups(st[:, 0, 0:ng]), gv, AX.X, ALU.add)
    V.drain()
    V.tensor_scalar(st[:, 0, 0:ng], st[:, 0, 0:ng], 1.0 / HD, None, ALU.mult)
    V.drain()
    for t in range(nt_q):
        g4 = gv[:, t]
        V.tensor_tensor(g4, g4, st[:, 0, 4 * t:4 * t + 4].unsqueeze(2).broadcast_to([P, 4, HD]), ALU.subtract)
    V.drain()
    for t in range(nt_q):
        V.tensor_tensor(sqv[:, t], gv[:, t], gv[:, t], ALU.mult)
    V.drain()
    up(c.s_v, V.tensor_reduce(groups(st[:, 1, 0:ng]), sqv[:, 0:nt_q], AX.X, ALU.add))
    gate_sum = c.s_v.n

    def gate_norm():
        wt(A, c.s_v, gate_sum)
        up(c.s_a, A.activation(st[:, 1, 0:ng], st[:, 1, 0:ng], ACT.Sqrt, bias=EPS, scale=1.0 / HD))
        wt(V, c.s_a)
        V.reciprocal(st[:, 1, 0:ng], st[:, 1, 0:ng])
        V.drain()
        for t in range(nt_q):
            g4 = gv[:, t]
            V.tensor_tensor(g4, g4, st[:, 1, 4 * t:4 * t + 4].unsqueeze(2).broadcast_to([P, 4, HD]), ALU.mult)
        V.drain()
        V.wait_ge(d_s2, 16 * len(loads2))
        for t in range(nt_q):
            g4 = gv[:, t]
            ins = V.tensor_tensor(g4, g4, glg[:, :].unsqueeze(1).broadcast_to([P, 4, HD]), ALU.mult)
        up(c.s_v, ins)
        done = c.s_v.n
        V.tensor_scalar(gains[:, 0, :], gains[:, 0, :], A_QK ** -0.5, None, ALU.mult)
        V.tensor_scalar(gcol[0:A_NOPE, 0:1], gcol[0:A_NOPE, 0:1], A_QK ** -0.5, None, ALU.mult)
        V.memset(gcol[A_NOPE:A_QK, :], 1.0)
        V.drain()
        for w_ in range(2):
            V.tensor_tensor(rtab[:, w_, 0], rope[:, 0], gains[:, w_, A_NOPE:A_QK].unsqueeze(1)
                            .broadcast_to([P, TT, A_ROPE]), ALU.mult)
            for q in range(4):
                d0, g0 = 8 * q, A_NOPE + 8 * (q ^ 1)
                ins = V.tensor_tensor(rtab[:, w_, 1, :, d0:d0 + 8], rope[:, 1, :, d0:d0 + 8],
                                      gains[:, w_, g0:g0 + 8].unsqueeze(1).broadcast_to([P, TT, 8]), ALU.mult)
        up(c.s_v, ins)
        return done

    gu = c.ctx(L + "gu", [P, 2, ALLT])
    fg = c.ctx(L + "fg", [P, 2, ALLT])
    rows = (("cq", 0), ("cq", 1), ("ckv", 0), ("gg", 0), ("gg", 1), ("gu", 0), ("gu", 1), ("fg", 0), ("fg", 1),
            ("ag", 0), ("ag", 1), ("ag", 2), ("ag", 3))
    evac, pending = [], []
    for i, (what, kk) in enumerate(rows):
        b = Blk(n + i)
        bank = (4, 6)[i % 2]
        if i == 3:
            gate_done = gate_norm()
        sem, v = evac[-2] if i >= 2 else (c.s_a, (tm_done, kro_done)[i])
        wt(T, sem, v)
        c.use(b)
        wh = c.w_hi[:, b.slot, :].rearrange("p (k m) -> p k m", k=KT)
        wl = c.w_lo[:, b.slot, :].rearrange("p (k m) -> p k m", k=KT)
        width = ALLT if (both or what == "ckv") else SEQ
        for lo, nn in ((0, SEQ), (SEQ, CTX))[:2 if width == ALLT else 1]:
            for k in range(KT):
                ins = c.mm3(c.flat(bank, lo, nn), wh[:, k, :], wl[:, k, :], h_hi[:, k, lo:lo + nn],
                            h_lo[:, k, lo:lo + nn], k == 0, k == KT - 1)
        c.used(ins)
        c.split_hi(b)
        if i == 0:
            turn_rope()
        if pending:
            pending.pop()()
        done = n + i + 1 + PRIME
        src = c.flat(bank, 0, width)
        if what in ("cq", "ckv"):
            A.wait_ge(c.s_used.h, done)
            dst = cq[:, kk, 0:width] if what == "cq" else ckv[:, 0:width]
            gain_at = (V_["q_a_g"] + 2 * l + kk) if what == "cq" else V_["kv_a_g"] + l
            A.activation(dst, src, ACT.Copy, scale=vec[:, gain_at:gain_at + 1])
            c.norm_begin() if kk == 0 else None
            wt(A, c.s_ssq)
            up(c.s_sq, A.activation(c.sq[:, kk % 2, 0:width], src, ACT.Square))
            evac.append((c.s_sq, c.s_sq.n))

            def row_sums(kk=kk, width=width, cq_=what == "cq"):
                c.sum_squares(kk, 2 if cq_ else 1, 0, 0 if cq_ else 1, width // P)
                if not cq_ or kk == 1:
                    c.rstd(0 if cq_ else 1, width // P, 256 if cq_ else 128, row=1 if cq_ else 2)
            pending.append(row_sums)
        elif what == "gu":
            V.wait_ge(c.s_used.h, done)
            wt(V, c.s_a)
            up(c.s_v, V.tensor_tensor(gu[:, kk, 0:width], src, gu[:, kk, 0:width], ALU.mult))
            evac.append((c.s_v, c.s_v.n))
        else:
            dst = {"gg": gu, "fg": fg, "ag": ag}[what]
            A.wait_ge(c.s_used.h, done)
            up(c.s_a, A.activation(dst[:, kk, 0:width], src, ACT.Silu))
            evac.append((c.s_a, c.s_a.n))
    n += 13
    wt(T, c.s_a)
    wt(T, c.s_v)
    wt(V, c.s_a)
    wt(A, c.s_v)

    m_hi = nc.alloc_sbuf_tensor_at(L + "m_hi", [P, KT, ALLT], F32R, offset=h_end - 2 * KT * ALLT * 4)
    m_lo = nc.alloc_sbuf_tensor_at(L + "m_lo", [P, KT, ALLT], F32R, offset=h_end - KT * ALLT * 4)
    V.wait_ge(c.s_used.h, n + PRIME)
    A.wait_ge(c.s_used.h, n + PRIME)

    def split_out(kk, src, width):
        wt(A, c.s_v)
        up(c.s_hh, A.activation(m_hi[:, kk, 0:width], src, ACT.Copy))
        wt(V, c.s_hh)
        up(c.s_hl, V.tensor_tensor(m_lo[:, kk, 0:width], src, m_hi[:, kk, 0:width].bitcast(F32), ALU.subtract))

    at_ = lambda name, shape, off: nc.alloc_sbuf_tensor_at(L + name, shape, F32, offset=off)
    ua = h_end - KT * ALLT * 4 - 4 * ALLT * 4
    ub = h_end - 4 * ALLT * 4
    U = at_("U", [P, 2, 2, ALLT], ua)
    F_ = at_("F", [P, 2, ALLT], ub)
    wuq = at_("wuq", [P, 2, A_HEADS * A_QK], ub + 2 * ALLT * 4)
    d_uq, d_ukv = nc.alloc_semaphore(L + "d_uq"), nc.alloc_semaphore(L + "d_ukv")
    A.dma_start(wuq[:, :, :].rearrange("p a n -> p (a n)"), io["wuq"][l]).then_inc(d_uq, 16)
    T.wait_ge(d_s1, 16 * len(loads))

    wt(T, c.s_v, gate_done)
    for pr in range(2):
        bank = (4, 6)[pr]
        for t in range(nt_q):
            for e in range(2):
                hd = 2 * pr + e
                ins = T.matmul(c.flat(bank, t * P, P)[HD * e:HD * e + HD], tm[:, t, 256 + hd * HD:256 + (hd + 1) * HD],
                               wsT[:, hd, :], start=True, stop=True)
        up(c.s_t, ins)
        wt(V, c.s_t)
        mixed = sqv[:, :, :, :].rearrange("p t h d -> p (t h d)")[:, pr * ALLT:pr * ALLT + nq]
        V.tensor_tensor(mixed.rearrange("p (t n) -> p t n", n=P), c.flat(bank, 0, nq).rearrange("p (t n) -> p t n", n=P),
                        bsb[:, pr, :].unsqueeze(1).broadcast_to([P, nt_q, P]), ALU.add)
        V.drain()
        up(c.s_v, V.tensor_tensor(mixed, mixed, gu[:, pr, 0:nq], ALU.mult))
        mix_read = c.s_v.n
        split_out(2 + pr, mixed, nq)
    u_done = [0, 0]
    for ft in range(2):
        fs = slice(ft * P, (ft + 1) * P)
        for a in range(2):
            bank = (0, 2)[a]
            if ft:
                wt(T, c.s_a, u_done[a])
            for t in range(TT):
                ins = T.matmul(ps[:, bank, :], tm[:, t, fs], dft[a][:, t, :], start=t == 0, stop=t == TT - 1)
            if both:
                for t in range(2):
                    ins = T.matmul(ps[:, bank + 1, 0:CTX], tm[:, TT + t, fs], dfc[a][:, t, :], start=t == 0, stop=t == 1)
            up(c.s_t, ins)
            wt(A, c.s_t)
            up(c.s_a, A.activation(U[:, a, ft, 0:nq], c.flat(bank, 0, nq), ACT.Copy))
            u_done[a] = c.s_a.n
    pieces = ((0, SEQ), (SEQ, CTX))[:2 if both else 1]
    wt(T, c.s_a)
    wt(T, c.s_v, mix_read)
    for ft in range(2):
        bank = (4, 6)[ft]
        for lo, nn in pieces:
            T.matmul(c.flat(bank, lo, nn), dfd[:, 0, :], U[:, 0, ft, lo:lo + nn], start=True, stop=False)
            ins = T.matmul(c.flat(bank, lo, nn), dfd[:, 1, :], U[:, 1, ft, lo:lo + nn], start=False, stop=True)
        up(c.s_t, ins)
        wt(A, c.s_t)
        up(c.s_a, A.activation(F_[:, ft, 0:nq], c.flat(bank, 0, nq), ACT.Copy))
    wt(T, c.s_a)
    wukv = at_("wukv", [P, 1024], ua)
    A.dma_start(wukv[:, :], io["wukv"][l]).then_inc(d_ukv, 16)
    fm_read = []
    for ft in range(2):
        bank = (0, 2)[ft]
        for lo, nn in pieces:
            for k in range(2):
                ins = T.matmul(c.flat(bank, lo, nn), wfm[:, k, ft * P:(ft + 1) * P], F_[:, k, lo:lo + nn],
                               start=k == 0, stop=k == 1)
        up(c.s_t, ins)
        wt(V, c.s_t)
        up(c.s_v, V.tensor_tensor(fg[:, ft, 0:nq], c.flat(bank, 0, nq), fg[:, ft, 0:nq], ALU.mult))
        fm_read.append(c.s_v.n)
        split_out(ft, fg[:, ft, 0:nq], nq)

    wt(A, c.s_hl)
    c.close(stage1)

    kT = c.ctx(L + "kT", [A_QK, A_HEADS, ALLT])
    qT = c.ctx(L + "qT", [A_QK, A_HEADS, ALLT])
    vS = c.ctx(L + "vS", [P, NT, A_HEADS * A_V])
    stage2 = c.scope()
    work = [at_(f"work{i}", [P, A_HEADS, A_QK], (ub, ub + ALLT * 4, ua + 4096)[i]) for i in range(3)]
    flatw = [w[:, :, :].rearrange("p h d -> p (h d)") for w in work]
    wsq = [c.RB[:, :], c.sq[:, 1, :]]
    heads = lambda ap: ap.rearrange("p (h d) -> p h d", h=A_HEADS)
    T.wait_ge(d_uq, 16)
    T.wait_ge(d_ukv, 16)
    jobs = [("k", t) for t in range(NT)] + [("q", t) for t in range(nt_q)]
    nj = len(jobs)
    pj_, evac_, sum_, std_, fin_, turn_, out_ = ([0] * nj for _ in range(7))

    def project(i):
        what, t = jobs[i]
        bank, ts = (0, 2)[i % 2], slice(t * P, (t + 1) * P)
        if i >= 2:
            wt(T, c.s_a, evac_[i - 2])
        else:
            wt(T, c.s_v, fm_read[i])
        if what == "k":
            for half in range(2):
                ins = T.matmul(ps[:, bank + half, :], ckv[:, ts], wukv[:, half * 512:(half + 1) * 512],
                               start=True, stop=True)
        else:
            for half in range(2):
                for k in range(2):
                    ins = T.matmul(ps[:, bank + half, 0:384], cq[:, k, ts], wuq[:, k, half * 384:(half + 1) * 384],
                                   start=k == 0, stop=k == 1)
        pj_[i] = up(c.s_t, ins)

    def turn_heads(i):
        wt(T, c.s_v, fin_[i])
        if i >= 2:
            wt(T, c.s_a, out_[i - 2])
        for hd in range(A_HEADS):
            ins = T.transpose(c.flat((4, 6)[i % 2], hd * P, P)[0:A_QK], work[i % 3][:, hd, :], c.ident[:, :])
        turn_[i] = up(c.s_t, ins)

    def evacuate(i):
        what, t = jobs[i]
        bank, w = (0, 2)[i % 2], work[i % 3]
        wt(A, c.s_t, pj_[i])
        if i >= 3:
            wt(A, c.s_t, turn_[i - 3])
        if what == "k":
            r = c.r_tok[:, 2, t:t + 1]
            A.activation(w[:, :, A_NOPE:A_QK], kro[:, t, :].unsqueeze(1).broadcast_to([P, A_HEADS, A_ROPE]), ACT.Copy)
            A.activation(vS[:, t, :], ps[:, bank + 1, :], ACT.Copy, scale=r)
            evac_[i] = up(c.s_a, A.activation(w[:, :, 0:A_NOPE], heads(ps[:, bank, :]), ACT.Copy, scale=r))
        else:
            r = c.r_tok[:, 1, t:t + 1]
            for half in range(2):
                ins = A.activation(flatw[i % 3][:, half * 384:(half + 1) * 384], ps[:, bank + half, 0:384],
                                   ACT.Copy, scale=r)
            evac_[i] = up(c.s_a, ins)
        A.drain()
        if i >= 2:
            wt(A, c.s_v, sum_[i - 2])
        up(c.s_a, A.activation(wsq[i % 2], flatw[i % 3], ACT.Square))

    def finish_job(i):
        what, t = jobs[i]
        w, w_, sm = work[i % 3], 0 if what == "q" else 1, small[:, i % 2, :]
        wt(V, c.s_a, std_[i])
        V.reciprocal(sm, sm)
        V.drain()
        V.tensor_tensor(w[:, :, :], w[:, :, :], sm.unsqueeze(2).broadcast_to([P, A_HEADS, A_QK]), ALU.mult)
        V.drain()
        wr = w[:, :, A_NOPE:A_QK]
        if t < TT:
            wr4 = wr.rearrange("p h (a x) -> p h a x", a=2)
            rt4 = rtmp[:, :, :].rearrange("p h (a x) -> p h a x", a=2)
            tab = rtab[:, w_, 1, t, :].rearrange("p (a x) -> p a x", a=2)
            for q in range(2):
                a0, b0 = 8 * q, 8 * (1 - q)
                V.tensor_tensor(rt4[:, :, :, a0:a0 + 8], wr4[:, :, :, b0:b0 + 8],
                                tab[:, :, a0:a0 + 8].unsqueeze(1).broadcast_to([P, A_HEADS, 2, 8]), ALU.mult)
            V.drain()
            V.tensor_tensor(wr, wr, rtab[:, w_, 0, t, :].unsqueeze(1).broadcast_to([P, A_HEADS, A_ROPE]), ALU.mult)
            V.drain()
            ins = V.tensor_tensor(wr, wr, rtmp[:, :, :], ALU.add)
        else:
            ins = V.tensor_tensor(wr, wr, gains[:, w_, A_NOPE:A_QK].unsqueeze(1).broadcast_to([P, A_HEADS, A_ROPE]),
                                  ALU.mult)
        fin_[i] = up(c.s_v, ins)

    def copy_out(i):
        what, t = jobs[i]
        w_ = 0 if what == "q" else 1
        wt(A, c.s_t, turn_[i])
        src = c.flat((4, 6)[i % 2], 0, 1024)[0:A_QK].rearrange("p (h n) -> p h n", h=A_HEADS)
        out_[i] = up(c.s_a, A.activation((kT if what == "k" else qT)[:, :, t * P:(t + 1) * P], src, ACT.Copy,
                                         scale=gcol[0:A_QK, w_:w_ + 1]))

    for i in range(nj + 2):
        if i < nj:
            project(i)
        if i >= 2:
            turn_heads(i - 2)
        if i < nj:
            evacuate(i)
            squared = c.s_a.n
        if 1 <= i <= nj:
            finish_job(i - 1)
        if i < nj:
            wt(V, c.s_a, squared)
            sum_[i] = up(c.s_v, V.tensor_reduce(small[:, i % 2, :], heads(wsq[i % 2]), AX.X, ALU.add))
        if i >= 2:
            copy_out(i - 2)
        if i < nj:
            wt(A, c.s_v, sum_[i])
            std_[i] = up(c.s_a, A.activation(small[:, i % 2, :], small[:, i % 2, :], ACT.Sqrt, bias=EPS,
                                             scale=1.0 / A_QK))
    wt(T, c.s_a)
    wt(V, c.s_a)
    wt(A, c.s_v)
    wt(V, c.s_t)
    wt(A, c.s_t)
    c.close(stage2)
    for e in (T, V, A):
        wt(e, c.s_a)
        wt(e, c.s_v)
    joint_attention(c, l, 0, TT, ALLT, 0, kT, qT, vS, ag, m_hi, m_lo, spare)
    if both:
        joint_attention(c, l, TT, NT - TT, CTX, SEQ, kT, qT, vS, ag, m_hi, m_lo, spare)
    c.close(tok)

    x0 = c.s_x.n
    c.norm_begin()
    add_base = c.s_v.n

    def add_squares(j):
        wt(V, c.s_sq, c.s_sq_base + j + 1)
        wt(V, c.s_v, add_base + j - 1)
        up(c.s_v, V.tensor_tensor(c.RB[:, :], c.RB[:, :], c.sq[:, j % 2, :], ALU.add))

    for u in range(KT):
        b, bank = Blk(n + u), (0, 2)[u % 2]
        c.use(b)
        wt(T, c.s_x, x0 + u - 1)
        for lo, nn in pieces:
            for k in range(KT):
                wh = c.w_hi[:, b.slot, k * P:(k + 1) * P]
                wl = c.w_lo[:, b.slot, k * P:(k + 1) * P]
                ins = c.mm3(c.flat(bank, lo, nn), wh, wl, m_hi[:, k, lo:lo + nn], m_lo[:, k, lo:lo + nn],
                            k == 0, k == KT - 1)
        c.used(ins)
        c.split_hi(b)
        V.wait_ge(c.s_used.h, n + u + 1 + PRIME)
        if both:
            V.scalar_tensor_tensor(c.y[:, u, :], ps[:, bank + 1, 0:CTX], modv[:, l, 2 * KT + u, 1:2], c.y[:, u, :],
                                   ALU.mult, ALU.add)
        c.s_x.up(V.scalar_tensor_tensor(c.x[:, u, :], ps[:, bank, :], modv[:, l, 2 * KT + u, 0:1], c.x[:, u, :],
                                        ALU.mult, ALU.add))
        if both:
            wt(A, c.s_x)
            if u >= 3:
                wt(A, c.s_v, add_base + u - 2)
            to = c.RB if u == 0 else c.sq[:, u % 2, :]
            A.activation(to[:, 0:SEQ], c.x[:, u, :], ACT.Square)
            up(c.s_sq, A.activation(to[:, SEQ:ALLT], c.y[:, u, :], ACT.Square))
            if u >= 2:
                add_squares(u - 1)
    if both:
        add_squares(KT - 1)
        c.sum_over_partitions([(4, c.RB[:, 0:SEQ]), (5, c.RB[:, SEQ:ALLT])])
        c.rstd_rows(4, ALLT, c.RB[:, :])
        wt(T, c.s_std)
    wt(A, c.s_x)
    wt(T, c.s_x)
    c.close(outer)
    return n + KT


def joint_attention(c, l, t0, nqb, nk, k0, kT, qT, vS, ag, m_hi, m_lo, spare):
    nc, T, V, A = c.nc, c.T, c.V, c.A
    L = f"j{l}{t0}_"
    sc = c.scope()
    KTL = nk // P
    mk = lambda nme, e: c.sem(L + nme, e)
    s_q, s_exp, s_hi = (mk(x, A) for x in ("q", "exp", "hi"))
    s_mx, s_pt, s_on, s_g, s_lo = (mk(x, V) for x in ("mx", "pt", "on", "g", "lo"))
    s_qk, s_tr, s_pv, s_ot = (mk(x, T) for x in ("qk", "tr", "pv", "ot"))
    qc = c.ctx(L + "qc", [A_QK, A_HEADS, P])
    prob = [nc.alloc_sbuf_tensor_at(L + f"prob{i}", [P, nk], F32, offset=spare + i * ALLT * 4) for i in range(2)]
    probT = [nc.alloc_sbuf_tensor_at(L + "probT0", [P, nk], F32, offset=spare + 2 * ALLT * 4)[:, :], c.sq[:, 0, 0:nk]]
    nm = c.ctx(L + "nm", [P, A_HEADS])
    den = c.ctx(L + "den", [P, A_HEADS])
    rden = c.ctx(L + "rden", [P, A_HEADS])
    osb = c.ctx(L + "osb", [P, 512])
    gt = c.sq[:, 1, 0:512].rearrange("p (f n) -> p f n", f=4)
    cut = [(0, min(nk, 512))] + ([(512, nk - 512)] if nk > 512 else [])
    sbank, tbank, o_bank, ot_bank = (0, 2), 4, 6, 7

    u = lambda i, s: i * 8 + (s + 1 + PRIME)

    def pe(i, head, tail):
        def pv(s):
            sl = s % 8
            wt(T, s_pt, u(i, s))
            if sl == 0:
                wt(T, s_on, i + PRIME)
            for k in range(KTL):
                ins = T.matmul(c.ps[:, o_bank, sl * A_V:(sl + 1) * A_V], probT[sl % 2][:, k * P:(k + 1) * P],
                               vS[:, k0 // P + k, sl * A_V:(sl + 1) * A_V], start=k == 0, stop=k == KTL - 1)
            ins.then_inc(s_pv.h, 1)

        def tr(s):
            wt(T, s_exp, u(i, s))
            wt(T, s_pt, u(i, s - 1))
            for k in range(KTL):
                ins = T.transpose(c.flat(tbank, k * P, P), prob[s % 2][:, k * P:(k + 1) * P], c.ident[:, :])
            ins.then_inc(s_tr.h, 1)

        for s in range(8):
            if head:
                if s == 0:
                    wt(T, s_q, i + (1 + PRIME))
                wt(T, s_exp, u(i, s - 2))
                for lo, nn in cut:
                    ins = T.matmul(c.flat(sbank[s % 2], lo, nn), qc[:, s, :], kT[:, s, k0 + lo:k0 + lo + nn],
                                   start=True, stop=True)
                ins.then_inc(s_qk.h, 1)
            if s >= 1 and head or s < 1 and tail:
                tr(s - 1)
            if s >= 2 and head or s < 2 and tail:
                pv(s - 2)
            if s == 2 and tail:
                wt(T, s_on, i + PRIME)
                wt(T, s_g, i + (PRIME - 1))
                for b in range(4):
                    ins = T.transpose(c.ps[:, ot_bank, b * P:(b + 1) * P], osb[:, b * P:(b + 1) * P], c.ident[:, :])
                ins.then_inc(s_ot.h, 1)

    def ve(i, head, tail):
        def ptc(s):
            wt(V, s_tr, u(i, s))
            wt(V, s_pv, u(i, s - 2))
            V.tensor_copy(probT[s % 2][:, 0:nk], c.flat(tbank, 0, nk)).then_inc(s_pt.h, 1)

        if tail:
            wt(V, s_exp, u(i, -1))
            V.reciprocal(rden[:, :], den[:, :])
        for s in range(8):
            if head:
                wt(V, s_qk, u(i, s))
                V.tensor_reduce(nm[:, s:s + 1], c.flat(sbank[s % 2], 0, nk), AX.X, ALU.max,
                                negate=True).then_inc(s_mx.h, 1)
            if s >= 1 and head or s < 1 and tail:
                ptc(s - 1)
            if s == 1 and tail:
                V.drain()
                wt(V, s_pv, u(i, -1))
                V.tensor_tensor(osb[:, :].rearrange("p (h d) -> p h d", h=A_HEADS),
                                c.ps[:, o_bank, :].rearrange("p (h d) -> p h d", h=A_HEADS),
                                rden[:, :].unsqueeze(2).broadcast_to([P, A_HEADS, A_V]), ALU.mult).then_inc(s_on.h, 1)
            if s == 3 and tail:
                wt(V, s_ot, i + PRIME)
                wt(V, s_lo, i + (PRIME - 1))
                V.tensor_tensor(gt, c.ps[:, ot_bank, :].rearrange("p (f n) -> p f n", f=4), ag[:, :, cols(i)],
                                ALU.mult).then_inc(s_g.h, 1)
            if s == 5 and tail:
                wt(V, s_hi, i + PRIME)
                V.tensor_tensor(m_lo[:, 4:8, cols(i)], gt, m_hi[:, 4:8, cols(i)].bitcast(F32),
                                ALU.subtract).then_inc(s_lo.h, 1)

    def ac(i, head, tail):
        for s in range(8):
            if head:
                wt(A, s_mx, u(i, s))
                wt(A, s_tr, u(i, s - 2))
                A.activation(prob[s % 2][:, :], c.flat(sbank[s % 2], 0, nk), ACT.Exp, bias=nm[:, s:s + 1],
                             accum_out=den[:, s:s + 1]).then_inc(s_exp.h, 1)
            if s == 3 and tail:
                wt(A, s_g, i + PRIME)
                c.absorb(A)
                A.activation(m_hi[:, 4:8, cols(i)], gt, ACT.Copy).then_inc(s_hi.h, 1)

    def queries(i, s):
        wt(A, s_qk, u(i, s))
        c.absorb(A)
        A.activation(qc[:, :, :], qT[:, :, bass.ds(i * P + t0 * P, P)], ACT.Copy).then_inc(s_q.h, 1)

    cols = lambda i: bass.ds(i * P + (t0 - 1) * P, P)
    for eng, part in ((T, pe), (V, ve), (A, ac)):
        if eng is A:
            queries(0, -1)
        part(0, True, False)
        with eng.Fori(0, nqb - 1, 1) as i:
            if eng is A:
                queries(i + 1, -1)
            part(i + 1, True, True)
        part(nqb, False, True)
    for s in (s_exp, s_mx, s_pt, s_qk, s_tr, s_pv):
        s.n = PRIME + 8 * nqb
    for s in (s_q, s_hi, s_on, s_g, s_lo, s_ot):
        s.n = PRIME + nqb
    for e in (T, A):
        wt(e, s_lo)
    wt(V, s_pv)
    wt(V, s_hi)
    wt(A, s_pv)
    c.close(sc)


def build(nc, io, V_):
    c = Core(nc, io)
    T, V, A, S = c.T, c.V, c.A, c.S

    c.top = (nc.sbuf_base + 31) // 32 * 32
    c.offset = c.top

    def ctx(name, shape, dt=F32):
        size = int(np.prod(shape[1:])) * 4
        t = nc.alloc_sbuf_tensor_at(name, shape, dt, offset=c.offset)
        c.offset += (size + 31) // 32 * 32
        return t

    c.ctx = ctx
    c.scope = lambda: c.offset

    def close(mark):
        c.offset = mark
    c.close = close

    S.dma_start(c.vec[:, :], io["vec"]).then_inc(c.d_const, 16)
    S.dma_start(c.ident[:, :], io["ident"]).then_inc(c.d_const, 16)
    S.dma_start(c.slope[:, :], io["slope"]).then_inc(c.d_const, 16)
    d_x = [nc.alloc_semaphore(f"d_x{i}") for i in range(4)]
    for i in range(4):
        S.dma_start(c.x[:, 2 * i:2 * i + 2, :], io["x"][:, 2 * i:2 * i + 2, :]).then_inc(d_x[i], 16)
    d_y = nc.alloc_semaphore("d_y")
    S.dma_start(c.y[:, :, :], io["ctx"]).then_inc(d_y, 16)
    V.memset(c.ones[:, :], 1.0).then_inc(c.s_v.h, 1)
    c.s_v.n += 1
    wt(T, c.s_v)
    for e in (T, V, A):
        e.wait_ge(c.d_const, 48)
    c1 = c.scope()
    cs = c.ctx("cs", [P, KT, 2])
    A.activation(cs[:, :, :], c.vec[:, V_["c"]:V_["c"] + 2 * KT].rearrange("p (k a) -> p k a", a=2), ACT.Silu)
    A.drain()
    c.s_a.up(A.activation(c.c4[:, :, 0:2], cs[:, :, :], ACT.Copy))
    wt(V, c.s_a)
    c.s_v.up(V.tensor_tensor(c.c4[:, :, 2:4], cs[:, :, :], c.c4[:, :, 0:2].bitcast(F32), ALU.subtract))
    wt(T, c.s_v)

    c.stream_loops()
    h = (c.ctx("h_hi", [P, KT, SEQ], F32R), c.ctx("h_lo", [P, KT, SEQ], F32R))
    vcol = lambda name, i=0: c.vec[:, V_[name] + i * KT:V_[name] + (i + 1) * KT]
    body = c.scope()

    c.norm_begin()
    c.s_hh_base = c.s_hh.n
    for k in range(KT):
        norm_tile(c, h, k, vcol("norm_mix", 0), natural, 16, d_x[k // 2])
        norm_tile_lo(c, h, k, vcol("norm_mix", 0), natural)
        c.sum_rows(k, KT, [(0, c.sq[:, k % 2, 0:SEQ])])
    x_summed = c.s_ssq.n
    for b in range(LEAD):
        c.split_hi(Blk(b - LEAD))
    A.wait_ge(d_y, 16)
    V.wait_ge(d_y, 16)
    context_sums(c)
    c.rstd_rows(0, SEQ, c.RB[:, 0:SEQ], x_summed)
    c.rstd_rows(2, CTX, c.RB[:, SEQ:ALLT])
    wt(T, c.s_hl)
    wt(T, c.s_std)
    n = 0
    ah, al = c.ctx("a_hi", [P, KT * SEQ], F32R), c.ctx("a_lo", [P, KT * SEQ], F32R)
    ready = window_attention(c, n, h, ah, al)
    n += 16
    contract_out(c, n, KT, (ah, al), natural, (h, vcol("norm_ffn", 0), natural), ready)
    norm_finish(c)
    n += KT
    c.close(body)

    def ffn(n, name, mod, nxt):
        mh, ml = c.ctx(name + "m_hi", [P, FT * SEQ], F32R), c.ctx(name + "m_lo", [P, FT * SEQ], F32R)
        ready = swiglu(c, n, name, h, mh, ml, mod)
        if mod:
            wt(V, *ready[0][1])
            for l in range(2):
                modulation(c, l, V_)
        n += 2 * FT + (20 if mod else 0)
        contract_out(c, n, FT, (mh, ml), natural, nxt, ready)
        c.close(body)
        return n + FT

    n = ffn(n, "f0", False, (h, vcol("norm_mix", 1), residues))
    norm_finish(c)
    ah, al = c.ctx("b_hi", [P, KT * SEQ], F32R), c.ctx("b_lo", [P, KT * SEQ], F32R)
    ready = dilated_attention(c, n, h, ah, al)
    n += 96
    contract_out(c, n, KT, (ah, al), residues, (h, vcol("norm_ffn", 1), natural), ready)
    norm_finish(c)
    n += KT
    c.close(body)
    n = ffn(n, "f1", True, (None, vcol("norm_final"), natural))
    c.close(c1)
    update = final_norm(c, vcol("norm_final"))
    for l in range(2):
        n = block_two_layer(c, l, n, V_, update if l == 0 else None)
    assert n == len(PLAN), (n, len(PLAN))
    d_out = nc.alloc_semaphore("d_out")
    S.wait_ge(c.s_x.h, c.s_x.n)
    S.dma_start(io["out"], c.x[:, :, :]).then_inc(d_out, 16)
    S.wait_ge(d_out, 16)



def shape_constants():
    j = np.arange(P)
    k = np.arange(3 * P)
    rel = np.abs(k[None, :] - WIN - j[:, None]).astype(np.float64)
    dist0 = np.where(rel <= WIN, -rel, -BIG)
    t = 4 * j[:, None]
    keys = np.concatenate([DIL * np.arange(P) + r for r in range(DIL)])
    cols = []
    dj = np.abs(j[:, None] - j[None, :])
    own2 = np.where(dj <= 64, -4.0 * dj, -BIG)
    own3 = np.where(dj % 4 == 0, -4.0 * dj, -BIG)
    for r in range(DIL):
        d = np.abs(t + r - keys[None, :]).astype(np.float64)
        cols += [np.where(d <= 64, -d, -BIG), own2, own3]
    dist1 = np.concatenate(cols, axis=1)
    slope = lambda hd: 2.0 ** (-8.0 * (hd + 1) / 16) * 8.0
    row = [slope(4 * (2 * (tt // 4) + e) + tt % 4) for tt in range(8) for e in range(2)] + [slope(hd) for hd in range(16)]
    slopes = np.tile(np.array(row)[None, :], (P, 1))

    def dft(n, scale):
        a = np.arange(n)
        ang = 2 * np.pi * ((a[:, None] * a[None, :]) % n) / n
        m = np.stack([np.cos(ang), np.sin(ang)]) * scale
        return m.reshape(2, n // P, P, n).transpose(2, 0, 1, 3)
    a = np.arange(64)
    ang = 2 * np.pi * ((a[:, None] * a[None, :]) % 64) / 64
    bd = np.zeros((2, P, P))
    for g in range(2):
        s = slice(64 * g, 64 * g + 64)
        bd[0, s, s] = np.cos(ang) / 8.0
        bd[1, s, s] = -np.sin(ang) / 8.0
    half = A_ROPE // 2
    tok = np.arange(SEQ)
    inv = (10000.0 ** (-np.arange(0, half, 2, dtype=np.float32) / half)).astype(np.float32)
    ar = (tok // 64).astype(np.float32)[:, None] * inv[None, :]
    ac = (tok % 64).astype(np.float32)[:, None] * inv[None, :]
    angs = np.concatenate([ar, ar, ac, ac], -1).astype(np.float32)
    sign = np.repeat(np.array([-1.0, 1.0, -1.0, 1.0]), 8)
    rope = np.stack([np.cos(angs), np.sin(angs) * sign[None, :]])
    rope = rope.reshape(2, TT, P, A_ROPE).transpose(2, 0, 1, 3).reshape(P, -1)
    out = {"dist0": dist0, "dist1": dist1, "slope": slopes, "ident": np.eye(P), "dft": dft(SEQ, SEQ ** -0.5),
           "dfc": dft(CTX, CTX ** -0.5), "dfd": bd.transpose(1, 0, 2).reshape(P, -1), "rope": rope}
    return {n: np.ascontiguousarray(v, dtype=np.float32) for n, v in out.items()}


def lay_out(x):
    g = {n: np.asarray(v) for n, v in x.items()}
    colblk = lambda w, t: w[:, t * P:(t + 1) * P].reshape(KT, P, P).transpose(1, 0, 2).reshape(P, 1024)
    hcols = lambda hd: np.arange(hd * HD, (hd + 1) * HD)
    pair = lambda tt: (4 * (2 * (tt // 4)) + tt % 4, 4 * (2 * (tt // 4) + 1) + tt % 4)
    qa = np.concatenate([hcols(hd) for tt in range(8) for hd in pair(tt)])
    wa = g["w_qkv_a"][0]
    waq, wak, wav = wa[:, :1024][:, qa], wa[:, 1024:1280], wa[:, 1280:1536]
    woa = g["w_out_a"][0][qa, :]
    wb = g["w_qkv_b"][0].reshape(D_MODEL, 3, 3, 1024)
    win = g["w_in_2"]
    o = dict(f=0, fg=256, gu=512, gv=768, gg=1024, cq=1280, ckv=1536, kr=1664, ag=1696)
    tokcols = np.concatenate([np.arange(256), np.arange(o["gv"], o["gv"] + 256)])
    feat = np.concatenate([np.arange(o[nme], o[nme] + w) for nme, w in
                           (("cq", 256), ("ckv", 128), ("gg", 256), ("gu", 256), ("fg", 256), ("ag", 512))])
    blocks = []
    for kind, *w in PLAN:
        if kind == "ak":
            b = colblk(wak, w[0])
        elif kind == "av":
            b = colblk(wav, w[0])
        elif kind == "aq":
            b = colblk(waq, w[0])
        elif kind == "mod":
            b = colblk(g["w_mod_2"][w[0]], w[1])
        elif kind == "modrow":
            first = (MT - 4 * MROWS + 4 * w[0]) * P
            b = g["w_mod_2"][1][w[1] * 2 * P:(w[1] + 1) * 2 * P, first:first + 4 * P]
            b = b.reshape(2, P, 4 * P).transpose(1, 0, 2).reshape(P, 1024)
        elif kind == "oa":
            b = woa[w[0] * P:(w[0] + 1) * P]
        elif kind == "ob":
            b = g["w_out_b"][0][w[0] * P:(w[0] + 1) * P]
        elif kind == "gate":
            b = colblk(g["w_gate"][w[0]], w[1])
        elif kind == "up":
            b = colblk(g["w_up"][w[0]], w[1])
        elif kind == "down":
            b = g["w_down"][w[0]][w[1] * P:(w[1] + 1) * P]
        elif kind in ("bq", "bk", "bv"):
            b = colblk(wb[:, w[0], "qkv".index(kind[1])], w[1])
        elif kind == "kr":
            b = np.zeros((P, 1024), np.float32)
            b[:, :KT * A_ROPE] = win[w[0]][:, o["kr"]:o["kr"] + 32].reshape(KT, P, 32).transpose(1, 0, 2).reshape(P, -1)
        elif kind == "tok":
            b = win[w[0]][:, tokcols][w[1] * 256:(w[1] + 1) * 256].reshape(2, P, 512).transpose(1, 0, 2).reshape(P, 1024)
        elif kind == "feat":
            b = colblk(win[w[0]][:, feat], w[1])
        elif kind == "out":
            b = colblk(g["w_out_2"][w[0]], w[1])
        blocks.append(b)
    arr = {"wstream": np.stack(blocks)}
    ft = lambda a: a.reshape(-1, P).T
    vec, V_ = [], {}

    def add(name, a):
        V_[name] = sum(v.shape[1] for v in vec)
        vec.append(a)
    add("norm_mix", ft(g["norm_mix"]))
    add("norm_ffn", ft(g["norm_ffn"]))
    add("norm_final", ft(g["norm_final"]))
    add("norm_g", ft(g["norm_g_2"]))
    add("b_mod", ft(g["b_mod_2"]))
    add("q_a_g", ft(g["q_a_g_2"]))
    add("kv_a_g", ft(g["kv_a_g_2"]))
    add("c", np.stack([ft(g["c_2"][0]), ft(g["c_ctx_2"])], axis=2).reshape(P, 2 * KT))
    arr["vec"] = np.concatenate(vec, axis=1)
    arr["x"] = g["x"][0].T.reshape(KT, P, SEQ).transpose(1, 0, 2)
    arr["ctx"] = g["ctx_2"][0].T.reshape(KT, P, CTX).transpose(1, 0, 2)
    arr["sinks"] = np.broadcast_to(np.concatenate(
        [np.tile(g["sink_a"][0][list(pair(tt))], 4) for tt in range(8)])[None, :], (P, 64))
    arr["wfmix"] = g["w_fmix_2"].reshape(2, 2, P, 256).transpose(0, 2, 1, 3).reshape(2, P, 512)
    arr["gws"] = g["g_ws_2"].transpose(0, 3, 1, 2).reshape(2, P, 512)
    arr["gbs"] = np.repeat(g["g_bs_2"].reshape(2, 2, 2, 1, P), HD, axis=3).reshape(2, 2, P, P).transpose(0, 2, 1, 3).reshape(2, P, 2 * P)
    arr["glg"] = np.broadcast_to(g["g_ln_g_2"][:, None, :], (2, P, HD))
    arr["wuq"] = g["w_uq_2"].reshape(2, 2, P, 768).transpose(0, 2, 1, 3).reshape(2, P, 1536)
    arr["wukv"] = g["w_ukv_2"].reshape(2, P, A_HEADS, 2, 64).transpose(0, 1, 3, 2, 4).reshape(2, P, 1024)
    arr["qkg"] = np.broadcast_to(np.stack([g["q_norm_g_2"], g["k_norm_g_2"]], 1)[:, None], (2, P, 2, A_QK)).reshape(2, P, 2 * A_QK)
    arr["qkgT"] = np.stack([g["q_norm_g_2"], g["k_norm_g_2"]], 2)[:, :A_NOPE]
    arr = {n: np.ascontiguousarray(v) for n, v in arr.items()}
    arr.update(shape_constants())
    return arr, V_


def kernel(**inputs):
    from concourse import bacc
    from concourse.bass_utils import run_bass_kernel_spmd
    arr, V_ = lay_out(inputs)
    nc = bacc.Bacc("TRN2", target_bir_lowering=False, num_devices=1)
    io = {n: nc.dram_tensor("in_" + n, a.shape, F32, kind="ExternalInput").ap() for n, a in arr.items()}
    io["out"] = nc.dram_tensor("out", (P, KT, SEQ), F32, kind="ExternalOutput").ap()
    build(nc, io, V_)
    r = run_bass_kernel_spmd(nc, [{"in_" + n: a for n, a in arr.items()}], core_ids=[0])
    o = r.results[0]["out"]
    return np.ascontiguousarray(o.transpose(1, 0, 2).reshape(D_MODEL, SEQ).T)[None]
```
